# Optimizing a Trainium2 kernel written in Bass

```python
import jax, jax.numpy as jnp
from jax import lax
import numpy as np

D_MODEL = 1024
BATCH = 1
SEQ = 256
DEPTH = 1

GRID_W = 64
CTX_LEN = 256

RET_HEADS = 8
RET_QK_DIM = 128
RET_V_DIM = 256
RET_QK = RET_HEADS * RET_QK_DIM
RET_V = RET_HEADS * RET_V_DIM
RET_CHUNK = 128
ROPE_BASE = 10000.0

CONV_DIM = D_MODEL
CONV_WIDTH = 31
N_BRANCHES = 2

N_GROUPS = 4
EXPERTS_PER_GROUP = 8
N_EXPERTS = N_GROUPS * EXPERTS_PER_GROUP
EXPERT_TOP_K = 2
EXPERT_FF = 512

LN_EPS = 1e-5
ALPHA = (2.0 * DEPTH) ** 0.25
BETA = (8.0 * DEPTH) ** -0.25

Q_OFF = 0
K_OFF = Q_OFF + RET_QK
V_OFF = K_OFF + RET_QK
G_OFF = V_OFF + RET_V
GLU_OFF = G_OFF + RET_V
GATE_OFF = GLU_OFF + 2 * CONV_DIM
IN_COLS = GATE_OFF + N_BRANCHES * D_MODEL


def _layernorm(x, g, b):
    xf = x.astype(jnp.float32)
    mu = xf.mean(-1, keepdims=True)
    var = jnp.square(xf - mu).mean(-1, keepdims=True)
    return (xf - mu) * lax.rsqrt(var + LN_EPS) * g + b

def _head_norm(o):
    of = o.astype(jnp.float32)
    mu = of.mean(-1, keepdims=True)
    var = jnp.square(of - mu).mean(-1, keepdims=True)
    return (of - mu) * lax.rsqrt(var + LN_EPS)

def _modulate(h, shift, scale):
    return h * (1.0 + scale) + shift

def _rope_2d(rows):
    r, col = jnp.meshgrid(jnp.arange(rows), jnp.arange(GRID_W), indexing='ij')
    r = r.reshape(-1).astype(jnp.float32)
    col = col.reshape(-1).astype(jnp.float32)
    n_freq = RET_QK_DIM // 4
    inv = ROPE_BASE ** (-jnp.arange(n_freq, dtype=jnp.float32) / n_freq)
    ang = jnp.concatenate([r[:, None] * inv, col[:, None] * inv], axis=-1)
    ang = jnp.concatenate([ang, ang], axis=-1)
    return jnp.cos(ang), jnp.sin(ang)

def _apply_rope(t, cos, sin):
    t1, t2 = jnp.split(t, 2, axis=-1)
    rot = jnp.concatenate([-t2, t1], axis=-1)
    return t * cos[None, :, None, :] + rot * sin[None, :, None, :]

def _split_proj(proj):
    b_, l_ = proj.shape[:2]
    q = proj[..., Q_OFF:K_OFF].reshape(b_, l_, RET_HEADS, RET_QK_DIM)
    k = proj[..., K_OFF:V_OFF].reshape(b_, l_, RET_HEADS, RET_QK_DIM) * RET_QK_DIM ** -0.5
    v = proj[..., V_OFF:G_OFF].reshape(b_, l_, RET_HEADS, RET_V_DIM)
    g = proj[..., G_OFF:GLU_OFF]
    glu = proj[..., GLU_OFF:GATE_OFF]
    gates = proj[..., GATE_OFF:]
    return q, k, v, g, glu, gates

def _retention_chunked(q, k, v, log_gamma, s0):
    b_, l_, h_, _ = q.shape
    dv = v.shape[-1]
    n_chunks = l_ // RET_CHUNK
    pos = jnp.arange(RET_CHUNK, dtype=jnp.float32)
    diff = pos[:, None] - pos[None, :]
    intra = jnp.where(diff >= 0, jnp.exp(jnp.maximum(diff, 0.0)[None] * log_gamma[:, None, None]), 0.0)
    q_dec = jnp.exp((pos[:, None] + 1.0) * log_gamma[None, :])
    k_dec = jnp.exp((RET_CHUNK - 1.0 - pos)[:, None] * log_gamma[None, :])
    c_dec = jnp.exp(RET_CHUNK * log_gamma)

    def to_chunks(t):
        return jnp.moveaxis(t.reshape(b_, n_chunks, RET_CHUNK, h_, t.shape[-1]), 1, 0)

    def step(s, qkv):
        qc, kc, vc = qkv
        scores = jnp.einsum('bihd,bjhd->bhij', qc, kc) * intra
        o = (jnp.einsum('bhij,bjhv->bihv', scores, vc)
             + jnp.einsum('bihd,bhdv->bihv', qc * q_dec[None, :, :, None], s))
        s = s * c_dec[None, :, None, None] + jnp.einsum('bjhd,bjhv->bhdv', kc * k_dec[None, :, :, None], vc)
        return s, o

    s_fin, o = lax.scan(step, s0, (to_chunks(q), to_chunks(k), to_chunks(v)))
    o = jnp.moveaxis(o, 0, 1).reshape(b_, l_, h_, dv)
    return o, s_fin

def _retention_bidir(q, k, v, lg_f, lg_b, s0_f, s0_b):
    o_f, s_f = _retention_chunked(q, k, v, lg_f, s0_f)
    o_b, s_b = _retention_chunked(q[:, ::-1], k[:, ::-1], v[:, ::-1], lg_b, s0_b)
    return o_f + o_b[:, ::-1], s_f, s_b

def _retention_final_state(k, v, log_gamma):
    l_ = k.shape[1]
    w = jnp.exp((l_ - 1.0 - jnp.arange(l_, dtype=jnp.float32))[:, None] * log_gamma[None, :])
    return jnp.einsum('blhd,blhv->bhdv', k * w[None, :, :, None], v)

def _depthwise_conv(z, w, b):
    out = lax.conv_general_dilated(
        z, w[:, None, :].astype(z.dtype), window_strides=(1,),
        padding=[(CONV_WIDTH // 2, CONV_WIDTH // 2)],
        dimension_numbers=('NWC', 'WIO', 'NWC'), feature_group_count=z.shape[-1])
    return out + b

def _merge_branches(o_ret, g, glu, gates, p):
    b_, l_ = g.shape[:2]
    ret = jax.nn.silu(g.astype(jnp.float32)) * _head_norm(o_ret).reshape(b_, l_, RET_V)
    y_a = ret @ p['w_ret_out']
    za, zb = jnp.split(glu, 2, axis=-1)
    z = za * jax.nn.sigmoid(zb)
    z = _depthwise_conv(z, p['conv_dw'], p['conv_dw_b'])
    z = jax.nn.silu(_layernorm(z, p['conv_ln_g'], p['conv_ln_b']))
    y_b = z @ p['w_conv_out'] + p['b_conv_out']
    ga, gb = jnp.split(jax.nn.sigmoid(gates.astype(jnp.float32)), 2, axis=-1)
    return (ga * y_a + gb * y_b) @ p['w_mix_out'] + p['b_mix_out']

def _hier_moe(u, p):
    b_, l_, d_ = u.shape
    t = u.reshape(b_ * l_, d_)
    grp_p = jax.nn.softmax((t @ p['w_router_grp'] + p['b_router_grp']).astype(jnp.float32), axis=-1)
    grp_w, grp_idx = lax.top_k(grp_p, 1)
    exp_logits = (t @ p['w_router_exp'] + p['b_router_exp']).astype(jnp.float32)
    exp_logits = exp_logits.reshape(-1, N_GROUPS, EXPERTS_PER_GROUP)
    in_grp = jnp.take_along_axis(exp_logits, grp_idx[:, :, None], axis=1)[:, 0]
    top_w, top_i = lax.top_k(jax.nn.softmax(in_grp, axis=-1), EXPERT_TOP_K)
    top_w = top_w / top_w.sum(-1, keepdims=True) * grp_w
    eid = grp_idx * EXPERTS_PER_GROUP + top_i
    combine = jnp.einsum('nk,nke->ne', top_w, jax.nn.one_hot(eid, N_EXPERTS, dtype=jnp.float32))
    y = jnp.zeros(t.shape, jnp.float32)
    for e in range(N_EXPERTS):
        h = jax.nn.silu(t @ p['w_exp_gate'][e]) * (t @ p['w_exp_up'][e])
        y = y + combine[:, e:e + 1] * (h @ p['w_exp_down'][e])
    return y.reshape(b_, l_, d_)

def _layer(h_lat, h_ctx, s_lat, s_ctx, p, cos, sin, update_ctx):
    mod_lat = s_lat @ p['w_ada'] + p['b_ada']
    mod_ctx = s_ctx @ p['w_ada'] + p['b_ada']
    sh_m, sc_m, gt_m, sh_f, sc_f, gt_f = jnp.split(mod_lat[:, None, :], 6, axis=-1)
    csh_m, csc_m, cgt_m, csh_f, csc_f, cgt_f = jnp.split(mod_ctx, 6, axis=-1)
    lg_f = jax.nn.log_sigmoid(p['ret_decay_fwd'].astype(jnp.float32))
    lg_b = jax.nn.log_sigmoid(p['ret_decay_bwd'].astype(jnp.float32))
    b_ = h_lat.shape[0]

    u_ctx = _modulate(h_ctx, csh_m, csc_m)
    if update_ctx:
        q_c, k_c, v_c, g_c, glu_c, gates_c = _split_proj(u_ctx @ p['w_in'] + p['b_in'])
        zeros = jnp.zeros((b_, RET_HEADS, RET_QK_DIM, RET_V_DIM), jnp.float32)
        o_c, s_f, s_b = _retention_bidir(q_c, k_c, v_c, lg_f, lg_b, zeros, zeros)
    else:
        kv = u_ctx @ p['w_in'][:, K_OFF:G_OFF] + p['b_in'][K_OFF:G_OFF]
        k_c = kv[..., :RET_QK].reshape(b_, -1, RET_HEADS, RET_QK_DIM) * RET_QK_DIM ** -0.5
        v_c = kv[..., RET_QK:].reshape(b_, -1, RET_HEADS, RET_V_DIM)
        s_f = _retention_final_state(k_c, v_c, lg_f)
        s_b = _retention_final_state(k_c[:, ::-1], v_c[:, ::-1], lg_b)

    u_lat = _modulate(h_lat, sh_m, sc_m)
    q, k, v, g, glu, gates = _split_proj(u_lat @ p['w_in'] + p['b_in'])
    q = _apply_rope(q, cos, sin)
    k = _apply_rope(k, cos, sin)
    o, _, _ = _retention_bidir(q, k, v, lg_f, lg_b, s_f, s_b)
    mix = _merge_branches(o, g, glu, gates, p)
    h_lat = _layernorm(ALPHA * h_lat + gt_m * mix, p['ln1_g'], p['ln1_b'])
    moe = _hier_moe(_modulate(h_lat, sh_f, sc_f), p)
    h_lat = _layernorm(ALPHA * h_lat + gt_f * moe, p['ln2_g'], p['ln2_b'])

    if update_ctx:
        mix_c = _merge_branches(o_c, g_c, glu_c, gates_c, p)
        h_ctx = _layernorm(ALPHA * h_ctx + cgt_m * mix_c, p['ln1_g'], p['ln1_b'])
        moe_c = _hier_moe(_modulate(h_ctx, csh_f, csc_f), p)
        h_ctx = _layernorm(ALPHA * h_ctx + cgt_f * moe_c, p['ln2_g'], p['ln2_b'])
    return h_lat, h_ctx

def first_inputs(seed: int = 0) -> dict:
    key = jax.random.key(seed)
    ks = jax.random.split(key, 32)
    f32 = jnp.float32
    D = D_MODEL

    def nrm(k, shape, scale):
        return jax.random.normal(k, shape, f32) * scale

    gamma0 = 1.0 - 2.0 ** (-5.0 - np.arange(RET_HEADS))
    logit0 = jnp.asarray(np.log(gamma0 / (1.0 - gamma0)), f32)
    return {
        'x': nrm(ks[0], (BATCH, SEQ, D), 1.0),
        'c': nrm(ks[1], (BATCH, D), 1.0),
        'ctx': nrm(ks[2], (BATCH, CTX_LEN, D), 1.0),
        'c_ctx': nrm(ks[3], (D,), 1.0),
        'w_ada': nrm(ks[4], (DEPTH, D, 6 * D), 0.5 * D ** -0.5),
        'b_ada': nrm(ks[5], (DEPTH, 6 * D), 0.01),
        'w_in': nrm(ks[6], (DEPTH, D, IN_COLS), D ** -0.5),
        'b_in': nrm(ks[7], (DEPTH, IN_COLS), 0.01),
        'ret_decay_fwd': logit0 + nrm(ks[8], (DEPTH, RET_HEADS), 0.1),
        'ret_decay_bwd': logit0 + nrm(ks[9], (DEPTH, RET_HEADS), 0.1),
        'w_ret_out': nrm(ks[10], (DEPTH, RET_V, D), RET_V ** -0.5),
        'conv_dw': nrm(ks[11], (DEPTH, CONV_WIDTH, CONV_DIM), CONV_WIDTH ** -0.5),
        'conv_dw_b': nrm(ks[12], (DEPTH, CONV_DIM), 0.01),
        'conv_ln_g': 1.0 + nrm(ks[13], (DEPTH, CONV_DIM), 0.02),
        'conv_ln_b': nrm(ks[14], (DEPTH, CONV_DIM), 0.01),
        'w_conv_out': nrm(ks[15], (DEPTH, CONV_DIM, D), CONV_DIM ** -0.5),
        'b_conv_out': nrm(ks[16], (DEPTH, D), 0.01),
        'w_mix_out': nrm(ks[17], (DEPTH, D, D), BETA * D ** -0.5),
        'b_mix_out': nrm(ks[18], (DEPTH, D), 0.01),
        'ln1_g': 1.0 + nrm(ks[19], (DEPTH, D), 0.02),
        'ln1_b': nrm(ks[20], (DEPTH, D), 0.01),
        'w_router_grp': nrm(ks[21], (DEPTH, D, N_GROUPS), D ** -0.5),
        'b_router_grp': nrm(ks[22], (DEPTH, N_GROUPS), 0.01),
        'w_router_exp': nrm(ks[23], (DEPTH, D, N_EXPERTS), D ** -0.5),
        'b_router_exp': nrm(ks[24], (DEPTH, N_EXPERTS), 0.01),
        'w_exp_gate': nrm(ks[25], (DEPTH, N_EXPERTS, D, EXPERT_FF), D ** -0.5),
        'w_exp_up': nrm(ks[26], (DEPTH, N_EXPERTS, D, EXPERT_FF), D ** -0.5),
        'w_exp_down': nrm(ks[27], (DEPTH, N_EXPERTS, EXPERT_FF, D), BETA * EXPERT_FF ** -0.5),
        'ln2_g': 1.0 + nrm(ks[28], (DEPTH, D), 0.02),
        'ln2_b': nrm(ks[29], (DEPTH, D), 0.01),
    }

def first_block(x, c, ctx, c_ctx, w_ada, b_ada, w_in, b_in, ret_decay_fwd, ret_decay_bwd, w_ret_out,
              conv_dw, conv_dw_b, conv_ln_g, conv_ln_b, w_conv_out, b_conv_out, w_mix_out, b_mix_out,
              ln1_g, ln1_b, w_router_grp, b_router_grp, w_router_exp, b_router_exp,
              w_exp_gate, w_exp_up, w_exp_down, ln2_g, ln2_b):
    rows = x.shape[1] // GRID_W
    cos, sin = _rope_2d(rows)
    s_lat = jax.nn.silu(c)
    s_ctx = jax.nn.silu(c_ctx)
    h_lat, h_ctx = x, ctx
    for layer in range(DEPTH):
        p = dict(
            w_ada=w_ada[layer], b_ada=b_ada[layer], w_in=w_in[layer], b_in=b_in[layer],
            ret_decay_fwd=ret_decay_fwd[layer], ret_decay_bwd=ret_decay_bwd[layer],
            w_ret_out=w_ret_out[layer], conv_dw=conv_dw[layer], conv_dw_b=conv_dw_b[layer],
            conv_ln_g=conv_ln_g[layer], conv_ln_b=conv_ln_b[layer], w_conv_out=w_conv_out[layer],
            b_conv_out=b_conv_out[layer], w_mix_out=w_mix_out[layer], b_mix_out=b_mix_out[layer],
            ln1_g=ln1_g[layer], ln1_b=ln1_b[layer], w_router_grp=w_router_grp[layer],
            b_router_grp=b_router_grp[layer], w_router_exp=w_router_exp[layer],
            b_router_exp=b_router_exp[layer], w_exp_gate=w_exp_gate[layer], w_exp_up=w_exp_up[layer],
            w_exp_down=w_exp_down[layer], ln2_g=ln2_g[layer], ln2_b=ln2_b[layer])
        h_lat, h_ctx = _layer(h_lat, h_ctx, s_lat, s_ctx, p, cos, sin, layer + 1 < DEPTH)
    return h_lat


DEPTH_2 = 2

N_MIXERS = 2
RMS_EPS = 1e-6

GMLP_EXPAND = 2
GMLP_WIDTH = GMLP_EXPAND * D_MODEL
GMLP_CHUNK = 128
GMLP_GROUPS = 8
GMLP_GROUP_WIDTH = GMLP_WIDTH // GMLP_GROUPS

HEAD_DIM = 64
HEADS_PER_GROUP = D_MODEL // HEAD_DIM
DILATED_GROUPS = ((128, 1), (512, 4), (2048, 16))
N_DIL_GROUPS = len(DILATED_GROUPS)
ATTN_WIDTH = HEADS_PER_GROUP * HEAD_DIM
ATTN_BLOCK = 128
ROPE_THETA = 10000.0

N_A_LAYERS = (DEPTH_2 + 1) // 2
N_B_LAYERS = DEPTH_2 // 2


def rms_norm(x, gain):
    xf = x.astype(jnp.float32)
    y = xf * lax.rsqrt(jnp.mean(xf * xf, axis=-1, keepdims=True) + RMS_EPS)
    return (y * gain.astype(jnp.float32)).astype(x.dtype)

def layer_norm(x, gain, bias):
    xf = x.astype(jnp.float32)
    mu = jnp.mean(xf, axis=-1, keepdims=True)
    var = jnp.mean(jnp.square(xf - mu), axis=-1, keepdims=True)
    y = (xf - mu) * lax.rsqrt(var + LN_EPS)
    return (y * gain.astype(jnp.float32) + bias.astype(jnp.float32)).astype(x.dtype)

def rope_tables(seq_len):
    inv_freq = 1.0 / (ROPE_THETA ** (jnp.arange(0, HEAD_DIM, 2, dtype=jnp.float32) / HEAD_DIM))
    ang = jnp.arange(seq_len, dtype=jnp.float32)[:, None] * inv_freq[None, :]
    return jnp.cos(ang), jnp.sin(ang)

def apply_rope(t, cos, sin):
    tf = t.astype(jnp.float32)
    t1, t2 = tf[..., : HEAD_DIM // 2], tf[..., HEAD_DIM // 2:]
    c = cos[None, :, None, :]
    s = sin[None, :, None, :]
    return jnp.concatenate([t1 * c - t2 * s, t2 * c + t1 * s], axis=-1).astype(t.dtype)

def gmlp_mixer(h, w_in, ln_g, ln_b, w_s, b_s, w_out):
    B, S, _ = h.shape
    proj = h @ w_in
    uv = jax.nn.gelu(proj[..., : 2 * GMLP_WIDTH], approximate=False)
    z = proj[..., 2 * GMLP_WIDTH:]
    u, v = uv[..., :GMLP_WIDTH], uv[..., GMLP_WIDTH:]
    v = layer_norm(v, ln_g, ln_b)
    n_chunks = S // GMLP_CHUNK
    vc = v.reshape(B, n_chunks, GMLP_CHUNK, GMLP_GROUPS, GMLP_GROUP_WIDTH)
    causal = jnp.tril(jnp.ones((GMLP_CHUNK, GMLP_CHUNK), dtype=bool))
    w_masked = jnp.where(causal[None], w_s, jnp.zeros_like(w_s))
    sv = jnp.einsum('gts,bnsgc->bntgc', w_masked, vc) + jnp.transpose(b_s)[None, None, :, :, None]
    sv = sv.reshape(B, S, GMLP_WIDTH)
    y = u * sv * jax.nn.silu(z)
    return y @ w_out

def dilated_window_attention(q, k, v, window, dilation):
    B, S, H, Dh = q.shape
    steps = window // dilation
    L = S // dilation
    Lp = ((L + ATTN_BLOCK - 1) // ATTN_BLOCK) * ATTN_BLOCK
    N = Lp // ATTN_BLOCK

    def to_blocks(t):
        t = t.reshape(B, L, dilation, H, Dh).transpose(0, 2, 1, 3, 4)
        t = jnp.pad(t, ((0, 0), (0, 0), (0, Lp - L), (0, 0), (0, 0)))
        return t.reshape(B, dilation, N, ATTN_BLOCK, H, Dh)

    qb, kb, vb = to_blocks(q), to_blocks(k), to_blocks(v)
    pad_prev = ((0, 0), (0, 0), (1, 0), (0, 0), (0, 0), (0, 0))
    kk = jnp.concatenate([jnp.pad(kb, pad_prev)[:, :, :-1], kb], axis=3)
    vv = jnp.concatenate([jnp.pad(vb, pad_prev)[:, :, :-1], vb], axis=3)

    scale = 1.0 / np.sqrt(HEAD_DIM)
    scores = jnp.einsum('brnihk,brnjhk->brnhij', qb.astype(jnp.float32), kk.astype(jnp.float32)) * scale
    i_idx = jnp.arange(ATTN_BLOCK)[:, None]
    j_idx = jnp.arange(2 * ATTN_BLOCK)[None, :]
    n_idx = jnp.arange(N)[:, None, None]
    rel = ATTN_BLOCK + i_idx - j_idx
    valid = (rel >= 0) & (rel <= steps)
    valid = valid[None] & ((n_idx - 1) * ATTN_BLOCK + j_idx[None] >= 0)
    scores = jnp.where(valid[None, None, :, None], scores, -jnp.inf)
    lse = jax.nn.logsumexp(scores, axis=-1)
    p = jnp.exp(scores - lse[..., None])
    o = jnp.einsum('brnhij,brnjhk->brnihk', p.astype(v.dtype), vv)

    o = o.reshape(B, dilation, Lp, H, Dh)[:, :, :L]
    o = o.transpose(0, 2, 1, 3, 4).reshape(B, S, H, Dh)
    lse = lse.transpose(0, 1, 2, 4, 3).reshape(B, dilation, Lp, H)[:, :, :L]
    lse = lse.transpose(0, 2, 1, 3).reshape(B, S, H)
    return o, lse

def dilated_attention_mixer(h, w_in, w_out, cos, sin):
    B, S, _ = h.shape
    proj = h @ w_in
    qkv_width = N_DIL_GROUPS * 3 * ATTN_WIDTH
    qkv = proj[..., :qkv_width].reshape(B, S, N_DIL_GROUPS, 3, HEADS_PER_GROUP, HEAD_DIM)
    z = proj[..., qkv_width:]
    outs, lses = [], []
    for g, (window, dilation) in enumerate(DILATED_GROUPS):
        q = apply_rope(qkv[:, :, g, 0], cos, sin)
        k = apply_rope(qkv[:, :, g, 1], cos, sin)
        o, lse = dilated_window_attention(q, k, qkv[:, :, g, 2], window, dilation)
        outs.append(o)
        lses.append(lse)
    alpha = jax.nn.softmax(jnp.stack(lses, axis=0), axis=0)
    o = jnp.einsum('gbsh,gbshk->bshk', alpha, jnp.stack(outs, axis=0).astype(jnp.float32))
    y = o.astype(h.dtype).reshape(B, S, ATTN_WIDTH) * jax.nn.silu(z)
    return y @ w_out

def second_inputs(seed: int = 0) -> dict:
    key = jax.random.key(seed)
    ks = jax.random.split(key, 12)
    D = D_MODEL
    x = jax.random.normal(ks[0], (BATCH, SEQ, D), jnp.float32)
    norm_pre = 1.0 + 0.05 * jax.random.normal(ks[1], (DEPTH_2, D), jnp.float32)
    norm_post = 1.0 + 0.05 * jax.random.normal(ks[2], (DEPTH_2, D), jnp.float32)
    a_w_in = jax.random.normal(ks[3], (N_A_LAYERS, D, 3 * GMLP_WIDTH), jnp.float32) * D ** -0.5
    a_ln_g = 1.0 + 0.05 * jax.random.normal(ks[4], (N_A_LAYERS, GMLP_WIDTH), jnp.float32)
    a_ln_b = 0.02 * jax.random.normal(ks[5], (N_A_LAYERS, GMLP_WIDTH), jnp.float32)
    a_w_s = jax.random.normal(ks[6], (N_A_LAYERS, GMLP_GROUPS, GMLP_CHUNK, GMLP_CHUNK), jnp.float32) * GMLP_CHUNK ** -0.5
    a_b_s = 1.0 + 0.1 * jax.random.normal(ks[7], (N_A_LAYERS, GMLP_GROUPS, GMLP_CHUNK), jnp.float32)
    a_w_out = jax.random.normal(ks[8], (N_A_LAYERS, GMLP_WIDTH, D), jnp.float32) * GMLP_WIDTH ** -0.5
    b_w_in = jax.random.normal(ks[9], (N_B_LAYERS, D, N_DIL_GROUPS * 3 * ATTN_WIDTH + ATTN_WIDTH), jnp.float32) * D ** -0.5
    b_w_out = jax.random.normal(ks[10], (N_B_LAYERS, ATTN_WIDTH, D), jnp.float32) * ATTN_WIDTH ** -0.5
    return {"x": x, "norm_pre": norm_pre, "norm_post": norm_post,
            "a_w_in": a_w_in, "a_ln_g": a_ln_g, "a_ln_b": a_ln_b, "a_w_s": a_w_s,
            "a_b_s": a_b_s, "a_w_out": a_w_out, "b_w_in": b_w_in, "b_w_out": b_w_out}

def second_block(x, norm_pre, norm_post, a_w_in, a_ln_g, a_ln_b, a_w_s, a_b_s, a_w_out, b_w_in, b_w_out):
    cos, sin = rope_tables(x.shape[1])
    for i in range(DEPTH_2):
        h = rms_norm(x, norm_pre[i])
        j = i // N_MIXERS
        if i % N_MIXERS == 0:
            y = gmlp_mixer(h, a_w_in[j], a_ln_g[j], a_ln_b[j], a_w_s[j], a_b_s[j], a_w_out[j])
        else:
            y = dilated_attention_mixer(h, b_w_in[j], b_w_out[j], cos, sin)
        x = x + rms_norm(y, norm_post[i])
    return x


def setup_inputs(seed=0):
    out = dict(first_inputs(seed))
    for name, value in second_inputs(seed + 1).items():
        if name != "x":
            out[name + "_2"] = value
    return out


def reference(
    x, c, ctx, c_ctx, w_ada, b_ada, w_in, b_in, ret_decay_fwd, ret_decay_bwd, w_ret_out,
    conv_dw, conv_dw_b, conv_ln_g, conv_ln_b, w_conv_out, b_conv_out, w_mix_out, b_mix_out,
    ln1_g, ln1_b, w_router_grp, b_router_grp, w_router_exp, b_router_exp, w_exp_gate, w_exp_up,
    w_exp_down, ln2_g, ln2_b, norm_pre_2, norm_post_2, a_w_in_2, a_ln_g_2, a_ln_b_2, a_w_s_2,
    a_b_s_2, a_w_out_2, b_w_in_2, b_w_out_2,
):
    x = first_block(
        x, c, ctx, c_ctx, w_ada, b_ada, w_in, b_in, ret_decay_fwd, ret_decay_bwd, w_ret_out,
        conv_dw, conv_dw_b, conv_ln_g, conv_ln_b, w_conv_out, b_conv_out, w_mix_out, b_mix_out,
        ln1_g, ln1_b, w_router_grp, b_router_grp, w_router_exp, b_router_exp, w_exp_gate,
        w_exp_up, w_exp_down, ln2_g, ln2_b,
    )
    return second_block(
        x, norm_pre_2, norm_post_2, a_w_in_2, a_ln_g_2, a_ln_b_2, a_w_s_2, a_b_s_2, a_w_out_2,
        b_w_in_2, b_w_out_2,
    )


_drawn_inputs = setup_inputs


def setup_inputs(seed=0):
    import zlib

    import numpy as np

    out = dict(_drawn_inputs(seed))
    spreads = {}
    factors = {'b_ada': 5.249,
     'b_in': 8.0,
     'conv_dw_b': 8.0,
     'conv_ln_g': 26.051,
     'conv_ln_b': 49.476,
     'b_conv_out': 32.61,
     'b_mix_out': 21.913,
     'b_router_grp': 22.998,
     'b_router_exp': 28.041,
     'a_ln_b_2': 5.443,
     'ret_decay_fwd': 3.601,
     'ret_decay_bwd': 3.572,
     'ln1_b': 2.957,
     'ln2_b': 3.235}
    for name, (base, spread) in spreads.items():
        noise = np.random.default_rng([zlib.crc32(name.encode()), seed]).standard_normal(out[name].shape)
        drawn = base * np.exp(spread * noise) if base else spread * noise
        out[name] = __import__('jax').numpy.asarray(drawn.astype(out[name].dtype))
    for name, factor in factors.items():
        out[name] = (out[name] * factor).astype(out[name].dtype)
    return out
```

```python
from contextlib import ExitStack

import numpy as np

import concourse.bass as bass
from concourse import mybir

F32 = mybir.dt.float32
ALU = mybir.AluOpType
ACT = mybir.ActivationFunctionType
AX_X = mybir.AxisListType.X

P = 128
T = 256
NT = T // P
D = 1024
KC = D // P
W = 512
HALF_K = 512
UC = HALF_K // P
H = 8
DK = 128
DV = 256
TAPS = 31
PAD = TAPS // 2
NG, NEG = 4, 8
NE = NG * NEG
FF = 512
SLOTS = 128
ROUNDS = T // SLOTS
HEADS = 16
HD = 64
DIL = 3
LN_EPS = 1e-5
RMS_EPS = 1e-6
ALPHA = 2.0 ** 0.25
RING = 6
ARENA = 53200
AUXN = 4

GLU = [12, 14, 13, 15]
KCOLS = [2, 3]
VCOLS = [4, 5, 6, 7]
QCOLS = [0, 1]
GCOLS = [8, 9, 10, 11]
GATECOLS = [16, 17, 18, 19]
BCOLS = list(range(12)) + [12, 13, 14, 15, 18, 19, 16, 17]
BKIND = (["q", "q", "k", "k", "v", "v"] * 2) + ["q", "q", "k", "k", "z", "z", "v", "v"]
BGROUP = [0] * 6 + [1] * 6 + [2] * 8
BIDX = [0, 1] * 10


def attention_slots():
    after = {t: [] for t in range(20)}
    for g, first in ((0, 5), (1, 11), (2, 16)):
        for c in range(4):
            for stage, name in enumerate(("scores", "turn", "values")):
                t = first + c + stage
                late = t > 19 or (g == 2 and name == "values")
                after[19 if late else t].append(((3 + stage, c) if late else (2 - stage, c), name, g, c))
    return {t: [s[1:] for s in sorted(steps)] for t, steps in after.items()}


def build(nc, a, out):
    with ExitStack() as ctx:
        sems = {}

        def S(name):
            if name not in sems:
                sems[name] = ctx.enter_context(nc.semaphore(name))
            return sems[name]

        arena = ctx.enter_context(nc.sbuf_tensor("arena", [P, ARENA], F32))
        at = [0]

        def carve(*shape, on=None):
            n = int(np.prod(shape))
            o = at[0] if on is None else on
            if on is None:
                at[0] += n
                assert at[0] <= ARENA, at[0]
            v = arena[:, o:o + n]
            if len(shape) == 2:
                v = v.rearrange("p (a b) -> p a b", a=shape[0])
            if len(shape) == 3:
                v = v.rearrange("p (a b c) -> p a b c", a=shape[0], b=shape[1])
            if len(shape) == 4:
                v = v.rearrange("p (a b c d) -> p a b c d", a=shape[0], b=shape[1], c=shape[2])
            return v, o

        ring, _ = carve(RING, UC, W)
        aux, _ = carve(AUXN, W)
        x, _ = carve(NT, D)
        XT, o_XT = carve(16, T)
        XT2, o_XT2 = carve(8, T)
        mod_lat, o_ml = carve(2048)
        z_pad, o_zp = carve(KC, T + 2 * PAD)
        tmp, o_tmp = carve(6, W)
        qT, o_qT = carve(H, T)
        kT, o_kT = carve(H, T)
        v_lat, o_v = carve(NT, H * DV)
        k_ctx, o_kc = carve(NT, D)
        v_ctx, o_vc = carve(NT, H * DV)
        state, o_S = carve(H, 2, DV)
        consts, o_cn = carve(3 * NT * T + 2 * T + 2 * NT * P + 4 * NT * HD + DIL * 2 * P + P)
        small, o_sm = carve(836)

        conv, _ = carve(KC, T, on=o_ml)
        cz, _ = carve(NT, D, on=o_zp)
        mod_ctx, _ = carve(2048, on=o_S)
        z_tok, _ = carve(2, NT, W, on=o_S + 2048)
        roped, _ = carve(2, NT, W, on=o_XT2)
        o_lo, _ = carve(NT, 4 * DV, on=o_kc)
        o_hi, _ = carve(NT, 4 * DV, on=o_XT2)
        sg, _ = carve(NT, H * DV, on=o_vc)
        gates, _ = carve(NT, 2048, on=o_v)
        mod_tail, _ = carve(4096, on=o_S)
        u_lat, _ = carve(NT, D, on=o_v)
        u_ctx, _ = carve(NT, D, on=o_v + 2048)
        x_ctx, _ = carve(NT, D, on=o_vc)
        s_lat, _ = carve(KC, P, on=o_qT)
        s_ctx, _ = carve(KC, P, on=o_kT)
        rows16 = arena[0:16, o_tmp:o_tmp + P]
        rows32 = arena[0:32, o_tmp + 1024:o_tmp + 2048]

        o = o_cn

        def const(*shape):
            nonlocal o
            v, _ = carve(*shape, on=o)
            o += int(np.prod(shape))
            return v
        dist_f = const(NT, T)
        dist_b = const(NT, T)
        log_c = const(NT, T)
        row_fb = const(2, T)
        rope1 = const(2, NT, P)
        rope2 = const(2, 2, NT, HD)
        amask = const(DIL, 2 * P)
        ident = const(P)
        o = o_sm
        lg = const(2 * H)
        la = const(3, 2 * H)
        pos = const(2, NT)
        wdec = const(2, NT, H)
        sT = const(2 * KC)
        cwT = const(KC, 32)
        stats = const(NT, 4, 6)
        mv = const(NT, 2)
        ms = const(NT)
        rstd = const(NT)
        minus_half = const(NT)
        sq = const(NT)
        wr = const(KC, 36)
        br = const(36)
        lgt = const(NT, 36)
        assert o <= o_sm + 836

        flag = ctx.enter_context(nc.sbuf_tensor("flag", [1, 1], mybir.dt.int32))
        ps = ctx.enter_context(nc.psum_tensor("ps", [P, 8, W], F32))

        def pair(p):
            return ps[:, 2 * p:2 * p + 2, :]

        units = []
        first = {}

        def stream(name, w, cols, nk):
            first[name] = len(units)
            for c in cols:
                for j in range(nk):
                    units.append(w[HALF_K * j:HALF_K * (j + 1), W * c:W * (c + 1)])

        w_in = a["w_in"][0]
        stream("ada", a["w_ada"][0], range(4), 2)
        for name, cols in (("glu", GLU), ("k", KCOLS), ("v", VCOLS), ("q", QCOLS), ("g", GCOLS), ("gate", GATECOLS)):
            stream(name, w_in, cols, 2)
        stream("ada_tail", a["w_ada"][0], range(4, 12), 2)
        stream("ret", a["w_ret_out"][0], range(2), 4)
        stream("conv", a["w_conv_out"][0], range(2), 2)
        stream("mix", a["w_mix_out"][0], range(2), 2)
        n_before = len(units)
        first["moe"] = n_before
        n_moe = 6 * NE
        units += [None] * n_moe
        stream("a", a["a_w_in_2"][0], [4, 5, 6, 7, 0, 1, 2, 3, 8, 9, 10, 11], 2)
        stream("a_out", a["a_w_out_2"][0], range(2), 4)
        stream("b", a["b_w_in_2"][0], BCOLS, 2)
        stream("b_out", a["b_w_out_2"][0], range(2), 2)

        def moe_src(kind, e, j):
            if kind == "down":
                return a["w_exp_down"][0, bass.ds(e, 1), :, W * j:W * (j + 1)].rearrange("e (k p) c -> p (e k) c", p=P)
            w = a["w_exp_gate"] if kind == "gate" else a["w_exp_up"]
            return w[0, bass.ds(e, 1), HALF_K * j:HALF_K * (j + 1), :].rearrange("e (k p) c -> p (e k) c", p=P)

        def end_of(name, t, nk=2):
            return first[name] + (t + 1) * nk

        rows = []
        row_after = {}
        row_of = {}

        def bring(key, vec, unit):
            row_of[key] = len(rows)
            rows.append(vec)
            row_after.setdefault(unit, []).append(len(rows) - 1)

        def vec(name, c, i=0):
            return a[name][i:i + 1, W * c:W * (c + 1)]

        used = [0] * 4
        plan = {}

        def take(key, p):
            used[p] += 1
            plan[key] = (p, used[p])

        main = [0]

        def take_main(key):
            take(key, main[0] % 2)
            main[0] += 1

        side = [0]

        def take_side(key):
            take(key, 2 + side[0] % 2)
            side[0] += 1

        take("turn_rows", 2)
        for t in range(4):
            take_main(("ada", t))
            bring(("ada", t), vec("b_ada", t), t)
        for s in range(2):
            for c in range(2):
                take_side(("uT", s, c))
        for t in range(4):
            take_main(("glu", t))
            bring(("glu", t), vec("b_in", GLU[t]), first["glu"] + 2 * t + 1)
        take_side(("zT", 0))
        take_side(("zT", 1))
        if main[0] % 2:
            main[0] += 1
        for t in range(2):
            take("k_lat%d" % t, 0)
            take("k_ctx%d" % t, 1)
            bring(("k", t), vec("b_in", KCOLS[t]), first["k"] + 2 * t + 1)
        take_side(("kT", 0))
        for t in range(4):
            take("v_lat%d" % t, 0)
            take("v_ctx%d" % t, 1)
            bring(("v", t), vec("b_in", VCOLS[t]), first["v"] + 2 * t + 1)
        take_side(("kT", 1))
        for t in range(2):
            take_main(("q", t))
            bring(("q", t), vec("b_in", QCOLS[t]), first["q"] + 2 * t + 1)
        take_side(("qT", 0))
        take_side(("qT", 1))
        for i in range(4):
            take_side(("S", i))
        for c in range(2):
            take_side(("cz", c))
        side[0] += side[0] % 2
        for i in range(4):
            take(("sc", i), 2)
            take(("av", i), 3)
            take_main(("g", i))
            bring(("g", i), vec("b_in", GCOLS[i]), first["g"] + 2 * i + 1)
        for c in range(2):
            bring(("conv_g", c), vec("conv_ln_g", c), first["gate"] + 1)
            bring(("conv_b", c), vec("conv_ln_b", c), first["gate"] + 1)
        for t in range(4):
            take_main(("gate", t))
            bring(("gate", t), vec("b_in", GATECOLS[t]), first["gate"] + 2 * t + 4)
        for t in range(8):
            take_main(("ada_tail", t))
            bring(("ada_tail", t), vec("b_ada", 4 + t), first["ada_tail"] + 2 * t + 4)
        for c in range(4):
            take_side(("retT", c))
        for c in range(2):
            take_side(("cvT", c))
        for t in range(2):
            take_main(("ret", t))
        for t in range(2):
            take_main(("conv", t))
            bring(("conv", t), vec("b_conv_out", t), first["conv"] + 2 * t + 1)
        for c in range(2):
            take_side(("mT", c))
        for t in range(2):
            take_main(("mix", t))
            bring(("mix", t), vec("b_mix_out", t), first["mix"] + 2 * t + 1)
        for c in range(2):
            bring(("ln1_g", c), vec("ln1_g", c), first["mix"] + 3)
            bring(("ln1_b", c), vec("ln1_b", c), first["mix"] + 3)
        for c in range(2):
            take_side(("eT", c))
        main[0] += main[0] % 2
        take("router", 0)
        take_side(("rank", 0))
        take_side("most")
        entry0, entry1 = used[0], used[1]
        take("moe_y0", 2)
        take("moe_y1", 3)
        for c in range(2):
            bring(("ln2_g", c), vec("ln2_g", c), first["a"])
            bring(("ln2_b", c), vec("ln2_b", c), first["a"])
        for c in range(2):
            bring(("pre0", c), vec("norm_pre_2", c, 0), first["a"] + 5)
        for c in range(2):
            take_side(("aT", c))
        for t in range(8):
            take_main(("a", t))
        for c in range(4):
            bring(("a_ln_g", c), vec("a_ln_g_2", c), first["a"] + (8 if c < 2 else 14))
            bring(("a_ln_b", c), vec("a_ln_b_2", c), first["a"] + (8 if c < 2 else 14))
        for c in range(2):
            take_side(("wsT", c))
        for i in range(4):
            take_side(("sv", i))
        for t in range(8, 12):
            take_main(("a", t))
        for c in range(4):
            take_side(("yT", c))
        for t in range(2):
            take_main(("a_out", t))
        for c in range(2):
            bring(("post0", c), vec("norm_post_2", c, 0), first["a_out"] + 7)
        for c in range(2):
            bring(("pre1", c), vec("norm_pre_2", c, 1), first["a_out"] + 7)
        for c in range(2):
            take_side(("bT", c))
        slots = attention_slots()
        for t in range(20):
            take_main(("b", t))
            if t and BKIND[t - 1] in "qk":
                take_side(("bqk", t - 1))
            for act, g, c in slots[t]:
                if act in ("scores", "turn"):
                    for i in range(2):
                        take((act, g, c, i), 2 + i)
                else:
                    take_main((act, g, c))
        for c in range(2):
            take_side(("oT", c))
        for t in range(2):
            take_main(("b_out", t))
        for c in range(2):
            bring(("post1", c), vec("norm_post_2", c, 1), first["b_out"] + 3)

        def row_ready(eng, key):
            n = row_of[key]
            eng.wait_ge(S("row_full%d" % (n % AUXN)), 16 * (n // AUXN + 1))
            return aux[:, n % AUXN, :]

        def bc2(v, n=W):
            return v.unsqueeze(1).broadcast_to([P, NT, n])

        def pair_evacuated(eng, key):
            p, k = plan[key]
            eng.wait_ge(S("pair_free%d" % p), k)

        def freed(ins, key):
            ins.then_inc(S("pair_free%d" % plan[key][0]), 1)

        def buf(key):
            return pair(plan[key][0])

        def heads_T(t, tt):
            return slice(4 * t, 4 * t + 4), slice(P * tt, P * (tt + 1))

        free0 = o_XT2 + 2048
        b_qT, _ = carve(2, KC, T, on=o_XT)
        b_kT, _ = carve(2, KC, T, on=free0)
        b_v, _ = carve(NT, D, on=free0 + 4096)
        b_acc, _ = carve(DIL, NT, HEADS, HD, on=free0 + 6144)
        b_z, _ = carve(NT, D, on=free0 + 12288)
        b_p, _ = carve(4, 384, on=free0 + 14336)
        b_pT, _ = carve(4, 4, 384, on=free0 + 15872)
        b_t2, _ = carve(NT, W, on=free0 + 22016)
        b_rope, _ = carve(2, NT, W, on=free0 + 23040)
        assert free0 + 25088 <= o_cn
        b_nm, _ = carve(DIL, NT, HEADS, on=o_sm)
        b_s, _ = carve(DIL, NT, HEADS, on=o_sm + 96)
        b_e, _ = carve(DIL, NT, HEADS, on=o_sm + 192)
        b_q, _ = carve(NT, HEADS, on=o_sm + 288)
        a_v, _ = carve(NT, 2048, on=free0)
        a_u, _ = carve(NT, 2048, on=free0 + 4096)
        a_z, _ = carve(NT, 2048, on=free0 + 8192)
        a_ws, _ = carve(KC, P, on=free0 + 12288)
        a_wsT, _ = carve(KC, P, on=free0 + 13312)
        a_tri, _ = carve(P, on=free0 + 14336)
        a_bs, _ = carve(KC, on=free0 + 14336 + P)
        a_bsr = arena[0:KC, free0 + 14600:free0 + 14600 + P]
        y2, _ = carve(NT, D, on=free0 + 15000)
        xe, _ = carve(KC, SLOTS, on=free0)
        sge, _ = carve(FF, on=free0 + 1024)
        he, _ = carve(FF, on=free0 + 1536)
        heT, _ = carve(FF // P, SLOTS, on=free0 + 2048)
        ye, _ = carve(D, on=free0 + 2560)
        sel, _ = carve(NT, SLOTS, on=free0 + 3584)
        selw, _ = carve(NT, SLOTS, on=free0 + 3840)
        selT, _ = carve(T, on=free0 + 4096)
        iota, _ = carve(T, on=free0 + 4352)
        before, _ = carve(P, on=free0 + 4608)
        ones, _ = carve(P, on=free0 + 4736)
        hits, _ = carve(NT, NE, on=free0 + 4864)
        slot_of, _ = carve(NT, NE, on=free0 + 4928)
        most, _ = carve(2, on=free0 + 4992)
        flag_f = arena[0:1, free0 + 5000:free0 + 5001]
        comb, _ = carve(NT, NE, on=free0 + 6144)
        rt, o_rt = carve(1024, on=free0 + 6300)
        h_tok, _ = carve(NT, D, on=free0 + 8192)
        assert free0 + 8192 + 2048 <= o_v + 4096

        norm_eps = [LN_EPS] * H + [LN_EPS, LN_EPS, LN_EPS, RMS_EPS, LN_EPS, RMS_EPS, RMS_EPS, RMS_EPS]

        block = ctx.enter_context(nc.Block())

        @block.sync
        def _(sp):
            names = ["c_dist_f", "c_dist_b", "c_log", "c_rows", "c_rope1", "c_rope2", "c_mask", "c_ident"]
            views = [dist_f, dist_b, log_c, row_fb, rope1, rope2, amask, ident]
            sp.dma_start(ident, a["c_ident"]).then_inc(S("load_ident"), 16)
            sp.dma_start(rows16[0:8], a["c"].rearrange("o (k p) -> (o k) p", p=P)).then_inc(S("load_c"), 16)
            sp.dma_start(rows16[8:16], a["c_ctx"].rearrange("(k p) -> k p", p=P)).then_inc(S("load_cc"), 16)
            sp.dma_start(rows32[0:TAPS], a["conv_dw"][0]).then_inc(S("load_taps"), 16)
            sp.dma_start(rows32[TAPS:32], a["conv_dw_b"]).then_inc(S("load_tapb"), 16)
            sp.dma_start(lg[:, 0:H], a["ret_decay_fwd"].broadcast_to([P, H])).then_inc(S("load_df"), 16)
            sp.dma_start(lg[:, H:2 * H], a["ret_decay_bwd"].broadcast_to([P, H])).then_inc(S("load_db"), 16)
            sp.dma_start(pos, a["c_pos"]).then_inc(S("load_pos"), 16)

            def unit(n, src):
                if n >= RING:
                    sp.wait_ge(S("unit_done"), n - RING + 1)
                sp.dma_start(ring[:, n % RING], src.rearrange("(k p) c -> p k c", p=P)).then_inc(S("w_full%d" % (n % RING)), 16)

            def rows_for(n):
                for r in row_after.get(n, []):
                    if r >= AUXN:
                        sp.wait_ge(S("row_used"), r - AUXN + 1)
                    sp.dma_start(aux[:, r % AUXN, :], rows[r].broadcast_to([P, W])).then_inc(S("row_full%d" % (r % AUXN)), 16)

            for n in range(n_before):
                unit(n, units[n])
                rows_for(n)
                if n == n_before - 1:
                    sp.wait_ge(S("unit_done"), end_of("conv", 1))
                    sp.wait_ge(S("mT_turned"), 2)
                    sp.dma_start(iota, a["c_iota"]).then_inc(S("load_iota"), 16)
                    sp.dma_start(before, a["c_before"]).then_inc(S("load_before"), 16)
                if n == 3:
                    sp.dma_start(x, a["x"][0].rearrange("(t p) c -> p t c", p=P)).then_inc(S("load_x"), 16)
                    sp.dma_start(x_ctx, a["ctx"][0].rearrange("(t p) c -> p t c", p=P)).then_inc(S("load_ctx"), 16)
                    for name, v in list(zip(names, views))[:-1]:
                        sp.dma_start(v, a[name]).then_inc(S("load_" + name), 16)
                    sp.dma_start(wr[:, :, 0:NG], a["w_router_grp"][0].rearrange("(k p) g -> p k g", p=P)).then_inc(S("load_wrg"), 16)
                    sp.dma_start(wr[:, :, NG:36], a["w_router_exp"][0].rearrange("(k p) g -> p k g", p=P)).then_inc(S("load_wre"), 16)
                    sp.dma_start(br[:, 0:NG], a["b_router_grp"].broadcast_to([P, NG])).then_inc(S("load_brg"), 16)
                    sp.dma_start(br[:, NG:36], a["b_router_exp"].broadcast_to([P, NE])).then_inc(S("load_bre"), 16)

            def expert_units(r, e0, base, shift):
                for j, kind in enumerate(("gate", "gate", "up", "up", "down", "down")):
                    n = base + j
                    if shift is None:
                        wait = n - RING + 1
                    else:
                        wait = shift * 6 + (n - RING + 1)
                    sp.wait_ge(S("unit_done" + r), wait)
                    sp.dma_start(ring[:, n % RING], moe_src(kind, e0, j % 2)).then_inc(S("w_full%d%s" % (n % RING, r)), 16)
            with sp.Fori(0, NE) as e:
                expert_units("", e, n_before, e)
            sp.wait_ge(S("flag_set"), 1)
            more = sp.value_load(flag[0:1, 0:1], min_val=0, max_val=1)
            with sp.If(more > 0):
                sp.wait_ge(S("unit_done"), n_before + n_moe)
                for j, kind in enumerate(("gate", "gate", "up", "up", "down", "down")):
                    sp.dma_start(ring[:, j], moe_src(kind, 0, j % 2)).then_inc(S("w_full%d_b" % j), 16)
                with sp.Fori(1, NE) as e:
                    expert_units("_b", e, 0, e)
                sp.wait_ge(S("unit_done_b"), n_moe)

            for n in range(n_before + n_moe, len(units)):
                if n == first["a"]:
                    sp.wait_ge(S("unit_done"), n)
                    sp.dma_start(a_ws, a["a_w_s_2"][0].rearrange("g t s -> t g s")).then_inc(S("load_ws"), 16)
                    sp.dma_start(a_tri, a["c_tri"]).then_inc(S("load_tri"), 16)
                    sp.dma_start(a_bsr, a["a_b_s_2"][0]).then_inc(S("load_bs"), 16)
                unit(n, units[n])
                rows_for(n)
            sp.wait_ge(S("out_ready"), 1)
            sp.dma_start(out[0].rearrange("(t p) c -> p t c", p=P), x).then_inc(S("stored"), 16)
            sp.wait_ge(S("stored"), 16)

        @block.tensor
        def _(pe):
            def claim(key):
                p, k = plan[key]
                if k > 1:
                    pe.wait_ge(S("pair_free%d" % p), k - 1)
                return pair(p)

            def weights(n):
                pe.wait_ge(S("w_full%d" % (n % RING)), 16 * (n // RING + 1))
                return ring[:, n % RING]

            def gemm(name, t, key, lhs, nk=2, moving=NT):
                o = claim(key)
                for j in range(nk):
                    n = first[name] + nk * t + j
                    w = weights(n)
                    for tt in range(moving):
                        for c in range(UC):
                            mm = pe.matmul(o[:, tt, :], lhs(UC * j + c, tt), w[:, c, :],
                                           start=(j == 0 and c == 0), stop=(j == nk - 1 and c == UC - 1))
                    mm.then_inc(S("unit_done"), 1)

            def xt(k, tt):
                return XT[:, k, P * tt:P * (tt + 1)]

            def xt2(k, tt):
                return XT2[:, k, P * tt:P * (tt + 1)]

            def turn(key, src, sem, value=1):
                o = claim(key)
                for tt in range(NT):
                    for j in range(4):
                        mm = pe.transpose(o[:, tt, P * j:P * (j + 1)], src(tt, j), ident)
                mm.then_inc(S(sem), 1)

            pe.wait_ge(S("load_ident"), 16)
            pe.wait_ge(S("load_c"), 16)
            pe.wait_ge(S("load_cc"), 16)
            pe.wait_ge(S("load_taps"), 16)
            pe.wait_ge(S("load_tapb"), 16)
            o = claim("turn_rows")
            pe.transpose(o[:, 0, 0:16], rows16, ident[0:16, 0:16])
            for k in range(KC):
                mm = pe.transpose(o[:, 1, 32 * k:32 * (k + 1)], rows32[:, P * k:P * (k + 1)], ident[0:32, 0:32])
            mm.then_inc(S("rows_turned"), 1)
            pe.wait_ge(S("s_ready"), 2)
            for t in range(4):
                gemm("ada", t, ("ada", t), lambda k, m: (s_lat, s_ctx)[m][:, k, :])
            for s in range(2):
                pe.wait_ge(S("u_ready"), s + 1)
                src = (u_lat, u_ctx)[s]
                for c in range(2):
                    turn(("uT", s, c), lambda tt, j: src[:, tt, W * c + P * j:W * c + P * (j + 1)], "uT_turned")
            pair_evacuated(pe, ("uT", 0, 0))
            pair_evacuated(pe, ("uT", 0, 1))
            for t in range(3):
                gemm("glu", t, ("glu", t), xt)

            def turn_z(i):
                pe.wait_ge(S("z_ready"), i + 1)
                turn(("zT", i), lambda tt, j: z_tok[:, i, tt, P * j:P * (j + 1)], "zT_turned")
            turn_z(0)
            gemm("glu", 3, ("glu", 3), xt)
            pair_evacuated(pe, ("uT", 1, 0))
            pair_evacuated(pe, ("uT", 1, 1))

            def gemm_both(name, t):
                for s in range(2):
                    o = claim("%s_%s%d" % (name, ("lat", "ctx")[s], t))
                    for j in range(2):
                        n = first[name] + 2 * t + j
                        w = weights(n)
                        for tt in range(NT):
                            for c in range(UC):
                                mm = pe.matmul(o[:, tt, :], XT[:, 8 * s + UC * j + c, P * tt:P * (tt + 1)], w[:, c, :],
                                               start=(j == 0 and c == 0), stop=(j == 1 and c == UC - 1))
                        if s == 1:
                            mm.then_inc(S("unit_done"), 1)
                    if s == 0:
                        mm.then_inc(S("lat_done"), 1)

            def turn_roped(sem, t, key):
                pe.wait_ge(S(sem), t + 1)
                turn(key, lambda tt, j: roped[:, t, tt, P * j:P * (j + 1)], "heads_turned")

            gemm_both("k", 0)
            turn_z(1)
            gemm_both("k", 1)
            turn_roped("k_roped", 0, ("kT", 0))
            gemm_both("v", 0)
            turn_roped("k_roped", 1, ("kT", 1))
            for t in range(1, 4):
                gemm_both("v", t)
            for t in range(2):
                gemm("q", t, ("q", t), xt)
            for t in range(2):
                turn_roped("q_roped", t, ("qT", t))
            for i in range(4):
                o = claim(("S", i))
                for h in (2 * i, 2 * i + 1):
                    pe.wait_ge(S("k_decayed"), h + 1)
                    kd = tmp[:, h % 2, :].rearrange("p (t d n) -> p t d n", t=NT, d=2)
                    for d in range(2):
                        for tt in range(NT):
                            mm = pe.matmul(o[:, h % 2, DV * d:DV * (d + 1)], kd[:, tt, d, :],
                                           v_ctx[:, tt, DV * h:DV * (h + 1)], start=(tt == 0), stop=(tt == NT - 1))
                    mm.then_inc(S("state_done"), 1)
            pe.wait_ge(S("conv_done"), 1)
            for c in range(2):
                turn(("cz", c), lambda tt, j: conv[:, 4 * c + j, P * tt:P * (tt + 1)], "cz_turned")

            def ret_scores(i):
                o = claim(("sc", i))
                for h in (2 * i, 2 * i + 1):
                    for mt in range(NT):
                        mm = pe.matmul(o[:, h % 2, T * mt:T * (mt + 1)], kT[:, h, P * mt:P * (mt + 1)], qT[:, h, :],
                                       start=True, stop=True)
                mm.then_inc(S("ret_scored"), 1)

            def ret_values(i):
                o = claim(("av", i))
                for h in (2 * i, 2 * i + 1):
                    pe.wait_ge(S("ret_masked"), h + 1)
                    A = tmp[:, h % 2, :].rearrange("p (m n) -> p m n", m=NT)
                    Q = tmp[:, 4 + h % 2, :].rearrange("p (d n) -> p d n", d=2)
                    for nt in range(NT):
                        for mt in range(NT):
                            pe.matmul(o[:, h % 2, DV * nt:DV * (nt + 1)], A[:, mt, P * nt:P * (nt + 1)],
                                      v_lat[:, mt, DV * h:DV * (h + 1)], start=(mt == 0), stop=False)
                        for d in range(2):
                            mm = pe.matmul(o[:, h % 2, DV * nt:DV * (nt + 1)], Q[:, d, P * nt:P * (nt + 1)],
                                           state[:, h, d, :], start=False, stop=(d == 1))
                    mm.then_inc(S("ret_summed"), 1)

            for i in range(4):
                pair_evacuated(pe, ("S", i))
            pair_evacuated(pe, ("kT", 0))
            pair_evacuated(pe, ("kT", 1))
            pair_evacuated(pe, ("qT", 0))
            pair_evacuated(pe, ("qT", 1))
            ret_scores(0)
            for i in range(4):
                gemm("g", i, ("g", i), xt)
                ret_values(i)
                if i < 3:
                    ret_scores(i + 1)
            for t in range(4):
                gemm("gate", t, ("gate", t), xt)
            pe.wait_ge(S("s_ready"), 3)
            for t in range(8):
                gemm("ada_tail", t, ("ada_tail", t), lambda k, m: kT[:, 0:4, :].rearrange("p a b -> p (a b)")[:, P * k:P * (k + 1)], moving=1)
            pe.wait_ge(S("ret_ready"), 2)
            for c in range(4):
                turn(("retT", c), lambda tt, j: sg[:, tt, W * c + P * j:W * c + P * (j + 1)], "retT_turned")
            pe.wait_ge(S("cz_ready"), 1)
            for c in range(2):
                turn(("cvT", c), lambda tt, j: cz[:, tt, W * c + P * j:W * c + P * (j + 1)], "cvT_turned")
            for c in range(4):
                pair_evacuated(pe, ("retT", c))
            for t in range(2):
                gemm("ret", t, ("ret", t), xt, nk=4)
            for c in range(2):
                pair_evacuated(pe, ("cvT", c))
            for t in range(2):
                gemm("conv", t, ("conv", t), xt2)
            pe.wait_ge(S("merged"), 1)
            for c in range(2):
                turn(("mT", c), lambda tt, j: cz[:, tt, W * c + P * j:W * c + P * (j + 1)], "mT_turned")
            for c in range(2):
                pair_evacuated(pe, ("mT", c))
            for t in range(2):
                gemm("mix", t, ("mix", t), xt)
            pe.wait_ge(S("h_ready"), 1)
            for c in range(2):
                turn(("eT", c), lambda tt, j: h_tok[:, tt, W * c + P * j:W * c + P * (j + 1)], "eT_turned")
            for c in range(2):
                pair_evacuated(pe, ("eT", c))
            pe.wait_ge(S("load_wrg"), 16)
            pe.wait_ge(S("load_wre"), 16)
            o = claim("router")
            for tt in range(NT):
                for k in range(KC):
                    mm = pe.matmul(o[:, tt, 0:36], xt2(k, tt), wr[:, k, :], start=(k == 0), stop=(k == KC - 1))
            mm.then_inc(S("routed"), 1)

            pe.wait_ge(S("load_before"), 16)
            pe.wait_ge(S("hits_ready"), 1)
            o = claim(("rank", 0))
            pe.matmul(o[:, 0, 0:NE], before, hits[:, 0, :], start=True, stop=True)
            pe.matmul(o[:, 1, 0:NE], ones, hits[:, 0, :], start=True, stop=False)
            pe.matmul(o[:, 1, 0:NE], before, hits[:, 1, :], start=False, stop=True).then_inc(S("ranked"), 1)
            pe.wait_ge(S("most_ready"), 1)
            pe.transpose(ps[0:1, 2 * plan["most"][0], 0:P], most[:, 0:1], ident).then_inc(S("most_turned"), 1)

            y = [claim("moe_y0"), claim("moe_y1")]

            def wide_product(bank, lhs, n, base, e, r, begin, end):
                m = base + n
                pe.wait_ge(S("w_full%d%s" % (m % RING, r)), (16 * (m // RING + 1)) + e * 16)
                for c in range(UC):
                    mm = pe.matmul(ps[:, bank, :], lhs(c), ring[:, m % RING, c, :],
                                   start=(begin and c == 0), stop=(end and c == UC - 1))
                mm.then_inc(S("unit_done" + r), 1)

            def gather(half, e, r):
                for k in range(4):
                    for tt in range(NT):
                        mm = pe.matmul(ps[:, (2, 0)[half], P * k:P * (k + 1)],
                                       h_tok[:, tt, P * (4 * half + k):P * (4 * half + k + 1)], sel[:, tt, :],
                                       start=(tt == 0), stop=(tt == NT - 1))
                mm.then_inc(S("gathered%d%s" % (half, r)), 1)

            def turn_selection(r):
                for tt in range(NT):
                    mm = pe.transpose(ps[:, 3, P * tt:P * (tt + 1)], selw[:, tt, :], ident)
                mm.then_inc(S("sel_turned" + r), 1)

            def scatter(begin, r):
                for tt in range(NT):
                    for j in range(2):
                        mm = pe.matmul(y[tt][:, j, :], selT[:, P * tt:P * (tt + 1)], ye[:, W * j:W * (j + 1)],
                                       start=begin, stop=False, skip_group_check=True)
                mm.then_inc(S("scattered" + r), 1)

            def expert(e, base, r, head, tail, begin):
                pe.wait_ge(S("xe0" + r), e + 1)
                pe.wait_ge(S("xe1" + r), e + 1)
                for j in range(2):
                    wide_product(0, lambda c: xe[:, UC * j + c, :], j, base, e, r, j == 0, j == 1)
                if not head:
                    pe.wait_ge(S("ye0" + r), e)
                    pe.wait_ge(S("ye1" + r), e)
                    pe.wait_ge(S("selT" + r), e)
                    scatter(begin, r)
                for j in range(2):
                    wide_product(1, lambda c: xe[:, UC * j + c, :], 2 + j, base, e, r, j == 0, j == 1)
                if not tail:
                    pe.wait_ge(S("sel_ready" + r), e + 2)
                    gather(0, e, r)
                pe.wait_ge(S("selT" + r), e + 1)
                pe.wait_ge(S("act_ready" + r), e + 1)
                for j in range(FF // P):
                    mm = pe.transpose(ps[:, 3, P * j:P * (j + 1)], he[:, P * j:P * (j + 1)], ident)
                mm.then_inc(S("h_turned" + r), 1)
                if not tail:
                    pe.wait_ge(S("silu" + r), e + 1)
                    gather(1, e, r)
                pe.wait_ge(S("hT" + r), e + 1)
                wide_product(1, lambda c: heT[:, c, :], 4, base, e, r, True, True)
                if not tail:
                    pe.wait_ge(S("xe0" + r), e + 2)
                wide_product(2, lambda c: heT[:, c, :], 5, base, e, r, True, True)
                if not tail:
                    pe.wait_ge(S("selw_ready" + r), e + 2)
                    turn_selection(r)

            def experts(base, r, first_round):
                pe.wait_ge(S("sel_ready" + r), 1)
                gather(0, 0, r)
                gather(1, 0, r)
                pe.wait_ge(S("selw_ready" + r), 1)
                turn_selection(r)
                expert(0, base, r, True, False, False)
                expert(1, base, r, False, False, first_round)
                with pe.Fori(2, NE - 1) as e:
                    expert(e, base, r, False, False, False)
                expert(NE - 1, base, r, False, True, False)
                pe.wait_ge(S("ye0" + r), NE)
                pe.wait_ge(S("ye1" + r), NE)
                pe.wait_ge(S("selT" + r), NE)
                scatter(False, r)

            pe.wait_ge(S("flag_set"), 1)
            pe.wait_ge(S("pair_free0"), entry0)
            pe.wait_ge(S("pair_free1"), entry1)
            experts(n_before, "", True)
            more = pe.value_load(flag[0:1, 0:1], min_val=0, max_val=1)
            with pe.If(more > 0):
                experts(0, "_b", False)

            pe.wait_ge(S("a_in_ready"), 1)
            for c in range(2):
                turn(("aT", c), lambda tt, j: h_tok[:, tt, W * c + P * j:W * c + P * (j + 1)], "aT_turned")
            for c in range(2):
                pair_evacuated(pe, ("aT", c))
            for t in range(8):
                gemm("a", t, ("a", t), xt2)
            pe.wait_ge(S("load_ws"), 16)
            pe.wait_ge(S("load_bs"), 16)
            for c in range(2):
                o = claim(("wsT", c))
                for j in range(4):
                    mm = pe.transpose(o[:, 0, P * j:P * (j + 1)], a_ws[:, 4 * c + j, :], ident)
                if c == 1:
                    mm = pe.transpose(o[:, 1, 0:KC], a_bsr, ident[0:KC, 0:KC])
                mm.then_inc(S("wsT_turned"), 1)
            pe.wait_ge(S("wsT_ready"), 2)
            pe.wait_ge(S("v_normed"), 1)
            for i in range(4):
                o = claim(("sv", i))
                for tt in range(NT):
                    for g in (2 * i, 2 * i + 1):
                        mm = pe.matmul(o[:, tt, 256 * (g % 2):256 * (g % 2 + 1)], a_wsT[:, g, :],
                                       a_v[:, tt, 256 * g:256 * (g + 1)], start=True, stop=True)
                mm.then_inc(S("sv_done"), 1)
            for t in range(8, 12):
                gemm("a", t, ("a", t), xt2)
            for c in range(4):
                pe.wait_ge(S("y_gated"), c + 1)
                turn(("yT", c), lambda tt, j: a_z[:, tt, W * c + P * j:W * c + P * (j + 1)], "yT_turned")
            for c in range(4):
                pair_evacuated(pe, ("yT", c))
            for t in range(2):
                gemm("a_out", t, ("a_out", t), xt, nk=4)

            pe.wait_ge(S("b_in_ready"), 1)
            for c in range(2):
                turn(("bT", c), lambda tt, j: y2[:, tt, W * c + P * j:W * c + P * (j + 1)], "bT_turned")
            for c in range(2):
                pair_evacuated(pe, ("bT", c))
            n_rope = 0
            for t in range(20):
                gemm("b", t, ("b", t), xt2)
                if t and BKIND[t - 1] in "qk":
                    n_rope += 1
                    pe.wait_ge(S("b_roped"), n_rope)
                    turn(("bqk", t - 1), lambda tt, j: b_rope[:, (n_rope - 1) % 2, tt, P * j:P * (j + 1)], "b_turned")
                for act, g, c in slots[t]:
                    if act == "scores":
                        if c == 0:
                            for key in [("bqk", tq) for tq in range(20) if BKIND[tq] in "qk" and BGROUP[tq] == g]:
                                pair_evacuated(pe, key)
                        for i in range(2):
                            o = claim((act, g, c, i))
                            for hh in range(2):
                                h = 4 * c + 2 * i + hh
                                r = slice(HD * (h % 2), HD * (h % 2) + HD)
                                for tt in range(NT):
                                    n = P * (tt + 1)
                                    mm = pe.matmul(o[:, hh, P * tt:P * tt + n], b_qT[r, g % 2, h // 2, P * tt:P * (tt + 1)],
                                                   b_kT[r, g % 2, h // 2, 0:n], start=True, stop=True)
                            mm.then_inc(S("b_scored"), 1)
                    elif act == "turn":
                        pe.wait_ge(S("b_probs"), 4 * (4 * g + c) + 4)
                        for i in range(2):
                            o = claim((act, g, c, i))
                            for hh in range(2):
                                for s in range(3):
                                    mm = pe.transpose(o[:, hh, P * s:P * (s + 1)], b_p[:, 2 * i + hh, P * s:P * (s + 1)], ident)
                            mm.then_inc(S("b_p_turned"), 1)
                    else:
                        for i in range(2):
                            pair_evacuated(pe, ("turn", g, c, i))
                        if c == 0:
                            for tv in range(20):
                                if BKIND[tv] == "v" and BGROUP[tv] == g:
                                    pair_evacuated(pe, ("b", tv))
                        o = claim((act, g, c))
                        for hh in range(4):
                            h = 4 * c + hh
                            pT = b_pT[:, c, hh, :]
                            cols = slice(HD * h, HD * (h + 1))
                            pe.matmul(o[:, 0, HD * hh:HD * (hh + 1)], pT[:, 0:P], b_v[:, 0, cols], start=True, stop=True)
                            pe.matmul(o[:, 1, HD * hh:HD * (hh + 1)], pT[:, P:2 * P], b_v[:, 0, cols], start=True, stop=False)
                            mm = pe.matmul(o[:, 1, HD * hh:HD * (hh + 1)], pT[:, 2 * P:3 * P], b_v[:, 1, cols], start=False, stop=True)
                        mm.then_inc(S("b_valued"), 1)
            pe.wait_ge(S("b_o_ready"), 1)
            for c in range(2):
                turn(("oT", c), lambda tt, j: b_z[:, tt, W * c + P * j:W * c + P * (j + 1)], "oT_turned")
            for c in range(2):
                pair_evacuated(pe, ("oT", c))
            for t in range(2):
                gemm("b_out", t, ("b_out", t), xt)

        @block.vector
        def _(dve):
            chain = [0]

            def link(ins):
                chain[0] += 1
                ins.then_inc(S("dve_step"), 1)

            def settle():
                dve.wait_ge(S("dve_step"), chain[0])

            def row_done(key=None):
                if key is None:
                    settle()
                else:
                    pair_evacuated(dve, key)
                dve.sem_inc(S("row_used"), 1)

            def free_pair(key):
                dve.sem_inc(S("pair_free%d" % plan[key][0]), 1)

            norms = [0]

            def power(eps):
                norms[0] += 1
                return norms[0]

            def row_stats(src, width):
                n = width // W
                for tt in range(NT):
                    for c in range(n):
                        link(dve.bn_stats(stats[:, tt, c, :], src(tt)[:, W * c:W * (c + 1)]))
                settle()
                for tt in range(NT):
                    ins = dve.bn_aggr(mv[:, tt, :], stats[:, tt, 0:n, :])
                    if tt == 1:
                        norms[0] += 1
                        ins.then_inc(S("stats_ready"), 1)
                    else:
                        link(ins)
                dve.wait_ge(S("rstd_ready"), norms[0])
                settle()

            def apply_norm(dst, src):
                for tt in range(NT):
                    link(dve.tensor_scalar(dst(tt), src(tt), mv[:, tt, 0:1], rstd[:, tt:tt + 1], ALU.subtract, ALU.mult))
                settle()

            def gain_bias(buf2, g, b, c):
                v = buf2[:, :, W * c:W * (c + 1)]
                link(dve.tensor_tensor(v, v, bc2(row_ready(dve, (g, c))), ALU.mult))
                settle()
                row_done()
                link(dve.tensor_tensor(v, v, bc2(row_ready(dve, (b, c))), ALU.add))
                settle()
                row_done()

            def rms(src, dst, g, rows_key):
                for tt in range(NT):
                    for c in range(2):
                        link(dve.bn_stats(stats[:, tt, c, :], src[:, tt, W * c:W * (c + 1)]))
                settle()
                for tt in range(NT):
                    link(dve.bn_aggr(mv[:, tt, :], stats[:, tt, 0:2, :]))
                settle()
                link(dve.tensor_tensor(sq, mv[:, :, 0], mv[:, :, 0], ALU.mult))
                settle()
                norms[0] += 1
                dve.tensor_tensor(mv[:, :, 1], sq, mv[:, :, 1], ALU.add).then_inc(S("stats_ready"), 1)
                dve.wait_ge(S("rstd_ready"), norms[0])
                for tt in range(NT):
                    link(dve.tensor_scalar(dst[:, tt, :], src[:, tt, :], rstd[:, tt:tt + 1], None, ALU.mult))
                settle()
                for c in range(2):
                    v = dst[:, :, W * c:W * (c + 1)]
                    link(dve.tensor_tensor(v, v, bc2(row_ready(dve, (rows_key, c))), ALU.mult))
                    settle()
                    row_done()

            def biased(key, dst, wait_name, wait_value, free=True):
                dve.wait_ge(S(wait_name), wait_value)
                return dve.tensor_tensor(dst, buf(key), bc2(row_ready(dve, key)), ALU.add)

            dve.wait_ge(S("silu_c"), 1)
            dve.tensor_copy(s_lat, sT[:, 0:KC].unsqueeze(2).broadcast_to([P, KC, P])).then_inc(S("s_ready"), 1)
            dve.tensor_copy(s_ctx, sT[:, KC:2 * KC].unsqueeze(2).broadcast_to([P, KC, P])).then_inc(S("s_ready"), 1)
            dve.wait_ge(S("load_df"), 16)
            dve.wait_ge(S("load_db"), 16)
            link(dve.tensor_scalar(la[:, 0, :], lg, -1.0, None, ALU.mult))
            settle()
            dve.tensor_tensor(la[:, 0, :], la[:, 0, :], lg, ALU.min).then_inc(S("neg_abs"), 1)
            dve.wait_ge(S("exp_abs"), 1)
            link(dve.tensor_scalar(la[:, 1, :], la[:, 0, :], 2.0, None, ALU.add))
            settle()
            link(dve.reciprocal(la[:, 1, :], la[:, 1, :]))
            settle()
            link(dve.tensor_tensor(la[:, 0, :], la[:, 0, :], la[:, 1, :], ALU.mult))
            settle()
            link(dve.tensor_tensor(la[:, 1, :], la[:, 0, :], la[:, 0, :], ALU.mult))
            settle()
            link(dve.tensor_scalar(la[:, 2, :], la[:, 1, :], 2.0 / 17, 2.0 / 15, ALU.mult, ALU.add))
            settle()
            for n in (13, 11, 9, 7, 5, 3, 1):
                link(dve.tensor_tensor(la[:, 2, :], la[:, 2, :], la[:, 1, :], ALU.mult))
                settle()
                link(dve.tensor_scalar(la[:, 2, :], la[:, 2, :], 2.0 / n, None, ALU.add))
                settle()
            link(dve.tensor_tensor(la[:, 2, :], la[:, 2, :], la[:, 0, :], ALU.mult))
            link(dve.tensor_scalar(lg, lg, 0.0, None, ALU.min))
            settle()
            link(dve.tensor_tensor(lg, lg, la[:, 2, :], ALU.subtract))
            settle()
            dve.wait_ge(S("load_pos"), 16)
            for d in range(2):
                for tt in range(NT):
                    ins = dve.tensor_scalar(wdec[:, d, tt, :], lg[:, H * d:H * (d + 1)], pos[:, d, tt:tt + 1], None, ALU.mult)
                    if d == 1 and tt == 1:
                        ins.then_inc(S("wdec_exps"), 1)
                    else:
                        link(ins)

            for t in range(4):
                row = row_ready(dve, ("ada", t))
                dve.wait_ge(S("unit_done"), end_of("ada", t))
                p_ = buf(("ada", t))
                for m, dst in enumerate((mod_lat, mod_ctx)):
                    if t < 2:
                        ins = dve.tensor_tensor(dst[:, W * t:W * (t + 1)], p_[:, m, :], row, ALU.add)
                    else:
                        ins = dve.scalar_tensor_tensor(dst[:, W * t:W * (t + 1)], p_[:, m, :], 1.0, row, ALU.add, ALU.add)
                    if m == 0:
                        link(ins)
                    else:
                        freed(ins, ("ada", t))
                row_done(("ada", t))
            pair_evacuated(dve, ("ada", 2))
            pair_evacuated(dve, ("ada", 3))
            settle()
            for s, (src, dst, m) in enumerate(((x, u_lat, mod_lat), (x_ctx, u_ctx, mod_ctx))):
                dve.wait_ge(S(("load_x", "load_ctx")[s]), 16)
                link(dve.tensor_tensor(dst, src, m[:, D:2 * D].unsqueeze(1).broadcast_to([P, NT, D]), ALU.mult))
                settle()
                dve.tensor_tensor(dst, dst, m[:, 0:D].unsqueeze(1).broadcast_to([P, NT, D]), ALU.add).then_inc(S("u_ready"), 1)

            link(dve.memset(z_pad[:, :, 0:PAD], 0.0))
            link(dve.memset(z_pad[:, :, PAD + T:T + 2 * PAD], 0.0))
            dve.wait_ge(S("wdec_exp"), 1)
            link(dve.tensor_scalar(wdec, wdec, DK ** -0.5, None, ALU.mult))

            for i in range(2):
                ins = biased(("glu", 2 * i), z_tok[:, i], "unit_done", end_of("glu", 2 * i))
                freed(ins, ("glu", 2 * i))
                row_done(("glu", 2 * i))
                ins = biased(("glu", 2 * i + 1), tmp[:, 2 * i:2 * i + 2, :], "unit_done", end_of("glu", 2 * i + 1))
                freed(ins, ("glu", 2 * i + 1))
                row_done(("glu", 2 * i + 1))
                dve.wait_ge(S("sig_z"), i + 1)
                pair_evacuated(dve, ("glu", 2 * i))
                dve.tensor_tensor(z_tok[:, i], z_tok[:, i], tmp[:, 2 * i:2 * i + 2, :], ALU.mult).then_inc(S("z_ready"), 1)

            taps_done = [0]

            def conv_taps(n):
                for _ in range(n):
                    j = taps_done[0]
                    if j == 0:
                        dve.wait_ge(S("pair_free%d" % plan[("zT", 0)][0]), plan[("zT", 0)][1])
                        dve.wait_ge(S("pair_free%d" % plan[("zT", 1)][0]), plan[("zT", 1)][1])
                        pair_evacuated(dve, "turn_rows")
                    settle()
                    for k in range(KC):
                        z = z_pad[:, k, j:j + T]
                        if j == 0:
                            link(dve.tensor_scalar(conv[:, k, :], z, cwT[:, k, 0:1], cwT[:, k, TAPS:TAPS + 1], ALU.mult, ALU.add))
                        elif j < TAPS - 1 or k < KC - 1:
                            link(dve.scalar_tensor_tensor(conv[:, k, :], z, cwT[:, k, j:j + 1], conv[:, k, :], ALU.mult, ALU.add))
                        else:
                            dve.scalar_tensor_tensor(conv[:, k, :], z, cwT[:, k, j:j + 1], conv[:, k, :], ALU.mult, ALU.add).then_inc(S("conv_done"), 1)
                    taps_done[0] += 1

            def rope_four(t, ready):
                for tt in range(NT):
                    s = tmp[:, tt, :].rearrange("p (h s d) -> p h s d", h=4, s=2)
                    r = roped[:, t, tt, :].rearrange("p (h s d) -> p h s d", h=4, s=2)
                    q = tmp[:, 2 + tt, :].rearrange("p (h s d) -> p h s d", h=4, s=2)
                    cos = rope1[:, 0, tt, :].unsqueeze(1).broadcast_to([P, 4, P])
                    link(dve.tensor_tensor(roped[:, t, tt, :].rearrange("p (h d) -> p h d", h=4),
                                           tmp[:, tt, :].rearrange("p (h d) -> p h d", h=4), cos, ALU.mult))
                    for s_ in range(2):
                        sin = rope1[:, 1, tt, 64 * s_:64 * (s_ + 1)].unsqueeze(1).broadcast_to([P, 4, 64])
                        link(dve.tensor_tensor(q[:, :, s_, :], s[:, :, 1 - s_, :], sin, ALU.mult))
                settle()
                for tt in range(NT):
                    ins = dve.tensor_tensor(roped[:, t, tt, :], roped[:, t, tt, :], tmp[:, 2 + tt, :], ALU.add)
                    if tt == 1:
                        ins.then_inc(S(ready), 1)
                    else:
                        link(ins)

            dve.wait_ge(S("load_c_rope1"), 16)
            for t in range(2):
                row = row_ready(dve, ("k", t))
                dve.wait_ge(S("lat_done"), t + 1)
                freed(dve.tensor_tensor(tmp[:, 0:2, :], buf("k_lat%d" % t), bc2(row), ALU.add), "k_lat%d" % t)
                pair_evacuated(dve, "k_lat%d" % t)
                rope_four(t, "k_roped")
                if t == 1:
                    conv_taps(4)
                dve.wait_ge(S("unit_done"), end_of("k", t))
                freed(dve.tensor_tensor(k_ctx[:, :, W * t:W * (t + 1)], buf("k_ctx%d" % t), bc2(row), ALU.add), "k_ctx%d" % t)
                row_done("k_ctx%d" % t)
            for t in range(4):
                row = row_ready(dve, ("v", t))
                dve.wait_ge(S("lat_done"), t + 3)
                freed(dve.tensor_tensor(v_lat[:, :, W * t:W * (t + 1)], buf("v_lat%d" % t), bc2(row), ALU.add), "v_lat%d" % t)
                conv_taps(4)
                dve.wait_ge(S("unit_done"), end_of("v", t))
                freed(dve.tensor_tensor(v_ctx[:, :, W * t:W * (t + 1)], buf("v_ctx%d" % t), bc2(row), ALU.add), "v_ctx%d" % t)
                row_done("v_ctx%d" % t)
                conv_taps(3 if t < 3 else 2)
            assert taps_done[0] == TAPS, taps_done
            for t in range(2):
                if t == 0:
                    dve.wait_ge(S("heads_turned"), 2)
                ins = biased(("q", t), tmp[:, 0:2, :], "unit_done", end_of("q", t))
                freed(ins, ("q", t))
                pair_evacuated(dve, ("q", t))
                row_done(("q", t))
                rope_four(t, "q_roped")
            pair_evacuated(dve, "k_ctx0")
            pair_evacuated(dve, "k_ctx1")
            for h in range(H):
                if h >= 2:
                    dve.wait_ge(S("state_done"), h - 1)
                kd = tmp[:, h % 2, :].rearrange("p (t d n) -> p t d n", t=NT, d=2)
                for tt in range(NT):
                    for d in range(2):
                        ins = dve.tensor_scalar(kd[:, tt, d, :], k_ctx[:, tt, DK * h:DK * (h + 1)], wdec[:, d, tt, h:h + 1], None, ALU.mult)
                        if tt == 1 and d == 1:
                            ins.then_inc(S("k_decayed"), 1)
                        else:
                            link(ins)

            def decay_exponents(h):
                E = tmp[:, 2 + h % 2, :]
                link(dve.scalar_tensor_tensor(E, dist_f.rearrange("p a b -> p (a b)"), lg[:, h:h + 1], log_c.rearrange("p a b -> p (a b)"), ALU.mult, ALU.add))
                settle()
                dve.scalar_tensor_tensor(E, dist_b.rearrange("p a b -> p (a b)"), lg[:, H + h:H + h + 1], E, ALU.mult, ALU.add).then_inc(S("ret_exps"), 1)

            def mask_scores(i):
                dve.wait_ge(S("ret_scored"), i + 1)
                for h in (2 * i, 2 * i + 1):
                    dve.wait_ge(S("ret_exped"), h + 1)
                    if h >= 2:
                        dve.wait_ge(S("ret_summed"), h - 1)
                    Q = tmp[:, 4 + h % 2, :].rearrange("p (d n) -> p d n", d=2)
                    link(dve.tensor_tensor(Q, Q, qT[:, h:h + 1, :].broadcast_to([P, 2, T]), ALU.mult))
                    settle()
                    dve.tensor_tensor(tmp[:, h % 2, :], buf(("sc", i))[:, h % 2, :], tmp[:, 2 + h % 2, :], ALU.mult).then_inc(S("ret_masked"), 1)
                dve.wait_ge(S("ret_masked"), 2 * i + 2)
                free_pair(("sc", i))

            def head_norm(i):
                o = buf(("av", i))
                for h in (2 * i, 2 * i + 1):
                    dve.wait_ge(S("ret_summed"), h + 1)
                    for tt in range(NT):
                        link(dve.bn_stats(stats[:, tt, 0, :], o[:, h % 2, DV * tt:DV * (tt + 1)]))
                    settle()
                    for tt in range(NT):
                        ins = dve.bn_aggr(mv[:, tt, :], stats[:, tt, 0:1, :])
                        if tt == 0:
                            link(ins)
                        else:
                            norms[0] += 1
                            ins.then_inc(S("stats_ready"), 1)
                    dve.wait_ge(S("rstd_ready"), norms[0])
                    settle()
                    dst = (o_lo, o_hi)[h // 4]
                    for tt in range(NT):
                        link(dve.tensor_scalar(dst[:, tt, DV * (h % 4):DV * (h % 4 + 1)], o[:, h % 2, DV * tt:DV * (tt + 1)],
                                               mv[:, tt, 0:1], rstd[:, tt:tt + 1], ALU.subtract, ALU.mult))
                settle()
                free_pair(("av", i))

            dve.wait_ge(S("state_done"), H)
            for name in ("load_c_dist_f", "load_c_dist_b", "load_c_log"):
                dve.wait_ge(S(name), 16)
            pair_evacuated(dve, ("qT", 0))
            pair_evacuated(dve, ("qT", 1))
            decay_exponents(0)
            decay_exponents(1)
            for i in range(4):
                mask_scores(i)
                if i < 3:
                    decay_exponents(2 * i + 2)
                    decay_exponents(2 * i + 3)
                ins = biased(("g", i), sg[:, :, W * i:W * (i + 1)], "unit_done", end_of("g", i))
                freed(ins, ("g", i))
                row_done(("g", i))
                head_norm(i)

            dve.wait_ge(S("silu_g"), 4)
            for half, src in ((0, o_lo), (1, o_hi)):
                v = sg[:, :, D * half:D * (half + 1)]
                dve.tensor_tensor(v, v, src, ALU.mult).then_inc(S("ret_ready"), 1)
            dve.tensor_copy(kT[:, 0:4, :].rearrange("p a b -> p (a b)").rearrange("p (k n) -> p k n", k=KC),
                            sT[:, 0:KC].unsqueeze(2).broadcast_to([P, KC, P])).then_inc(S("s_ready"), 1)
            pair_evacuated(dve, ("cz", 0))
            pair_evacuated(dve, ("cz", 1))
            row_stats(lambda tt: cz[:, tt, :], D)
            apply_norm(lambda tt: cz[:, tt, :], lambda tt: cz[:, tt, :])
            for c in range(2):
                gain_bias(cz, "conv_g", "conv_b", c)
            dve.sem_inc(S("cz_normed"), 1)
            for t in range(4):
                ins = biased(("gate", t), gates[:, :, W * t:W * (t + 1)], "unit_done", end_of("gate", t))
                freed(ins, ("gate", t))
                row_done(("gate", t))
            for t in range(8):
                row = row_ready(dve, ("ada_tail", t))
                dve.wait_ge(S("unit_done"), end_of("ada_tail", t))
                src = buf(("ada_tail", t))[:, 0, :]
                dst = mod_tail[:, W * t:W * (t + 1)]
                if t in (4, 5):
                    freed(dve.scalar_tensor_tensor(dst, src, 1.0, row, ALU.add, ALU.add), ("ada_tail", t))
                else:
                    freed(dve.tensor_tensor(dst, src, row, ALU.add), ("ada_tail", t))
                row_done(("ada_tail", t))
            dve.wait_ge(S("sig_gates"), 4)
            for t in range(2):
                dve.wait_ge(S("unit_done"), end_of("ret", t, 4))
                v = gates[:, :, W * t:W * (t + 1)]
                freed(dve.tensor_tensor(v, v, buf(("ret", t)), ALU.mult), ("ret", t))
            for t in range(2):
                dve.wait_ge(S("cvT_turned"), 2)
                v = cz[:, :, W * t:W * (t + 1)]
                freed(biased(("conv", t), v, "unit_done", end_of("conv", t)), ("conv", t))
                pair_evacuated(dve, ("conv", t))
                row_done(("conv", t))
                link(dve.tensor_tensor(v, v, gates[:, :, D + W * t:D + W * (t + 1)], ALU.mult))
                settle()
                pair_evacuated(dve, ("ret", t))
                ins = dve.tensor_tensor(v, v, gates[:, :, W * t:W * (t + 1)], ALU.add)
                if t == 1:
                    ins.then_inc(S("merged"), 1)
                else:
                    link(ins)
            pair_evacuated(dve, ("ada_tail", 7))
            gt = mod_tail

            def residual_ln(t, gate_row):
                v = h_tok[:, :, W * t:W * (t + 1)]
                link(dve.tensor_tensor(v, v, bc2(gate_row), ALU.mult))
                settle()
                xv = x[:, :, W * t:W * (t + 1)]
                link(dve.scalar_tensor_tensor(xv, xv, ALPHA, v, ALU.mult, ALU.add))
                settle()

            for t in range(2):
                v = h_tok[:, :, W * t:W * (t + 1)]
                freed(biased(("mix", t), v, "unit_done", end_of("mix", t)), ("mix", t))
                pair_evacuated(dve, ("mix", t))
                row_done(("mix", t))
                residual_ln(t, gt[:, W * t:W * (t + 1)])
            row_stats(lambda tt: x[:, tt, :], D)
            apply_norm(lambda tt: x[:, tt, :], lambda tt: x[:, tt, :])
            for c in range(2):
                gain_bias(x, "ln1_g", "ln1_b", c)
            link(dve.tensor_tensor(h_tok, x, gt[:, 2 * D:3 * D].unsqueeze(1).broadcast_to([P, NT, D]), ALU.mult))
            settle()
            dve.tensor_tensor(h_tok, h_tok, gt[:, D:2 * D].unsqueeze(1).broadcast_to([P, NT, D]), ALU.add).then_inc(S("h_ready"), 1)

            dve.wait_ge(S("load_brg"), 16)
            dve.wait_ge(S("load_bre"), 16)
            dve.wait_ge(S("load_c_rows"), 16)
            dve.wait_ge(S("routed"), 1)
            freed(dve.tensor_tensor(lgt, buf("router")[:, :, 0:36], br.unsqueeze(1).broadcast_to([P, NT, 36]), ALU.add), "router")
            pair_evacuated(dve, "router")
            oo = [o_rt]

            def rb(*shape):
                v, _ = carve(*shape, on=oo[0])
                oo[0] += int(np.prod(shape))
                return v
            g_max, g_e, g_sum, g_hit, g_first = rb(NT), rb(NT, NG), rb(NT), rb(NT, NG), rb(NT)
            pick, l8, m1, hit1, hit2, m2, e2, wsum, w1, w2 = rb(NT, NG, NEG), rb(NT, NEG), rb(NT), rb(NT, NEG), rb(NT, NEG), rb(NT), rb(NT), rb(NT), rb(NT), rb(NT)
            l8b, c8, m8 = rb(NT, NEG), rb(NT, NEG), rb(NT, NEG)
            rank = rb(NEG)

            def one(ins):
                link(ins)
                settle()

            def wide(v, n):
                return v.unsqueeze(2).broadcast_to([P, NT, n])

            one(dve.tensor_scalar(rank, row_fb[:, 1, 0:NEG], -(T - NEG - 1.0), None, ALU.add))

            def first_max(hit, src, mx, n):
                one(dve.tensor_reduce(mx, src, AX_X, ALU.max))
                one(dve.tensor_tensor(hit, src, wide(mx, n), ALU.is_equal))
                one(dve.tensor_tensor(hit, hit, rank[:, 0:n].unsqueeze(1).broadcast_to([P, NT, n]), ALU.mult))
                one(dve.tensor_reduce(g_first, hit, AX_X, ALU.max))
                one(dve.tensor_tensor(hit, hit, wide(g_first, n), ALU.is_equal))

            gl = lgt[:, :, 0:NG]
            first_max(g_hit, gl, g_max, NG)
            dve.tensor_tensor(g_e, gl, wide(g_max, NG), ALU.subtract).then_inc(S("router_exp"), 1)
            el = lgt[:, :, NG:36].rearrange("p t (g e) -> p t g e", g=NG)
            for tt in range(NT):
                link(dve.tensor_tensor(pick[:, tt], el[:, tt], g_hit[:, tt].unsqueeze(2).broadcast_to([P, NG, NEG]), ALU.mult))
            settle()
            for tt in range(NT):
                link(dve.tensor_reduce(l8[:, tt], pick[:, tt].rearrange("p g e -> p e g"), AX_X, ALU.add))
            settle()
            first_max(hit1, l8, m1, NEG)
            one(dve.tensor_scalar(l8b, hit1, -3.0e38, None, ALU.mult))
            one(dve.tensor_tensor(l8b, l8b, l8, ALU.add))
            first_max(hit2, l8b, m2, NEG)
            dve.tensor_tensor(e2, m2, m1, ALU.subtract).then_inc(S("router_exp"), 1)
            dve.wait_ge(S("router_exped"), 2)
            one(dve.tensor_reduce(g_sum, g_e, AX_X, ALU.add))
            one(dve.tensor_tensor(m8, hit1, hit2, ALU.add))
            for tt in range(NT):
                one(dve.tensor_tensor(hits[:, tt].rearrange("p (g e) -> p g e", g=NG), g_hit[:, tt].unsqueeze(2).broadcast_to([P, NG, NEG]),
                                      m8[:, tt].unsqueeze(1).broadcast_to([P, NG, NEG]), ALU.mult))
            dve.memset(ones, 1.0).then_inc(S("hits_ready"), 1)
            one(dve.tensor_scalar(wsum, e2, 1.0, None, ALU.add))
            one(dve.tensor_tensor(wsum, wsum, g_sum, ALU.mult))
            one(dve.reciprocal(w1, wsum))
            one(dve.tensor_tensor(w2, w1, e2, ALU.mult))
            one(dve.tensor_tensor(hit1, hit1, wide(w1, NEG), ALU.mult))
            one(dve.tensor_tensor(hit2, hit2, wide(w2, NEG), ALU.mult))
            one(dve.tensor_tensor(c8, hit1, hit2, ALU.add))
            for tt in range(NT):
                one(dve.tensor_tensor(comb[:, tt].rearrange("p (g e) -> p g e", g=NG), g_hit[:, tt].unsqueeze(2).broadcast_to([P, NG, NEG]),
                                      c8[:, tt].unsqueeze(1).broadcast_to([P, NG, NEG]), ALU.mult))

            dve.wait_ge(S("ranked"), 1)
            settle()
            link(dve.scalar_tensor_tensor(slot_of, buf(("rank", 0))[:, :, 0:NE], 1.0, hits, ALU.add, ALU.mult))
            settle()
            free_pair(("rank", 0))
            one(dve.tensor_scalar(slot_of, slot_of, -1.0, None, ALU.add))
            dve.tensor_reduce(most[:, 0:1], slot_of.rearrange("p t e -> p (t e)"), AX_X, ALU.max).then_inc(S("most_ready"), 1)
            dve.wait_ge(S("most_turned"), 1)
            dve.tensor_reduce(flag_f, ps[0:1, 2 * plan["most"][0], 0:P], AX_X, ALU.max).then_inc(S("pair_free%d" % plan["most"][0]), 1)
            pair_evacuated(dve, "most")
            dve.tensor_scalar(flag[0:1, 0:1], flag_f, float(SLOTS), None, ALU.is_ge).then_inc(S("flag_set"), 1)

            def select(e, rd, r, wait):
                if wait:
                    dve.wait_ge(S("gathered1" + r), e)
                slots_ = iota[:, SLOTS * rd:SLOTS * (rd + 1)]
                for tt in range(NT):
                    ins = dve.tensor_scalar(sel[:, tt, :], slots_, slot_of[:, tt, bass.ds(e, 1)], None, ALU.is_equal)
                    if tt == NT - 1:
                        ins.then_inc(S("sel_ready" + r), 1)
                if wait:
                    dve.wait_ge(S("sel_turned" + r), e)
                for tt in range(NT):
                    ins = dve.tensor_scalar(selw[:, tt, :], slots_, slot_of[:, tt, bass.ds(e, 1)], comb[:, tt, bass.ds(e, 1)],
                                            ALU.is_equal, ALU.mult)
                    if tt == NT - 1:
                        ins.then_inc(S("selw_ready" + r), 1)

            def gathered(e, base, r):
                dve.wait_ge(S("gathered1" + r), e + 1)
                dve.tensor_copy(xe[:, 4:8, :], ps[:, 0, :].rearrange("p (k s) -> p k s", k=4)).then_inc(S("xe1" + r), 1)

            def expert(e, base, r, rd, tail):
                if not tail:
                    select(e + 1, rd, r, True)
                dve.wait_ge(S("silu" + r), e + 1)
                dve.wait_ge(S("unit_done" + r), e * 6 + (base + 4))
                dve.tensor_tensor(he, ps[:, 1, :], sge, ALU.mult).then_inc(S("act_ready" + r), 1)
                if not tail:
                    gathered(e + 1, base, r)
                dve.wait_ge(S("unit_done" + r), e * 6 + (base + 5))
                dve.tensor_copy(ye[:, 0:W], ps[:, 1, :]).then_inc(S("ye0" + r), 1)

            def experts(base, r, rd):
                select(0, rd, r, False)
                gathered(0, base, r)
                with dve.Fori(0, NE - 1) as e:
                    expert(e, base, r, rd, False)
                expert(NE - 1, base, r, rd, True)
                dve.wait_ge(S("scattered" + r), NE)

            dve.wait_ge(S("load_iota"), 16)
            dve.wait_ge(S("flag_set"), 1)
            settle()
            experts(n_before, "", 0)
            more = dve.value_load(flag[0:1, 0:1], min_val=0, max_val=1)
            with dve.If(more > 0):
                experts(0, "_b", 1)

            for tt in range(NT):
                g2 = gt[:, 3 * D:4 * D].rearrange("p (a b) -> p a b", a=2)
                hv = h_tok[:, tt, :].rearrange("p (a b) -> p a b", a=2)
                freed(dve.tensor_tensor(hv, buf("moe_y%d" % tt), g2, ALU.mult), "moe_y%d" % tt)
            pair_evacuated(dve, "moe_y0")
            pair_evacuated(dve, "moe_y1")
            link(dve.scalar_tensor_tensor(x, x, ALPHA, h_tok, ALU.mult, ALU.add))
            settle()
            row_stats(lambda tt: x[:, tt, :], D)
            apply_norm(lambda tt: x[:, tt, :], lambda tt: x[:, tt, :])
            for c in range(2):
                gain_bias(x, "ln2_g", "ln2_b", c)

            rms(x, h_tok, None, "pre0")
            dve.sem_inc(S("a_in_ready"), 1)
            for t in range(4):
                pair_evacuated(dve, ("a", t))
            row_stats(lambda tt: a_v[:, tt, :], 2048)
            apply_norm(lambda tt: a_v[:, tt, :], lambda tt: a_v[:, tt, :])
            for c in range(4):
                gain_bias(a_v, "a_ln_g", "a_ln_b", c)
            dve.sem_inc(S("v_normed"), 1)
            dve.wait_ge(S("load_tri"), 16)
            for c in range(2):
                dve.wait_ge(S("wsT_turned"), c + 1)
                o = buf(("wsT", c))
                ins = dve.tensor_tensor(a_wsT[:, 4 * c:4 * c + 4, :], o[:, 0, :].rearrange("p (g t) -> p g t", g=4),
                                        a_tri.unsqueeze(1).broadcast_to([P, 4, P]), ALU.mult)
                ins.then_inc(S("wsT_ready"), 1)
                if c == 1:
                    link(dve.tensor_copy(a_bs, o[:, 1, 0:KC]))
                dve.wait_ge(S("wsT_ready"), c + 1)
                settle()
                free_pair(("wsT", c))
            for i in range(4):
                pair_evacuated(dve, ("a", 4 + i))
                dve.wait_ge(S("sv_done"), i + 1)
                o = buf(("sv", i))
                for g in (2 * i, 2 * i + 1):
                    uv = a_u[:, :, 256 * g:256 * (g + 1)]
                    link(dve.scalar_tensor_tensor(uv, o[:, :, 256 * (g % 2):256 * (g % 2 + 1)], a_bs[:, g:g + 1], uv, ALU.add, ALU.mult))
                settle()
                free_pair(("sv", i))
            for t in range(4):
                pair_evacuated(dve, ("a", 8 + t))
                v = a_z[:, :, W * t:W * (t + 1)]
                dve.tensor_tensor(v, v, a_u[:, :, W * t:W * (t + 1)], ALU.mult).then_inc(S("y_gated"), 1)
            for t in range(2):
                pair_evacuated(dve, ("a_out", t))
            rms(y2, y2, None, "post0")
            link(dve.tensor_tensor(x, x, y2, ALU.add))
            settle()
            rms(x, y2, None, "pre1")
            dve.sem_inc(S("b_in_ready"), 1)

            dve.wait_ge(S("load_c_rope2"), 16)
            dve.wait_ge(S("load_c_mask"), 16)
            n_rope = 0
            for t in range(20):
                if BKIND[t] in "qk":
                    tab = 0 if BKIND[t] == "q" else 1
                    dve.wait_ge(S("unit_done"), end_of("b", t))
                    raw = buf(("b", t))
                    if n_rope >= 1:
                        dve.wait_ge(S("b_roped"), n_rope)
                    if n_rope >= 2:
                        dve.wait_ge(S("b_turned"), n_rope - 1)
                    dst = b_rope[:, n_rope % 2]
                    for tt in range(NT):
                        s = raw[:, tt, :].rearrange("p (h s d) -> p h s d", h=8, s=2)
                        q = b_t2[:, tt, :].rearrange("p (h s d) -> p h s d", h=8, s=2)
                        cos = rope2[:, tab, 0, tt, :].unsqueeze(1).broadcast_to([P, 8, HD])
                        link(dve.tensor_tensor(dst[:, tt, :].rearrange("p (h d) -> p h d", h=8),
                                               raw[:, tt, :].rearrange("p (h d) -> p h d", h=8), cos, ALU.mult))
                        for s_ in range(2):
                            sin = rope2[:, tab, 1, tt, 32 * s_:32 * (s_ + 1)].unsqueeze(1).broadcast_to([P, 8, 32])
                            link(dve.tensor_tensor(q[:, :, s_, :], s[:, :, 1 - s_, :], sin, ALU.mult))
                    settle()
                    free_pair(("b", t))
                    dve.tensor_tensor(dst, dst, b_t2, ALU.add).then_inc(S("b_roped"), 1)
                    n_rope += 1
                for act, g, c in slots[t]:
                    if act == "scores":
                        for i in range(2):
                            dve.wait_ge(S("b_scored"), 2 * (4 * g + c) + i + 1)
                            o = buf((act, g, c, i))
                            for hh in range(2):
                                h = 4 * c + 2 * i + hh
                                if i == 0 and hh == 0 and (g or c):
                                    dve.wait_ge(S("b_p_turned"), 2 * (4 * g + c))
                                for tt in range(NT):
                                    r = slice(P * tt, P * tt + P * (tt + 1))
                                    link(dve.tensor_tensor(b_p[:, 2 * i + hh, r], o[:, hh, r], amask[:, g, P * (1 - tt):2 * P], ALU.add))
                            settle()
                            free_pair((act, g, c, i))
                            for hh in range(2):
                                h = 4 * c + 2 * i + hh
                                for tt in range(NT):
                                    r = slice(P * tt, P * tt + P * (tt + 1))
                                    ins = dve.tensor_reduce(b_nm[:, g, tt, h:h + 1], b_p[:, 2 * i + hh, r], AX_X, ALU.max, negate=True)
                                    if tt == 1:
                                        ins.then_inc(S("b_maxed"), 1)
                                    else:
                                        link(ins)
                    elif act == "values":
                        dve.wait_ge(S("b_valued"), 4 * g + c + 1)
                        o = buf((act, g, c))
                        freed(dve.tensor_copy(b_acc[:, g, :, 4 * c:4 * c + 4, :],
                                              o[:, :, 0:256].rearrange("p t (h d) -> p t h d", h=4)), (act, g, c))
            dve.wait_ge(S("b_maxed"), 48)
            settle()
            dve.wait_ge(S("b_probs"), 48)
            one(dve.tensor_tensor(b_q, b_nm[:, 0], b_nm[:, 1], ALU.min))
            one(dve.tensor_tensor(b_q, b_q, b_nm[:, 2], ALU.min))
            for g in range(DIL):
                ins = dve.tensor_tensor(b_e[:, g], b_q, b_nm[:, g], ALU.subtract)
                if g == 2:
                    ins.then_inc(S("b_ediff"), 1)
                else:
                    link(ins)
            dve.wait_ge(S("b_eexp"), 1)
            one(dve.tensor_tensor(b_s, b_s, b_e, ALU.mult))
            one(dve.tensor_tensor(b_q, b_s[:, 0], b_s[:, 1], ALU.add))
            one(dve.tensor_tensor(b_q, b_q, b_s[:, 2], ALU.add))
            one(dve.reciprocal(b_q, b_q))
            for g in range(DIL):
                link(dve.tensor_tensor(b_e[:, g], b_e[:, g], b_q, ALU.mult))
            settle()
            for c in range(4):
                pair_evacuated(dve, ("values", 2, c))
            for g in range(DIL):
                for tt in range(NT):
                    v = b_acc[:, g, tt]
                    link(dve.tensor_tensor(v, v, b_e[:, g, tt, :].unsqueeze(2).broadcast_to([P, HEADS, HD]), ALU.mult))
            settle()
            acc = [b_acc[:, g].rearrange("p t h d -> p t (h d)") for g in range(DIL)]
            one(dve.tensor_tensor(acc[0], acc[0], acc[1], ALU.add))
            one(dve.tensor_tensor(acc[0], acc[0], acc[2], ALU.add))
            for t in (16, 17):
                pair_evacuated(dve, ("b", t))
            dve.tensor_tensor(b_z, b_z, acc[0], ALU.mult).then_inc(S("b_o_ready"), 1)
            for t in range(2):
                pair_evacuated(dve, ("b_out", t))
            rms(y2, y2, None, "post1")
            dve.tensor_tensor(x, x, y2, ALU.add).then_inc(S("out_ready"), 1)

        @block.gpsimd
        def _(pool):
            pool.memset(minus_half, -0.5).then_inc(S("half_set"), 1)
            pool.wait_ge(S("half_set"), 1)
            for n, eps in enumerate(norm_eps):
                pool.wait_ge(S("stats_ready"), n + 1)
                pool.tensor_scalar(ms, mv[:, :, 1], eps, None, ALU.add).then_inc(S("eps_added"), 1)
                pool.wait_ge(S("eps_added"), n + 1)
                pool.tensor_tensor(rstd, ms, minus_half, ALU.pow).then_inc(S("rstd_ready"), 1)

        @block.scalar
        def _(act):
            def evacuate(key, dst, view=None, func=ACT.Copy):
                src = buf(key) if view is None else view(buf(key))
                freed(act.activation(dst, src, func), key)

            def chunks(dstT, c, o=0):
                return dstT[:, o + 4 * c:o + 4 * c + 4, :].rearrange("p k (t n) -> p t k n", t=NT)

            def four(p_):
                return p_.rearrange("p t (k n) -> p t k n", k=4)

            act.wait_ge(S("rows_turned"), 1)
            act.activation(sT, buf("turn_rows")[:, 0, 0:16], ACT.Silu).then_inc(S("silu_c"), 1)
            act.activation(cwT, buf("turn_rows")[:, 1, 0:256].rearrange("p (k n) -> p k n", k=KC), ACT.Copy).then_inc(S("pair_free2"), 1)
            act.wait_ge(S("neg_abs"), 1)
            act.activation(la[:, 0, :], la[:, 0, :], ACT.Exp).then_inc(S("exp_abs"), 1)
            act.wait_ge(S("wdec_exps"), 1)
            act.activation(wdec, wdec, ACT.Exp).then_inc(S("wdec_exp"), 1)
            for s in range(2):
                for c in range(2):
                    act.wait_ge(S("uT_turned"), 2 * s + c + 1)
                    evacuate(("uT", s, c), chunks(XT, c, 8 * s), four)

            def sigmoid_z(i):
                pair_evacuated(act, ("glu", 2 * i + 1))
                v = tmp[:, 2 * i:2 * i + 2, :]
                act.activation(v, v, ACT.Sigmoid).then_inc(S("sig_z"), 1)

            def turned_z(i):
                act.wait_ge(S("zT_turned"), i + 1)
                evacuate(("zT", i), z_pad[:, 4 * i:4 * i + 4, PAD:PAD + T].rearrange("p k (t n) -> p t k n", t=NT), four)
            sigmoid_z(0)
            turned_z(0)
            sigmoid_z(1)
            turned_z(1)
            for n, (dst, t) in enumerate(((kT, 0), (kT, 1), (qT, 0), (qT, 1))):
                act.wait_ge(S("heads_turned"), n + 1)
                evacuate((("kT", t), ("qT", t))[n // 2], chunks(dst, t), four)
            for i in range(4):
                act.wait_ge(S("state_done"), 2 * i + 2)
                freed(act.activation(state[:, 2 * i:2 * i + 2].rearrange("p h d v -> p h (d v)"), buf(("S", i)), ACT.Copy), ("S", i))
            for c in range(2):
                act.wait_ge(S("cz_turned"), c + 1)
                evacuate(("cz", c), cz[:, :, W * c:W * (c + 1)])

            def decays(h):
                if h >= 2:
                    act.wait_ge(S("ret_summed"), h - 1)
                Q = tmp[:, 4 + h % 2, :].rearrange("p (d n) -> p d n", d=2)
                act.activation(Q[:, 0, :], row_fb[:, 0, :], ACT.Exp, scale=lg[:, h:h + 1])
                act.activation(Q[:, 1, :], row_fb[:, 1, :], ACT.Exp, scale=lg[:, H + h:H + h + 1])
                act.wait_ge(S("ret_exps"), h + 1)
                E = tmp[:, 2 + h % 2, :]
                act.activation(E, E, ACT.Exp).then_inc(S("ret_exped"), 1)
            act.wait_ge(S("load_c_rows"), 16)
            decays(0)
            decays(1)
            for i in range(4):
                pair_evacuated(act, ("g", i))
                v = sg[:, :, W * i:W * (i + 1)]
                act.activation(v, v, ACT.Silu).then_inc(S("silu_g"), 1)
                if i < 3:
                    decays(2 * i + 2)
                    decays(2 * i + 3)
            act.wait_ge(S("cz_normed"), 1)
            act.activation(cz, cz, ACT.Silu).then_inc(S("cz_ready"), 1)
            for t in range(4):
                pair_evacuated(act, ("gate", t))
                v = gates[:, :, W * t:W * (t + 1)]
                act.activation(v, v, ACT.Sigmoid).then_inc(S("sig_gates"), 1)
            act.wait_ge(S("unit_done"), end_of("gate", 3))
            for c in range(4):
                act.wait_ge(S("retT_turned"), c + 1)
                evacuate(("retT", c), chunks(XT, c), four)
            for c in range(2):
                act.wait_ge(S("cvT_turned"), c + 1)
                evacuate(("cvT", c), chunks(XT2, c), four)
            for c in range(2):
                act.wait_ge(S("mT_turned"), c + 1)
                evacuate(("mT", c), chunks(XT, c), four)
            for c in range(2):
                act.wait_ge(S("eT_turned"), c + 1)
                evacuate(("eT", c), chunks(XT2, c), four)
            act.wait_ge(S("router_exp"), 1)
            g_e, _ = carve(NT, NG, on=o_rt + NT)
            e2, _ = carve(NT, on=o_rt + NT + NT * NG + NT + NT * NG + NT + NT * NG * NEG + NT * NEG + NT + 2 * NT * NEG + NT)
            act.activation(g_e, g_e, ACT.Exp).then_inc(S("router_exped"), 1)
            act.wait_ge(S("router_exp"), 2)
            act.activation(e2, e2, ACT.Exp).then_inc(S("router_exped"), 1)

            def gathered(e, r):
                act.wait_ge(S("gathered0" + r), e + 1)
                act.activation(xe[:, 0:4, :], ps[:, 2, :].rearrange("p (k s) -> p k s", k=4), ACT.Copy).then_inc(S("xe0" + r), 1)

            def expert(e, base, r, head, tail):
                act.wait_ge(S("unit_done" + r), e * 6 + (base + 2))
                if not head:
                    act.wait_ge(S("act_ready" + r), e)
                act.activation(sge, ps[:, 0, :], ACT.Silu).then_inc(S("silu" + r), 1)
                act.wait_ge(S("sel_turned" + r), e + 1)
                if not head:
                    act.wait_ge(S("scattered" + r), e)
                act.activation(selT, ps[:, 3, 0:T], ACT.Copy).then_inc(S("selT" + r), 1)
                if not tail:
                    gathered(e + 1, r)
                act.wait_ge(S("h_turned" + r), e + 1)
                act.activation(heT, ps[:, 3, :].rearrange("p (k s) -> p k s", k=4), ACT.Copy).then_inc(S("hT" + r), 1)
                act.wait_ge(S("unit_done" + r), e * 6 + (base + 6))
                act.activation(ye[:, W:2 * W], ps[:, 2, :], ACT.Copy).then_inc(S("ye1" + r), 1)

            def experts(base, r):
                gathered(0, r)
                expert(0, base, r, True, False)
                with act.Fori(1, NE - 1) as e:
                    expert(e, base, r, False, False)
                expert(NE - 1, base, r, False, True)

            experts(n_before, "")
            act.wait_ge(S("flag_set"), 1)
            more = act.value_load(flag[0:1, 0:1], min_val=0, max_val=1)
            with act.If(more > 0):
                experts(0, "_b")

            for c in range(2):
                act.wait_ge(S("aT_turned"), c + 1)
                evacuate(("aT", c), chunks(XT2, c), four)
            for t in range(12):
                act.wait_ge(S("unit_done"), end_of("a", t))
                dst = (a_v, a_u, a_z)[t // 4][:, :, W * (t % 4):W * (t % 4 + 1)]
                freed(act.activation(dst, buf(("a", t)), ACT.Gelu if t < 8 else ACT.Silu), ("a", t))
            for c in range(4):
                act.wait_ge(S("yT_turned"), c + 1)
                evacuate(("yT", c), chunks(XT, c), four)

            def evac_y(key, ready):
                freed(act.activation(y2[:, :, W * key[1]:W * (key[1] + 1)], buf(key), ACT.Copy), key)
            for t in range(2):
                act.wait_ge(S("unit_done"), end_of("a_out", t, 4))
                evac_y(("a_out", t), None)
            for c in range(2):
                act.wait_ge(S("bT_turned"), c + 1)
                evacuate(("bT", c), chunks(XT2, c), four)
            n_rope = 0
            for t in range(20):
                g = BGROUP[t]
                if BKIND[t] in "vz":
                    act.wait_ge(S("unit_done"), end_of("b", t))
                    if BKIND[t] == "v":
                        if g:
                            act.wait_ge(S("b_valued"), 4 * (g - 1) + 2 * BIDX[t] + 2)
                        dst = b_v[:, :, W * BIDX[t]:W * (BIDX[t] + 1)]
                        freed(act.activation(dst, buf(("b", t)), ACT.Copy), ("b", t))
                    else:
                        freed(act.activation(b_z[:, :, W * BIDX[t]:W * (BIDX[t] + 1)], buf(("b", t)), ACT.Silu), ("b", t))
                if t and BKIND[t - 1] in "qk":
                    n_rope += 1
                    act.wait_ge(S("b_turned"), n_rope)
                    dst = (b_qT, b_kT)[BKIND[t - 1] == "k"][:, BGROUP[t - 1] % 2]
                    evacuate(("bqk", t - 1), chunks(dst, BIDX[t - 1]), four)
                for what, g, c in slots[t]:
                    if what == "turn":
                        n = 4 * g + c
                        for i in range(2):
                            act.wait_ge(S("b_p_turned"), 2 * n + i + 1)
                            if g:
                                act.wait_ge(S("b_valued"), 4 * (g - 1) + c + 1)
                            freed(act.activation(b_pT[:, c, 2 * i:2 * i + 2, :], buf(("turn", g, c, i))[:, :, 0:384], ACT.Copy), ("turn", g, c, i))
                    elif what == "scores":
                        for hh in range(4):
                            h = 4 * c + hh
                            act.wait_ge(S("b_maxed"), 4 * (4 * g + c) + hh + 1)
                            for tt in range(NT):
                                r = slice(P * tt, P * tt + P * (tt + 1))
                                ins = act.activation(b_p[:, hh, r], b_p[:, hh, r], ACT.Exp, bias=b_nm[:, g, tt, h:h + 1],
                                                     accum_out=b_s[:, g, tt, h:h + 1])
                                if tt == 1:
                                    ins.then_inc(S("b_probs"), 1)
            act.wait_ge(S("b_ediff"), 1)
            act.activation(b_e, b_e, ACT.Exp).then_inc(S("b_eexp"), 1)
            for c in range(2):
                act.wait_ge(S("oT_turned"), c + 1)
                evacuate(("oT", c), chunks(XT, c), four)
            for t in range(2):
                act.wait_ge(S("unit_done"), end_of("b_out", t))
                evac_y(("b_out", t), None)


def tables():
    f = np.float32
    tok = np.arange(T)
    m = (np.arange(P)[:, None] + P * np.arange(NT)[None, :])[:, :, None]
    n = tok[None, None, :]
    out = {
        "c_dist_f": np.maximum(n - m, 0).astype(f),
        "c_dist_b": np.maximum(m - n, 0).astype(f),
        "c_log": (np.log(DK ** -0.5) + np.log(2.0) * (n == m)).astype(f),
        "c_rows": np.broadcast_to(np.stack([tok + 1, T - tok]), (P, 2, T)).astype(f).copy(),
        "c_pos": np.stack([T - 1 - m[:, :, 0], m[:, :, 0]], axis=1).astype(f),
        "c_ident": np.eye(P, dtype=f),
        "c_tri": np.triu(np.ones((P, P), f)),
        "c_before": np.triu(np.ones((P, P), f), 1),
        "c_iota": np.broadcast_to(tok, (P, T)).astype(f).copy(),
    }

    def halves(ang, scale=1.0):
        cos, sin = np.cos(ang.astype(f)), np.sin(ang.astype(f))
        t = np.stack([np.concatenate([cos, cos], -1), np.concatenate([-sin, sin], -1)])
        return (t * scale).astype(f).reshape(2, NT, P, -1).transpose(2, 0, 1, 3)

    inv = (f(10000.0) ** (-np.arange(DK // 4, dtype=f) / f(DK // 4))).astype(f)
    r, col = (tok // 64).astype(f), (tok % 64).astype(f)
    out["c_rope1"] = halves(np.concatenate([r[:, None] * inv, col[:, None] * inv], -1)).copy()
    inv2 = (f(1.0) / (f(10000.0) ** (np.arange(0, HD, 2, dtype=f) / f(HD)))).astype(f)
    ang = tok.astype(f)[:, None] * inv2[None, :]
    out["c_rope2"] = np.stack([halves(ang, HD ** -0.5), halves(ang)], axis=1).copy()
    rel = np.concatenate([P + np.arange(P)[:, None] - np.arange(P), np.arange(P)[:, None] - np.arange(P)], -1)
    masks = []
    for window, step in ((128, 1), (512, 4), (2048, 16)):
        masks.append(np.where((rel >= 0) & (rel <= window) & (rel % step == 0), 0.0, -1.0e30))
    out["c_mask"] = np.stack(masks, axis=1).astype(f)
    return out


_INS = ["x", "c", "ctx", "c_ctx", "w_ada", "b_ada", "w_in", "b_in", "ret_decay_fwd", "ret_decay_bwd", "w_ret_out",
        "conv_dw", "conv_dw_b", "conv_ln_g", "conv_ln_b", "w_conv_out", "b_conv_out", "w_mix_out", "b_mix_out",
        "ln1_g", "ln1_b", "w_router_grp", "b_router_grp", "w_router_exp", "b_router_exp", "w_exp_gate", "w_exp_up",
        "w_exp_down", "ln2_g", "ln2_b", "norm_pre_2", "norm_post_2", "a_w_in_2", "a_ln_g_2", "a_ln_b_2", "a_w_s_2",
        "a_b_s_2", "a_w_out_2", "b_w_in_2", "b_w_out_2"]


def kernel(**inputs):
    import concourse.bacc as bacc
    from concourse.bass_utils import run_bass_kernel_spmd

    nc = bacc.Bacc("TRN2", target_bir_lowering=False, num_devices=1)
    given = {name: np.ascontiguousarray(inputs[name]) for name in _INS}
    given.update({name: np.ascontiguousarray(t) for name, t in tables().items()})
    arrays, aps = {}, {}
    for name, v in given.items():
        arrays["in_" + name] = v
        aps[name] = nc.dram_tensor("in_" + name, v.shape, mybir.dt.from_np(v.dtype), kind="ExternalInput").ap()
    out = nc.dram_tensor("out_0", (1, T, D), F32, kind="ExternalOutput").ap()
    build(nc, aps, out)
    r = run_bass_kernel_spmd(nc, [arrays], core_ids=[0])
    return r.results[0]["out_0"]
```

```python
from contextlib import ExitStack

import numpy as np

import concourse.bass as bass
from concourse import mybir

F32 = mybir.dt.float32
F32R = mybir.dt.float32r
ALU = mybir.AluOpType
ACT = mybir.ActivationFunctionType
AX_X = mybir.AxisListType.X

P = 128
T = 256
NT = T // P
D = 1024
KC = D // P
W = 512
HALF_K = 512
UC = HALF_K // P
H = 8
DK = 128
DV = 256
TAPS = 31
PAD = TAPS // 2
NG, NEG = 4, 8
NE = NG * NEG
FF = 512
SLOTS = 128
ROUNDS = T // SLOTS
HEADS = 16
HD = 64
DIL = 3
LN_EPS = 1e-5
RMS_EPS = 1e-6
ALPHA = 2.0 ** 0.25
RING = 6
ARENA = 53200 - RING * UC * W
FLAG_AT = 16512
RING_AT = FLAG_AT + 32
ARENA_AT = RING_AT + 4 * RING * UC * W
HI = 3
POOL_UNITS = (2, 4)
DVE_UNITS = (0, 1, 3, 5)
RING2 = 4
AUXN = 4

GLU = [12, 14, 13, 15]
KCOLS = [2, 3]
VCOLS = [4, 5, 6, 7]
QCOLS = [0, 1]
GCOLS = [8, 9, 10, 11]
GATECOLS = [16, 17, 18, 19]
BCOLS = list(range(12)) + [12, 13, 14, 15, 18, 19, 16, 17]
BKIND = (["q", "q", "k", "k", "v", "v"] * 2) + ["q", "q", "k", "k", "z", "z", "v", "v"]
BGROUP = [0] * 6 + [1] * 6 + [2] * 8
BIDX = [0, 1] * 10


def attention_slots():
    after = {t: [] for t in range(20)}
    for g, first in ((0, 5), (1, 11), (2, 16)):
        for c in range(4):
            for stage, name in enumerate(("scores", "turn", "values")):
                if first + c + stage < 19:
                    after[first + c + stage].append(((2 - stage, c), name, g, c))
    steps = {t: [s[1:] for s in sorted(a)] for t, a in after.items()}
    steps[18] = [s for s in steps[18] if s[0] != "values"]
    steps[19] = [("values", 2, 0), ("turn", 2, 2), ("scores", 2, 3), ("values", 2, 1), ("turn", 2, 3), ("values", 2, 2), ("values", 2, 3)]
    return steps


def build(nc, a, out):
    with ExitStack() as ctx:
        sems = {}

        def S(name):
            if name not in sems:
                sems[name] = ctx.enter_context(nc.semaphore(name))
            return sems[name]

        arena = nc.alloc_sbuf_tensor_at("arena", [P, ARENA], F32, offset=ARENA_AT)
        at = [0]

        def carve(*shape, on=None):
            n = int(np.prod(shape))
            o = at[0] if on is None else on
            if on is None:
                at[0] += n
                assert at[0] <= ARENA, at[0]
            v = arena[:, o:o + n]
            if len(shape) == 2:
                v = v.rearrange("p (a b) -> p a b", a=shape[0])
            if len(shape) == 3:
                v = v.rearrange("p (a b c) -> p a b c", a=shape[0], b=shape[1])
            if len(shape) == 4:
                v = v.rearrange("p (a b c d) -> p a b c d", a=shape[0], b=shape[1], c=shape[2])
            return v, o

        def single_pass(name, *shape, on=None):
            return nc.alloc_sbuf_tensor_at(name, [P] + list(shape), F32R, offset=RING_AT if on is None else ARENA_AT + 4 * on)

        ring = nc.alloc_sbuf_tensor_at("ring", [P, RING, UC, W], F32, offset=RING_AT)
        aux, _ = carve(AUXN, W)
        x, _ = carve(NT, D)
        XT, o_XT = carve(16, T)
        XT2, o_XT2 = carve(8, T)
        mod_lat, o_ml = carve(2048)
        z_pad, o_zp = carve(KC, T + 2 * PAD)
        tmp, o_tmp = carve(6, W)
        qT, o_qT = carve(H, T)
        kT, o_kT = carve(H, T)
        v_lat, o_v = carve(NT, H * DV)
        k_ctx, o_kc = carve(NT, D)
        v_ctx, o_vc = carve(NT, H * DV)
        state, o_S = carve(H, 2, DV)
        consts, o_cn = carve(3 * NT * T + 2 * T + 2 * NT * P + 4 * NT * HD + DIL * 2 * P + P)
        small, o_sm = carve(836)

        conv, _ = carve(KC, T, on=o_ml)
        cz, _ = carve(NT, D, on=o_zp)
        mod_ctx, _ = carve(2048, on=o_S)
        z_tok, _ = carve(2, NT, W, on=o_S + 2048)
        roped, _ = carve(2, NT, W, on=o_XT2)
        o_lo, _ = carve(NT, 4 * DV, on=o_kc)
        o_hi, _ = carve(NT, 4 * DV, on=o_XT2)
        sg, _ = carve(NT, H * DV, on=o_vc)
        gates, _ = carve(NT, 2048, on=o_v)
        mod_tail, _ = carve(4096, on=o_S)
        u_lat, _ = carve(NT, D, on=o_v)
        u_ctx, _ = carve(NT, D, on=o_v + 2048)
        x_ctx, _ = carve(NT, D, on=o_vc)
        s_lat, _ = carve(KC, P, on=o_qT)
        s_ctx, _ = carve(KC, P, on=o_kT)
        rows16 = arena[0:16, o_tmp:o_tmp + P]
        rows32 = arena[0:32, o_tmp + 1024:o_tmp + 2048]

        o = o_cn

        def const(*shape):
            nonlocal o
            v, _ = carve(*shape, on=o)
            o += int(np.prod(shape))
            return v
        dist_f = const(NT, T)
        dist_b = const(NT, T)
        log_c = const(NT, T)
        row_fb = const(2, T)
        rope1 = const(2, NT, P)
        rope2 = const(2, 2, NT, HD)
        amask = const(DIL, 2 * P)
        ident = const(P)
        o = o_sm
        lg = const(2 * H)
        la = const(3, 2 * H)
        pos = const(2, NT)
        wdec = const(2, NT, H)
        sT = const(2 * KC)
        cwT = const(KC, 32)
        stats = const(NT, 4, 6)
        mv = const(NT, 2)
        ms = const(NT)
        rstd = const(NT)
        minus_half = const(NT)
        sq = const(NT)
        wr = const(KC, 36)
        br = const(36)
        lgt = const(NT, 36)
        assert o <= o_sm + 836

        flag = nc.alloc_sbuf_tensor_at("flag", [1, 1], mybir.dt.int32, offset=FLAG_AT)
        ps = ctx.enter_context(nc.psum_tensor("ps", [P, 8, W], F32))

        def pair(p):
            return ps[:, 2 * p:2 * p + 2, :]

        units = []
        first = {}

        def stream(name, w, cols, nk):
            first[name] = len(units)
            for c in cols:
                for j in range(nk):
                    units.append(w[HALF_K * j:HALF_K * (j + 1), W * c:W * (c + 1)])

        w_in = a["w_in"][0]
        stream("ada", a["w_ada"][0], range(4), 2)
        for name, cols in (("glu", GLU), ("k", KCOLS), ("v", VCOLS), ("q", QCOLS), ("g", GCOLS), ("gate", GATECOLS)):
            stream(name, w_in, cols, 2)
        stream("ada_tail", a["w_ada"][0], range(4, 12), 2)
        stream("ret", a["w_ret_out"][0], range(2), 4)
        stream("conv", a["w_conv_out"][0], range(2), 2)
        stream("mix", a["w_mix_out"][0], range(2), 2)
        n_before = len(units)
        first["moe"] = n_before
        n_moe = 6 * NE
        units += [None] * n_moe
        stream("a", a["a_w_in_2"][0], [4, 5, 6, 7, 0, 1, 2, 3, 8, 9, 10, 11], 2)
        stream("a_out", a["a_w_out_2"][0], range(2), 4)
        stream("b", a["b_w_in_2"][0], BCOLS, 2)
        stream("b_out", a["b_w_out_2"][0], range(2), 2)

        slots_of, fills = [], []
        for n in range(len(units)):
            slots_of.append(n % RING if n < first["a"] else (n - first["a"]) % RING2)
            fills.append(slots_of.count(slots_of[n]))

        def moe_src(kind, e, j):
            if kind == "down":
                return a["w_exp_down"][0, bass.ds(e, 1), :, W * j:W * (j + 1)].rearrange("e (k p) c -> p (e k) c", p=P)
            w = a["w_exp_gate"] if kind == "gate" else a["w_exp_up"]
            return w[0, bass.ds(e, 1), HALF_K * j:HALF_K * (j + 1), :].rearrange("e (k p) c -> p (e k) c", p=P)

        def end_of(name, t, nk=2):
            return first[name] + (t + 1) * nk

        rows = []
        row_after = {}
        row_of = {}

        def bring(key, vec, unit):
            row_of[key] = len(rows)
            rows.append(vec)
            row_after.setdefault(unit, []).append(len(rows) - 1)

        def vec(name, c, i=0):
            return a[name][i:i + 1, W * c:W * (c + 1)]

        used = [0] * 4
        plan = {}

        def take(key, p):
            used[p] += 1
            plan[key] = (p, used[p])

        main = [0]

        def take_main(key):
            take(key, main[0] % 2)
            main[0] += 1

        side = [0]

        def take_side(key):
            take(key, 2 + side[0] % 2)
            side[0] += 1

        take("turn_rows", 2)
        for t in range(4):
            take_main(("ada", t))
            bring(("ada", t), vec("b_ada", t), t)
        for s in range(2):
            for c in range(2):
                take_side(("uT", s, c))
        for t in range(4):
            take_main(("glu", t))
            bring(("glu", t), vec("b_in", GLU[t]), first["glu"] + 2 * t + 1)
        take_side(("zT", 0))
        take_side(("zT", 1))
        if main[0] % 2:
            main[0] += 1
        for t in range(2):
            take("k_lat%d" % t, 0)
            take("k_ctx%d" % t, 1)
            bring(("k", t), vec("b_in", KCOLS[t]), first["k"] + 2 * t + 1)
        take_side(("kT", 0))
        for t in range(4):
            take("v_lat%d" % t, 0)
            take("v_ctx%d" % t, 1)
            bring(("v", t), vec("b_in", VCOLS[t]), first["v"] + 2 * t + 1)
        take_side(("kT", 1))
        for t in range(2):
            take_main(("q", t))
            bring(("q", t), vec("b_in", QCOLS[t]), first["q"] + 2 * t + 1)
        take_side(("qT", 0))
        take_side(("qT", 1))
        for i in range(4):
            take_side(("S", i))
        for c in range(2):
            take_side(("cz", c))
        side[0] += side[0] % 2
        for i in range(4):
            take(("sc", i), 2)
            take(("av", i), 3)
            take_main(("g", i))
            bring(("g", i), vec("b_in", GCOLS[i]), first["g"] + 2 * i + 1)
        for c in range(2):
            bring(("conv_g", c), vec("conv_ln_g", c), first["gate"] + 1)
            bring(("conv_b", c), vec("conv_ln_b", c), first["gate"] + 1)
        for t in range(4):
            take_main(("gate", t))
            bring(("gate", t), vec("b_in", GATECOLS[t]), first["gate"] + 2 * t + 4)
        for t in range(8):
            take_main(("ada_tail", t))
            bring(("ada_tail", t), vec("b_ada", 4 + t), first["ada_tail"] + 2 * t + 4)
        for c in range(4):
            take_side(("retT", c))
        for c in range(2):
            take_side(("cvT", c))
        for t in range(2):
            take_main(("ret", t))
        for t in range(2):
            take_main(("conv", t))
            bring(("conv", t), vec("b_conv_out", t), first["conv"] + 2 * t + 1)
        for c in range(2):
            take_side(("mT", c))
        for t in range(2):
            take_main(("mix", t))
            bring(("mix", t), vec("b_mix_out", t), first["mix"] + 2 * t + 1)
        for c in range(2):
            bring(("ln1_g", c), vec("ln1_g", c), first["mix"] + 3)
            bring(("ln1_b", c), vec("ln1_b", c), first["mix"] + 3)
        for c in range(2):
            take_side(("eT", c))
        main[0] += main[0] % 2
        take("router", 0)
        take_side(("rank", 0))
        take_side("most")
        entry0, entry1 = used[0], used[1]
        take("moe_y0", 2)
        take("moe_y1", 3)
        for c in range(2):
            bring(("ln2_g", c), vec("ln2_g", c), first["a"])
            bring(("ln2_b", c), vec("ln2_b", c), first["a"])
        for c in range(2):
            bring(("pre0", c), vec("norm_pre_2", c, 0), first["a"] + RING2 - 1)
        for c in range(2):
            take_side(("aT", c))
        for t in range(8):
            take_main(("a", t))
        for c in range(4):
            bring(("a_ln_g", c), vec("a_ln_g_2", c), first["a"] + (8 if c < 2 else 14))
            bring(("a_ln_b", c), vec("a_ln_b_2", c), first["a"] + (8 if c < 2 else 14))
        for c in range(2):
            take_side(("wsT", c))
        for i in range(4):
            take_side(("sv", i))
        for t in range(8, 12):
            take_main(("a", t))
        for c in range(4):
            take_side(("yT", c))
        for t in range(2):
            take_main(("a_out", t))
        for c in range(2):
            bring(("post0", c), vec("norm_post_2", c, 0), first["a_out"] + 7)
        for c in range(2):
            bring(("pre1", c), vec("norm_pre_2", c, 1), first["a_out"] + 7)
        for c in range(2):
            take_side(("bT", c))
        slots = attention_slots()
        for t in range(20):
            take_main(("b", t))
            if t and BKIND[t - 1] in "qk":
                take_side(("bqk", t - 1))
            for act, g, c in slots[t]:
                if act in ("scores", "turn"):
                    for i in range(2):
                        take((act, g, c, i), 2 + i)
                else:
                    take_main((act, g, c))
        for c in range(2):
            take_side(("oT", c))
        for t in range(2):
            take_main(("b_out", t))
        for c in range(2):
            bring(("post1", c), vec("norm_post_2", c, 1), first["b_out"] + 3)

        def row_ready(eng, key):
            n = row_of[key]
            eng.wait_ge(S("row_full%d" % (n % AUXN)), 16 * (n // AUXN + 1))
            return aux[:, n % AUXN, :]

        def bc2(v, n=W):
            return v.unsqueeze(1).broadcast_to([P, NT, n])

        def pair_evacuated(eng, key):
            p, k = plan[key]
            eng.wait_ge(S("pair_free%d" % p), k)

        def freed(ins, key):
            ins.then_inc(S("pair_free%d" % plan[key][0]), 1)

        def buf(key):
            return pair(plan[key][0])

        def heads_T(t, tt):
            return slice(4 * t, 4 * t + 4), slice(P * tt, P * (tt + 1))

        free0 = o_XT2 + 2048
        b_qT, _ = carve(2, KC, T, on=o_XT)
        b_kT, _ = carve(2, KC, T, on=free0)
        b_v, _ = carve(NT, D, on=free0 + 4096)
        b_acc, _ = carve(DIL, NT, HEADS, HD, on=free0 + 6144)
        b_z, _ = carve(NT, D, on=free0 + 12288)
        b_p, _ = carve(4, 384, on=free0 + 14336)
        b_pT, _ = carve(2, 4, 384, on=free0 + 15872)
        b_t2, _ = carve(NT, W, on=free0 + 18944)
        b_rope, _ = carve(2, NT, W, on=free0 + 19968)
        b_nm, _ = carve(DIL, NT, HEADS, on=o_sm)
        b_s, _ = carve(DIL, NT, HEADS, on=o_sm + 96)
        b_e, _ = carve(DIL, NT, HEADS, on=o_sm + 192)
        b_q, _ = carve(NT, HEADS, on=o_sm + 288)
        a_v, _ = carve(NT, 2048, on=free0)
        a_u, _ = carve(NT, 2048, on=free0 + 4096)
        a_z, _ = carve(NT, 2048, on=free0 + 8192)
        a_ws, _ = carve(KC, P, on=free0 + 12288)
        a_wsT, _ = carve(KC, P, on=free0 + 13312)
        a_tri, _ = carve(P, on=free0 + 14336)
        a_bs, _ = carve(KC, on=free0 + 14336 + P)
        a_bsr = arena[0:KC, free0 + 14600:free0 + 14600 + P]
        y2, _ = carve(NT, D, on=free0 + 6144)
        xt2_hi = single_pass("xt2_hi", KC, T, on=o_XT2)
        xt2_lo = single_pass("xt2_lo", KC, T, on=free0 + 22016)
        yt_hi = single_pass("yt_hi", 16, T, on=o_XT)
        yt_lo = single_pass("yt_lo", 16, T, on=free0)
        ot_hi = single_pass("ot_hi", KC, T, on=o_XT)
        ot_lo = single_pass("ot_lo", KC, T, on=o_XT + KC * T)
        w_hi2 = [single_pass("w_hi2_%d" % i, UC, W, on=(RING2 + i - RING) * UC * W) for i in range(2)]
        w_hi2.append(single_pass("w_hi2_2", UC, W, on=free0 + 24064))
        w_lo2 = single_pass("w_lo2", RING2, UC, W)
        xe_hi = single_pass("xe_hi", KC, SLOTS, on=free0)
        xe_lo = single_pass("xe_lo", KC, SLOTS, on=free0 + 10240)
        sge, _ = carve(FF, on=free0 + 1024)
        he, _ = carve(FF, on=free0 + 1536)
        heT_hi = single_pass("heT_hi", FF // P, SLOTS, on=free0 + 2048)
        heT_lo = single_pass("heT_lo", FF // P, SLOTS, on=free0 + 11264)
        ye_hi = single_pass("ye_hi", D, on=free0 + 2560)
        ye_lo = single_pass("ye_lo", D, on=free0 + 5008)
        slot_weight, _ = carve(2, on=free0 + 14740)
        weighted, _ = carve(T, on=free0 + 14744)
        w_hi = single_pass("w_hi", HI, UC, W, on=free0 + 15000)
        w_lo = single_pass("w_lo", RING, UC, W)
        assert free0 + 15000 + HI * UC * W <= o_S
        sel, _ = carve(NT, SLOTS, on=free0 + 3584)
        selw, _ = carve(NT, SLOTS, on=free0 + 3840)
        selT = single_pass("selT", T, on=free0 + 4096)
        iota, _ = carve(T, on=free0 + 4352)
        before, _ = carve(P, on=free0 + 4608)
        ones, _ = carve(P, on=free0 + 4736)
        hits, _ = carve(NT, NE, on=free0 + 4864)
        slot_of, _ = carve(NT, NE, on=free0 + 4928)
        most, _ = carve(2, on=free0 + 4992)
        flag_f = arena[0:1, free0 + 5000:free0 + 5001]
        comb, _ = carve(NT, NE, on=free0 + 6144)
        rt, o_rt = carve(1024, on=free0 + 6300)
        h_tok, _ = carve(NT, D, on=free0 + 8192)
        assert free0 + 8192 + 2048 <= o_v + 4096

        norm_eps = [LN_EPS] * H + [LN_EPS, LN_EPS, LN_EPS, RMS_EPS, LN_EPS, RMS_EPS, RMS_EPS, RMS_EPS]

        OFF = {"": 0, "_b": NE}
        MOE_NORM = H + 2

        block = ctx.enter_context(nc.Block())

        @block.sync
        def _(sp):
            names = ["c_dist_f", "c_dist_b", "c_log", "c_rows", "c_rope1", "c_rope2", "c_mask", "c_ident"]
            views = [dist_f, dist_b, log_c, row_fb, rope1, rope2, amask, ident]
            sp.dma_start(ident, a["c_ident"]).then_inc(S("load_ident"), 16)
            sp.dma_start(rows16[0:8], a["c"].rearrange("o (k p) -> (o k) p", p=P)).then_inc(S("load_c"), 16)
            sp.dma_start(rows16[8:16], a["c_ctx"].rearrange("(k p) -> k p", p=P)).then_inc(S("load_cc"), 16)
            sp.dma_start(rows32[0:TAPS], a["conv_dw"][0]).then_inc(S("load_taps"), 16)
            sp.dma_start(rows32[TAPS:32], a["conv_dw_b"]).then_inc(S("load_tapb"), 16)
            sp.dma_start(lg[:, 0:H], a["ret_decay_fwd"].broadcast_to([P, H])).then_inc(S("load_df"), 16)
            sp.dma_start(lg[:, H:2 * H], a["ret_decay_bwd"].broadcast_to([P, H])).then_inc(S("load_db"), 16)
            sp.dma_start(pos, a["c_pos"]).then_inc(S("load_pos"), 16)

            def unit(n, src):
                if n >= RING:
                    sp.wait_ge(S("unit_done"), n - RING + 1 if n < first["a"] else max(first["a"], n - RING2 + 1))
                k = slots_of[n]
                sp.dma_start(ring[:, k], src.rearrange("(k p) c -> p k c", p=P)).then_inc(S("w_full%d" % k), 16)

            def rows_for(n):
                for r in row_after.get(n, []):
                    if r >= AUXN:
                        sp.wait_ge(S("row_used"), r - AUXN + 1)
                    sp.dma_start(aux[:, r % AUXN, :], rows[r].broadcast_to([P, W])).then_inc(S("row_full%d" % (r % AUXN)), 16)

            for n in range(n_before):
                unit(n, units[n])
                rows_for(n)
                if n == n_before - 1:
                    sp.wait_ge(S("unit_done"), end_of("conv", 1))
                    sp.wait_ge(S("mT_turned"), 2)
                    sp.dma_start(iota, a["c_iota"]).then_inc(S("load_iota"), 16)
                    sp.dma_start(before, a["c_before"]).then_inc(S("load_before"), 16)
                if n == 3:
                    sp.dma_start(x, a["x"][0].rearrange("(t p) c -> p t c", p=P)).then_inc(S("load_x"), 16)
                    sp.dma_start(x_ctx, a["ctx"][0].rearrange("(t p) c -> p t c", p=P)).then_inc(S("load_ctx"), 16)
                    for name, v in list(zip(names, views))[:-1]:
                        sp.dma_start(v, a[name]).then_inc(S("load_" + name), 16)
                    sp.dma_start(wr[:, :, 0:NG], a["w_router_grp"][0].rearrange("(k p) g -> p k g", p=P)).then_inc(S("load_wrg"), 16)
                    sp.dma_start(wr[:, :, NG:36], a["w_router_exp"][0].rearrange("(k p) g -> p k g", p=P)).then_inc(S("load_wre"), 16)
                    sp.dma_start(br[:, 0:NG], a["b_router_grp"].broadcast_to([P, NG])).then_inc(S("load_brg"), 16)
                    sp.dma_start(br[:, NG:36], a["b_router_exp"].broadcast_to([P, NE])).then_inc(S("load_bre"), 16)

            def expert_units(r, e0, base, shift):
                for j, kind in enumerate(("gate", "gate", "up", "up", "down", "down")):
                    n = base + j
                    if shift is None:
                        wait = n - RING + 1
                    else:
                        wait = shift * 6 + (n - RING + 1)
                    sp.wait_ge(S("unit_done" + r), wait)
                    sp.dma_start(ring[:, n % RING], moe_src(kind, e0, j % 2)).then_inc(S("w_full%d%s" % (n % RING, r)), 16)
            with sp.Fori(0, NE) as e:
                expert_units("", e, n_before, e)
            sp.wait_ge(S("flag_set"), 1)
            more = sp.value_load(flag[0:1, 0:1], min_val=0, max_val=1)
            with sp.If(more > 0):
                sp.wait_ge(S("unit_done"), n_before + n_moe)
                for j, kind in enumerate(("gate", "gate", "up", "up", "down", "down")):
                    sp.dma_start(ring[:, j], moe_src(kind, 0, j % 2)).then_inc(S("w_full%d_b" % j), 16)
                with sp.Fori(1, NE) as e:
                    expert_units("_b", e, 0, e)
                sp.wait_ge(S("unit_done_b"), n_moe)

            for n in range(n_before + n_moe, len(units)):
                if n == first["a"]:
                    sp.wait_ge(S("unit_done"), n)
                    sp.dma_start(a_ws, a["a_w_s_2"][0].rearrange("g t s -> t g s")).then_inc(S("load_ws"), 16)
                    sp.dma_start(a_tri, a["c_tri"]).then_inc(S("load_tri"), 16)
                    sp.dma_start(a_bsr, a["a_b_s_2"][0]).then_inc(S("load_bs"), 16)
                unit(n, units[n])
                rows_for(n)
            sp.wait_ge(S("out_ready"), 1)
            sp.dma_start(out[0].rearrange("(t p) c -> p t c", p=P), x).then_inc(S("stored"), 16)
            sp.wait_ge(S("stored"), 16)

        @block.tensor
        def _(pe):
            def claim(key):
                p, k = plan[key]
                if k > 1:
                    pe.wait_ge(S("pair_free%d" % p), k - 1)
                return pair(p)

            def weights(n):
                pe.wait_ge(S("w_full%d" % (n % RING)), 16 * (n // RING + 1))
                return ring[:, n % RING]

            def gemm(name, t, key, lhs, nk=2, moving=NT):
                o = claim(key)
                for j in range(nk):
                    n = first[name] + nk * t + j
                    w = weights(n)
                    for tt in range(moving):
                        for c in range(UC):
                            mm = pe.matmul(o[:, tt, :], lhs(UC * j + c, tt), w[:, c, :],
                                           start=(j == 0 and c == 0), stop=(j == nk - 1 and c == UC - 1))
                    mm.then_inc(S("unit_done"), 1)

            def gemm_parts(name, t, key, hi, lo, nk=2):
                o = claim(key)
                for j in range(nk):
                    m = first[name] + nk * t + j - first["a"]
                    w = w_hi2[m % HI]
                    pe.wait_ge(S("w_hi_full"), m + 1)
                    for tt in range(NT):
                        for c in range(UC):
                            x_ = slice(P * tt, P * (tt + 1))
                            pe.matmul(o[:, tt, :], hi[:, UC * j + c, x_], w[:, c, :], start=(j == 0 and c == 0), stop=False)
                            pe.matmul(o[:, tt, :], lo[:, UC * j + c, x_], w[:, c, :], start=False, stop=False)
                    pe.wait_ge(S("w_lo_full"), m + 1)
                    for tt in range(NT):
                        for c in range(UC):
                            x_ = slice(P * tt, P * (tt + 1))
                            mm = pe.matmul(o[:, tt, :], hi[:, UC * j + c, x_], w_lo2[:, m % RING2, c, :],
                                           start=False, stop=(j == nk - 1 and c == UC - 1))
                    mm.then_inc(S("unit_done"), 1)

            def xt(k, tt):
                return XT[:, k, P * tt:P * (tt + 1)]

            def xt2(k, tt):
                return XT2[:, k, P * tt:P * (tt + 1)]

            def turn(key, src, sem, value=1):
                o = claim(key)
                for tt in range(NT):
                    for j in range(4):
                        mm = pe.transpose(o[:, tt, P * j:P * (j + 1)], src(tt, j), ident)
                mm.then_inc(S(sem), 1)

            pe.wait_ge(S("load_ident"), 16)
            pe.wait_ge(S("load_c"), 16)
            pe.wait_ge(S("load_cc"), 16)
            pe.wait_ge(S("load_taps"), 16)
            pe.wait_ge(S("load_tapb"), 16)
            o = claim("turn_rows")
            pe.transpose(o[:, 0, 0:16], rows16, ident[0:16, 0:16])
            for k in range(KC):
                mm = pe.transpose(o[:, 1, 32 * k:32 * (k + 1)], rows32[:, P * k:P * (k + 1)], ident[0:32, 0:32])
            mm.then_inc(S("rows_turned"), 1)
            pe.wait_ge(S("s_ready"), 2)
            for t in range(4):
                gemm("ada", t, ("ada", t), lambda k, m: (s_lat, s_ctx)[m][:, k, :])
            for s in range(2):
                pe.wait_ge(S("u_ready"), s + 1)
                src = (u_lat, u_ctx)[s]
                for c in range(2):
                    turn(("uT", s, c), lambda tt, j: src[:, tt, W * c + P * j:W * c + P * (j + 1)], "uT_turned")
            pair_evacuated(pe, ("uT", 0, 0))
            pair_evacuated(pe, ("uT", 0, 1))
            for t in range(3):
                gemm("glu", t, ("glu", t), xt)

            def turn_z(i):
                pe.wait_ge(S("z_ready"), i + 1)
                turn(("zT", i), lambda tt, j: z_tok[:, i, tt, P * j:P * (j + 1)], "zT_turned")
            turn_z(0)
            gemm("glu", 3, ("glu", 3), xt)
            pair_evacuated(pe, ("uT", 1, 0))
            pair_evacuated(pe, ("uT", 1, 1))

            def gemm_both(name, t):
                for s in range(2):
                    o = claim("%s_%s%d" % (name, ("lat", "ctx")[s], t))
                    for j in range(2):
                        n = first[name] + 2 * t + j
                        w = weights(n)
                        for tt in range(NT):
                            for c in range(UC):
                                mm = pe.matmul(o[:, tt, :], XT[:, 8 * s + UC * j + c, P * tt:P * (tt + 1)], w[:, c, :],
                                               start=(j == 0 and c == 0), stop=(j == 1 and c == UC - 1))
                        if s == 1:
                            mm.then_inc(S("unit_done"), 1)
                    if s == 0:
                        mm.then_inc(S("lat_done"), 1)

            def turn_roped(sem, t, key):
                pe.wait_ge(S(sem), t + 1)
                turn(key, lambda tt, j: roped[:, t, tt, P * j:P * (j + 1)], "heads_turned")

            gemm_both("k", 0)
            turn_z(1)
            gemm_both("k", 1)
            turn_roped("k_roped", 0, ("kT", 0))
            gemm_both("v", 0)
            turn_roped("k_roped", 1, ("kT", 1))
            for t in range(1, 4):
                gemm_both("v", t)
            for t in range(2):
                gemm("q", t, ("q", t), xt)
            for t in range(2):
                turn_roped("q_roped", t, ("qT", t))
            for i in range(4):
                o = claim(("S", i))
                for h in (2 * i, 2 * i + 1):
                    pe.wait_ge(S("k_decayed"), h + 1)
                    kd = tmp[:, h % 2, :].rearrange("p (t d n) -> p t d n", t=NT, d=2)
                    for d in range(2):
                        for tt in range(NT):
                            mm = pe.matmul(o[:, h % 2, DV * d:DV * (d + 1)], kd[:, tt, d, :],
                                           v_ctx[:, tt, DV * h:DV * (h + 1)], start=(tt == 0), stop=(tt == NT - 1))
                    mm.then_inc(S("state_done"), 1)
            pe.wait_ge(S("conv_done"), 1)
            for c in range(2):
                turn(("cz", c), lambda tt, j: conv[:, 4 * c + j, P * tt:P * (tt + 1)], "cz_turned")

            def ret_scores(i):
                o = claim(("sc", i))
                for h in (2 * i, 2 * i + 1):
                    for mt in range(NT):
                        mm = pe.matmul(o[:, h % 2, T * mt:T * (mt + 1)], kT[:, h, P * mt:P * (mt + 1)], qT[:, h, :],
                                       start=True, stop=True)
                mm.then_inc(S("ret_scored"), 1)

            def ret_values(i):
                o = claim(("av", i))
                for h in (2 * i, 2 * i + 1):
                    pe.wait_ge(S("ret_masked"), h + 1)
                    A = tmp[:, h % 2, :].rearrange("p (m n) -> p m n", m=NT)
                    Q = tmp[:, 4 + h % 2, :].rearrange("p (d n) -> p d n", d=2)
                    for nt in range(NT):
                        for mt in range(NT):
                            pe.matmul(o[:, h % 2, DV * nt:DV * (nt + 1)], A[:, mt, P * nt:P * (nt + 1)],
                                      v_lat[:, mt, DV * h:DV * (h + 1)], start=(mt == 0), stop=False)
                        for d in range(2):
                            mm = pe.matmul(o[:, h % 2, DV * nt:DV * (nt + 1)], Q[:, d, P * nt:P * (nt + 1)],
                                           state[:, h, d, :], start=False, stop=(d == 1))
                    mm.then_inc(S("ret_summed"), 1)

            for i in range(4):
                pair_evacuated(pe, ("S", i))
            pair_evacuated(pe, ("kT", 0))
            pair_evacuated(pe, ("kT", 1))
            pair_evacuated(pe, ("qT", 0))
            pair_evacuated(pe, ("qT", 1))
            ret_scores(0)
            for i in range(4):
                gemm("g", i, ("g", i), xt)
                ret_values(i)
                if i < 3:
                    ret_scores(i + 1)
            for t in range(4):
                gemm("gate", t, ("gate", t), xt)
            pe.wait_ge(S("s_ready"), 3)
            for t in range(8):
                gemm("ada_tail", t, ("ada_tail", t), lambda k, m: kT[:, 0:4, :].rearrange("p a b -> p (a b)")[:, P * k:P * (k + 1)], moving=1)
            pe.wait_ge(S("ret_ready"), 2)
            for c in range(4):
                turn(("retT", c), lambda tt, j: sg[:, tt, W * c + P * j:W * c + P * (j + 1)], "retT_turned")
            pe.wait_ge(S("cz_ready"), 1)
            for c in range(2):
                turn(("cvT", c), lambda tt, j: cz[:, tt, W * c + P * j:W * c + P * (j + 1)], "cvT_turned")
            for c in range(4):
                pair_evacuated(pe, ("retT", c))
            for t in range(2):
                gemm("ret", t, ("ret", t), xt, nk=4)
            for c in range(2):
                pair_evacuated(pe, ("cvT", c))
            for t in range(2):
                gemm("conv", t, ("conv", t), xt2)
            pe.wait_ge(S("merged"), 1)
            for c in range(2):
                turn(("mT", c), lambda tt, j: cz[:, tt, W * c + P * j:W * c + P * (j + 1)], "mT_turned")
            for c in range(2):
                pair_evacuated(pe, ("mT", c))
            for t in range(2):
                gemm("mix", t, ("mix", t), xt)
            pe.wait_ge(S("h_ready"), 1)
            for c in range(2):
                turn(("eT", c), lambda tt, j: h_tok[:, tt, W * c + P * j:W * c + P * (j + 1)], "eT_turned")
            for c in range(2):
                pair_evacuated(pe, ("eT", c))
            pe.wait_ge(S("load_wrg"), 16)
            pe.wait_ge(S("load_wre"), 16)
            o = claim("router")
            for tt in range(NT):
                for k in range(KC):
                    mm = pe.matmul(o[:, tt, 0:36], xt2(k, tt), wr[:, k, :], start=(k == 0), stop=(k == KC - 1))
            mm.then_inc(S("routed"), 1)

            pe.wait_ge(S("load_before"), 16)
            pe.wait_ge(S("hits_ready"), 1)
            o = claim(("rank", 0))
            pe.matmul(o[:, 0, 0:NE], before, hits[:, 0, :], start=True, stop=True)
            pe.matmul(o[:, 1, 0:NE], ones, hits[:, 0, :], start=True, stop=False)
            pe.matmul(o[:, 1, 0:NE], before, hits[:, 1, :], start=False, stop=True).then_inc(S("ranked"), 1)
            pe.wait_ge(S("most_ready"), 1)
            pe.transpose(ps[0:1, 2 * plan["most"][0], 0:P], most[:, 0:1], ident).then_inc(S("most_turned"), 1)

            y = [claim("moe_y0"), claim("moe_y1")]

            def wide_product(bank, lhs_hi, lhs_lo, n, base, e, r, begin, end):
                pe.wait_ge(S("hi_ready"), (e + OFF[r]) * 6 + (n + 1))
                for c in range(UC):
                    pe.matmul(ps[:, bank, :], lhs_hi(c), w_hi[:, n % HI, c, :], start=(begin and c == 0), stop=False)
                for c in range(UC):
                    pe.matmul(ps[:, bank, :], lhs_lo(c), w_hi[:, n % HI, c, :], start=False, stop=False)
                if n in POOL_UNITS:
                    pe.wait_ge(S("pool_lo"), (e + OFF[r]) * len(POOL_UNITS) + (POOL_UNITS.index(n) + 1))
                else:
                    pe.wait_ge(S("dve_lo"), (e + OFF[r]) * len(DVE_UNITS) + (DVE_UNITS.index(n) + 1))
                for c in range(UC):
                    mm = pe.matmul(ps[:, bank, :], lhs_hi(c), w_lo[:, (base + n) % RING, c, :], start=False, stop=(end and c == UC - 1))
                mm.then_inc(S("unit_done" + r), 1)

            def xe_part(part, j):
                return lambda c: part[:, UC * j + c, :]

            def gather(half, e, r):
                for k in range(4):
                    for tt in range(NT):
                        mm = pe.matmul(ps[:, (2, 0)[half], P * k:P * (k + 1)],
                                       h_tok[:, tt, P * (4 * half + k):P * (4 * half + k + 1)], sel[:, tt, :],
                                       start=(tt == 0), stop=(tt == NT - 1))
                mm.then_inc(S("gathered%d" % half), 1)

            def turn_selection(r):
                for tt in range(NT):
                    mm = pe.transpose(ps[:, 3, P * tt:P * (tt + 1)], selw[:, tt, :], ident)
                mm.then_inc(S("sel_turned"), 1)

            def scatter(begin, r):
                for tt in range(NT):
                    for j in range(2):
                        pe.matmul(y[tt][:, j, :], selT[:, P * tt:P * (tt + 1)], ye_hi[:, W * j:W * (j + 1)],
                                  start=begin, stop=False, skip_group_check=True)
                        mm = pe.matmul(y[tt][:, j, :], selT[:, P * tt:P * (tt + 1)], ye_lo[:, W * j:W * (j + 1)],
                                       start=False, stop=False, skip_group_check=True)
                mm.then_inc(S("scattered"), 1)

            def expert(e, base, r, head, tail, begin):
                pe.wait_ge(S("xe0"), (e + OFF[r]) + 1)
                pe.wait_ge(S("xe1"), (e + OFF[r]) + 1)
                for j in range(2):
                    wide_product(0, xe_part(xe_hi, j), xe_part(xe_lo, j), j, base, e, r, j == 0, j == 1)
                if not head:
                    pe.wait_ge(S("ye_hi"), (e + OFF[r]) * 2)
                    pe.wait_ge(S("ye_lo"), (e + OFF[r]) * 2)
                    pe.wait_ge(S("selT"), (e + OFF[r]))
                    scatter(begin, r)
                for j in range(2):
                    wide_product(1, xe_part(xe_hi, j), xe_part(xe_lo, j), 2 + j, base, e, r, j == 0, j == 1)
                if not tail:
                    pe.wait_ge(S("sel_ready"), (e + OFF[r]) + 2)
                    gather(0, e, r)
                pe.wait_ge(S("selT"), (e + OFF[r]) + 1)
                pe.wait_ge(S("slot_weight"), (e + OFF[r]) + 1)
                pe.wait_ge(S("act_ready"), (e + OFF[r]) + 1)
                for j in range(FF // P):
                    mm = pe.transpose(ps[:, 3, P * j:P * (j + 1)], he[:, P * j:P * (j + 1)], ident)
                mm.then_inc(S("h_turned"), 1)
                if not tail:
                    pe.wait_ge(S("silu"), (e + OFF[r]) + 1)
                    gather(1, e, r)
                pe.wait_ge(S("hT_lo"), (e + OFF[r]) + 1)
                wide_product(1, lambda c: heT_hi[:, c, :], lambda c: heT_lo[:, c, :], 4, base, e, r, True, True)
                if not tail:
                    pe.wait_ge(S("xe0"), (e + OFF[r]) + 2)
                wide_product(2, lambda c: heT_hi[:, c, :], lambda c: heT_lo[:, c, :], 5, base, e, r, True, True)
                if not tail:
                    pe.wait_ge(S("selw_ready"), (e + OFF[r]) + 2)
                    turn_selection(r)

            def experts(base, r, first_round):
                pe.wait_ge(S("sel_ready"), 1 + OFF[r])
                gather(0, 0, r)
                gather(1, 0, r)
                pe.wait_ge(S("selw_ready"), 1 + OFF[r])
                turn_selection(r)
                expert(0, base, r, True, False, False)
                expert(1, base, r, False, False, first_round)
                with pe.Fori(2, NE - 1) as e:
                    expert(e, base, r, False, False, False)
                expert(NE - 1, base, r, False, True, False)
                pe.wait_ge(S("ye_hi"), 2 * (NE + OFF[r]))
                pe.wait_ge(S("ye_lo"), 2 * (NE + OFF[r]))
                pe.wait_ge(S("selT"), (NE + OFF[r]))
                scatter(False, r)

            pe.wait_ge(S("flag_set"), 1)
            pe.wait_ge(S("pair_free0"), entry0)
            pe.wait_ge(S("pair_free1"), entry1)
            experts(n_before, "", True)
            more = pe.value_load(flag[0:1, 0:1], min_val=0, max_val=1)
            with pe.If(more > 0):
                experts(0, "_b", False)

            pe.wait_ge(S("a_in_ready"), 1)
            for c in range(2):
                turn(("aT", c), lambda tt, j: h_tok[:, tt, W * c + P * j:W * c + P * (j + 1)], "aT_turned")
            for c in range(2):
                pair_evacuated(pe, ("aT", c))
            for t in range(8):
                gemm_parts("a", t, ("a", t), xt2_hi, xt2_lo)
            pe.wait_ge(S("load_ws"), 16)
            pe.wait_ge(S("load_bs"), 16)
            for c in range(2):
                o = claim(("wsT", c))
                for j in range(4):
                    mm = pe.transpose(o[:, 0, P * j:P * (j + 1)], a_ws[:, 4 * c + j, :], ident)
                if c == 1:
                    mm = pe.transpose(o[:, 1, 0:KC], a_bsr, ident[0:KC, 0:KC])
                mm.then_inc(S("wsT_turned"), 1)
            pe.wait_ge(S("wsT_ready"), 2)
            pe.wait_ge(S("v_normed"), 1)
            for i in range(4):
                o = claim(("sv", i))
                for tt in range(NT):
                    for g in (2 * i, 2 * i + 1):
                        mm = pe.matmul(o[:, tt, 256 * (g % 2):256 * (g % 2 + 1)], a_wsT[:, g, :],
                                       a_v[:, tt, 256 * g:256 * (g + 1)], start=True, stop=True)
                mm.then_inc(S("sv_done"), 1)
            for t in range(8, 12):
                gemm_parts("a", t, ("a", t), xt2_hi, xt2_lo)
            for c in range(4):
                pe.wait_ge(S("y_gated"), c + 1)
                turn(("yT", c), lambda tt, j: a_z[:, tt, W * c + P * j:W * c + P * (j + 1)], "yT_turned")
            for c in range(4):
                pair_evacuated(pe, ("yT", c))
            for t in range(2):
                gemm_parts("a_out", t, ("a_out", t), yt_hi, yt_lo, nk=4)

            pe.wait_ge(S("b_in_ready"), 1)
            for c in range(2):
                turn(("bT", c), lambda tt, j: y2[:, tt, W * c + P * j:W * c + P * (j + 1)], "bT_turned")
            for c in range(2):
                pair_evacuated(pe, ("bT", c))
            n_rope = 0
            for t in range(20):
                gemm_parts("b", t, ("b", t), xt2_hi, xt2_lo)
                if t and BKIND[t - 1] in "qk":
                    n_rope += 1
                    pe.wait_ge(S("b_roped"), n_rope)
                    turn(("bqk", t - 1), lambda tt, j: b_rope[:, (n_rope - 1) % 2, tt, P * j:P * (j + 1)], "b_turned")
                for act, g, c in slots[t]:
                    if act == "scores":
                        if c == 0:
                            for key in [("bqk", tq) for tq in range(20) if BKIND[tq] in "qk" and BGROUP[tq] == g]:
                                pair_evacuated(pe, key)
                        for i in range(2):
                            o = claim((act, g, c, i))
                            for hh in range(2):
                                h = 4 * c + 2 * i + hh
                                r = slice(HD * (h % 2), HD * (h % 2) + HD)
                                for tt in range(NT):
                                    n = P * (tt + 1)
                                    mm = pe.matmul(o[:, hh, P * tt:P * tt + n], b_qT[r, g % 2, h // 2, P * tt:P * (tt + 1)],
                                                   b_kT[r, g % 2, h // 2, 0:n], start=True, stop=True)
                            mm.then_inc(S("b_scored"), 1)
                    elif act == "turn":
                        pe.wait_ge(S("b_probs"), 4 * (4 * g + c) + 4)
                        for i in range(2):
                            o = claim((act, g, c, i))
                            for hh in range(2):
                                for s in range(3):
                                    mm = pe.transpose(o[:, hh, P * s:P * (s + 1)], b_p[:, 2 * i + hh, P * s:P * (s + 1)], ident)
                            mm.then_inc(S("b_p_turned"), 1)
                    else:
                        for i in range(2):
                            pair_evacuated(pe, ("turn", g, c, i))
                        if c == 0:
                            for tv in range(20):
                                if BKIND[tv] == "v" and BGROUP[tv] == g:
                                    pair_evacuated(pe, ("b", tv))
                        o = claim((act, g, c))
                        for hh in range(4):
                            h = 4 * c + hh
                            pT = b_pT[:, c % 2, hh, :]
                            cols = slice(HD * h, HD * (h + 1))
                            pe.matmul(o[:, 0, HD * hh:HD * (hh + 1)], pT[:, 0:P], b_v[:, 0, cols], start=True, stop=True)
                            pe.matmul(o[:, 1, HD * hh:HD * (hh + 1)], pT[:, P:2 * P], b_v[:, 0, cols], start=True, stop=False)
                            mm = pe.matmul(o[:, 1, HD * hh:HD * (hh + 1)], pT[:, 2 * P:3 * P], b_v[:, 1, cols], start=False, stop=True)
                        mm.then_inc(S("b_valued"), 1)
            pe.wait_ge(S("b_o_ready"), 1)
            for c in range(2):
                turn(("oT", c), lambda tt, j: b_z[:, tt, W * c + P * j:W * c + P * (j + 1)], "oT_turned")
            for c in range(2):
                pair_evacuated(pe, ("oT", c))
            for t in range(2):
                gemm_parts("b_out", t, ("b_out", t), ot_hi, ot_lo)

        @block.vector
        def _(dve):
            chain = [0]

            def link(ins):
                chain[0] += 1
                ins.then_inc(S("dve_step"), 1)

            def settle():
                dve.wait_ge(S("dve_step"), chain[0])

            def row_done(key=None):
                if key is None:
                    settle()
                else:
                    pair_evacuated(dve, key)
                dve.sem_inc(S("row_used"), 1)

            def free_pair(key):
                dve.sem_inc(S("pair_free%d" % plan[key][0]), 1)

            norms = [0]

            def power(eps):
                norms[0] += 1
                return norms[0]

            def row_stats(src, width):
                n = width // W
                for tt in range(NT):
                    for c in range(n):
                        link(dve.bn_stats(stats[:, tt, c, :], src(tt)[:, W * c:W * (c + 1)]))
                settle()
                for tt in range(NT):
                    ins = dve.bn_aggr(mv[:, tt, :], stats[:, tt, 0:n, :])
                    if tt == 1:
                        norms[0] += 1
                        ins.then_inc(S("stats_ready"), 1)
                    else:
                        link(ins)
                dve.wait_ge(S("rstd_ready"), norms[0])
                settle()

            def apply_norm(dst, src):
                for tt in range(NT):
                    link(dve.tensor_scalar(dst(tt), src(tt), mv[:, tt, 0:1], rstd[:, tt:tt + 1], ALU.subtract, ALU.mult))
                settle()

            def gain_bias(buf2, g, b, c):
                v = buf2[:, :, W * c:W * (c + 1)]
                link(dve.tensor_tensor(v, v, bc2(row_ready(dve, (g, c))), ALU.mult))
                settle()
                row_done()
                link(dve.tensor_tensor(v, v, bc2(row_ready(dve, (b, c))), ALU.add))
                settle()
                row_done()

            def rms(src, dst, g, rows_key):
                for tt in range(NT):
                    for c in range(2):
                        link(dve.bn_stats(stats[:, tt, c, :], src[:, tt, W * c:W * (c + 1)]))
                settle()
                for tt in range(NT):
                    link(dve.bn_aggr(mv[:, tt, :], stats[:, tt, 0:2, :]))
                settle()
                link(dve.tensor_tensor(sq, mv[:, :, 0], mv[:, :, 0], ALU.mult))
                settle()
                norms[0] += 1
                dve.tensor_tensor(mv[:, :, 1], sq, mv[:, :, 1], ALU.add).then_inc(S("stats_ready"), 1)
                dve.wait_ge(S("rstd_ready"), norms[0])
                for tt in range(NT):
                    link(dve.tensor_scalar(dst[:, tt, :], src[:, tt, :], rstd[:, tt:tt + 1], None, ALU.mult))
                settle()
                for c in range(2):
                    v = dst[:, :, W * c:W * (c + 1)]
                    link(dve.tensor_tensor(v, v, bc2(row_ready(dve, (rows_key, c))), ALU.mult))
                    settle()
                    row_done()

            def biased(key, dst, wait_name, wait_value, free=True):
                dve.wait_ge(S(wait_name), wait_value)
                return dve.tensor_tensor(dst, buf(key), bc2(row_ready(dve, key)), ALU.add)

            dve.wait_ge(S("silu_c"), 1)
            dve.tensor_copy(s_lat, sT[:, 0:KC].unsqueeze(2).broadcast_to([P, KC, P])).then_inc(S("s_ready"), 1)
            dve.tensor_copy(s_ctx, sT[:, KC:2 * KC].unsqueeze(2).broadcast_to([P, KC, P])).then_inc(S("s_ready"), 1)
            dve.wait_ge(S("load_df"), 16)
            dve.wait_ge(S("load_db"), 16)
            link(dve.tensor_scalar(la[:, 0, :], lg, -1.0, None, ALU.mult))
            settle()
            dve.tensor_tensor(la[:, 0, :], la[:, 0, :], lg, ALU.min).then_inc(S("neg_abs"), 1)
            dve.wait_ge(S("exp_abs"), 1)
            link(dve.tensor_scalar(la[:, 1, :], la[:, 0, :], 2.0, None, ALU.add))
            settle()
            link(dve.reciprocal(la[:, 1, :], la[:, 1, :]))
            settle()
            link(dve.tensor_tensor(la[:, 0, :], la[:, 0, :], la[:, 1, :], ALU.mult))
            settle()
            link(dve.tensor_tensor(la[:, 1, :], la[:, 0, :], la[:, 0, :], ALU.mult))
            settle()
            link(dve.tensor_scalar(la[:, 2, :], la[:, 1, :], 2.0 / 17, 2.0 / 15, ALU.mult, ALU.add))
            settle()
            for n in (13, 11, 9, 7, 5, 3, 1):
                link(dve.tensor_tensor(la[:, 2, :], la[:, 2, :], la[:, 1, :], ALU.mult))
                settle()
                link(dve.tensor_scalar(la[:, 2, :], la[:, 2, :], 2.0 / n, None, ALU.add))
                settle()
            link(dve.tensor_tensor(la[:, 2, :], la[:, 2, :], la[:, 0, :], ALU.mult))
            link(dve.tensor_scalar(lg, lg, 0.0, None, ALU.min))
            settle()
            link(dve.tensor_tensor(lg, lg, la[:, 2, :], ALU.subtract))
            settle()
            dve.wait_ge(S("load_pos"), 16)
            for d in range(2):
                for tt in range(NT):
                    ins = dve.tensor_scalar(wdec[:, d, tt, :], lg[:, H * d:H * (d + 1)], pos[:, d, tt:tt + 1], None, ALU.mult)
                    if d == 1 and tt == 1:
                        ins.then_inc(S("wdec_exps"), 1)
                    else:
                        link(ins)

            for t in range(4):
                row = row_ready(dve, ("ada", t))
                dve.wait_ge(S("unit_done"), end_of("ada", t))
                p_ = buf(("ada", t))
                for m, dst in enumerate((mod_lat, mod_ctx)):
                    if t < 2:
                        ins = dve.tensor_tensor(dst[:, W * t:W * (t + 1)], p_[:, m, :], row, ALU.add)
                    else:
                        ins = dve.scalar_tensor_tensor(dst[:, W * t:W * (t + 1)], p_[:, m, :], 1.0, row, ALU.add, ALU.add)
                    if m == 0:
                        link(ins)
                    else:
                        freed(ins, ("ada", t))
                row_done(("ada", t))
            pair_evacuated(dve, ("ada", 2))
            pair_evacuated(dve, ("ada", 3))
            settle()
            for s, (src, dst, m) in enumerate(((x, u_lat, mod_lat), (x_ctx, u_ctx, mod_ctx))):
                dve.wait_ge(S(("load_x", "load_ctx")[s]), 16)
                link(dve.tensor_tensor(dst, src, m[:, D:2 * D].unsqueeze(1).broadcast_to([P, NT, D]), ALU.mult))
                settle()
                dve.tensor_tensor(dst, dst, m[:, 0:D].unsqueeze(1).broadcast_to([P, NT, D]), ALU.add).then_inc(S("u_ready"), 1)

            link(dve.memset(z_pad[:, :, 0:PAD], 0.0))
            link(dve.memset(z_pad[:, :, PAD + T:T + 2 * PAD], 0.0))
            dve.wait_ge(S("wdec_exp"), 1)
            link(dve.tensor_scalar(wdec, wdec, DK ** -0.5, None, ALU.mult))

            for i in range(2):
                ins = biased(("glu", 2 * i), z_tok[:, i], "unit_done", end_of("glu", 2 * i))
                freed(ins, ("glu", 2 * i))
                row_done(("glu", 2 * i))
                ins = biased(("glu", 2 * i + 1), tmp[:, 2 * i:2 * i + 2, :], "unit_done", end_of("glu", 2 * i + 1))
                freed(ins, ("glu", 2 * i + 1))
                row_done(("glu", 2 * i + 1))
                dve.wait_ge(S("sig_z"), i + 1)
                pair_evacuated(dve, ("glu", 2 * i))
                dve.tensor_tensor(z_tok[:, i], z_tok[:, i], tmp[:, 2 * i:2 * i + 2, :], ALU.mult).then_inc(S("z_ready"), 1)

            taps_done = [0]

            def conv_taps(n):
                for _ in range(n):
                    j = taps_done[0]
                    if j == 0:
                        dve.wait_ge(S("pair_free%d" % plan[("zT", 0)][0]), plan[("zT", 0)][1])
                        dve.wait_ge(S("pair_free%d" % plan[("zT", 1)][0]), plan[("zT", 1)][1])
                        pair_evacuated(dve, "turn_rows")
                    settle()
                    for k in range(KC):
                        z = z_pad[:, k, j:j + T]
                        if j == 0:
                            link(dve.tensor_scalar(conv[:, k, :], z, cwT[:, k, 0:1], cwT[:, k, TAPS:TAPS + 1], ALU.mult, ALU.add))
                        elif j < TAPS - 1 or k < KC - 1:
                            link(dve.scalar_tensor_tensor(conv[:, k, :], z, cwT[:, k, j:j + 1], conv[:, k, :], ALU.mult, ALU.add))
                        else:
                            dve.scalar_tensor_tensor(conv[:, k, :], z, cwT[:, k, j:j + 1], conv[:, k, :], ALU.mult, ALU.add).then_inc(S("conv_done"), 1)
                    taps_done[0] += 1

            def rope_four(t, ready):
                for tt in range(NT):
                    s = tmp[:, tt, :].rearrange("p (h s d) -> p h s d", h=4, s=2)
                    r = roped[:, t, tt, :].rearrange("p (h s d) -> p h s d", h=4, s=2)
                    q = tmp[:, 2 + tt, :].rearrange("p (h s d) -> p h s d", h=4, s=2)
                    cos = rope1[:, 0, tt, :].unsqueeze(1).broadcast_to([P, 4, P])
                    link(dve.tensor_tensor(roped[:, t, tt, :].rearrange("p (h d) -> p h d", h=4),
                                           tmp[:, tt, :].rearrange("p (h d) -> p h d", h=4), cos, ALU.mult))
                    for s_ in range(2):
                        sin = rope1[:, 1, tt, 64 * s_:64 * (s_ + 1)].unsqueeze(1).broadcast_to([P, 4, 64])
                        link(dve.tensor_tensor(q[:, :, s_, :], s[:, :, 1 - s_, :], sin, ALU.mult))
                settle()
                for tt in range(NT):
                    ins = dve.tensor_tensor(roped[:, t, tt, :], roped[:, t, tt, :], tmp[:, 2 + tt, :], ALU.add)
                    if tt == 1:
                        ins.then_inc(S(ready), 1)
                    else:
                        link(ins)

            dve.wait_ge(S("load_c_rope1"), 16)
            for t in range(2):
                row = row_ready(dve, ("k", t))
                dve.wait_ge(S("lat_done"), t + 1)
                freed(dve.tensor_tensor(tmp[:, 0:2, :], buf("k_lat%d" % t), bc2(row), ALU.add), "k_lat%d" % t)
                pair_evacuated(dve, "k_lat%d" % t)
                rope_four(t, "k_roped")
                if t == 1:
                    conv_taps(4)
                dve.wait_ge(S("unit_done"), end_of("k", t))
                freed(dve.tensor_tensor(k_ctx[:, :, W * t:W * (t + 1)], buf("k_ctx%d" % t), bc2(row), ALU.add), "k_ctx%d" % t)
                row_done("k_ctx%d" % t)
            for t in range(4):
                row = row_ready(dve, ("v", t))
                dve.wait_ge(S("lat_done"), t + 3)
                freed(dve.tensor_tensor(v_lat[:, :, W * t:W * (t + 1)], buf("v_lat%d" % t), bc2(row), ALU.add), "v_lat%d" % t)
                conv_taps(4)
                dve.wait_ge(S("unit_done"), end_of("v", t))
                freed(dve.tensor_tensor(v_ctx[:, :, W * t:W * (t + 1)], buf("v_ctx%d" % t), bc2(row), ALU.add), "v_ctx%d" % t)
                row_done("v_ctx%d" % t)
                conv_taps(3 if t < 3 else 2)
            assert taps_done[0] == TAPS, taps_done
            for t in range(2):
                if t == 0:
                    dve.wait_ge(S("heads_turned"), 2)
                ins = biased(("q", t), tmp[:, 0:2, :], "unit_done", end_of("q", t))
                freed(ins, ("q", t))
                pair_evacuated(dve, ("q", t))
                row_done(("q", t))
                rope_four(t, "q_roped")
            pair_evacuated(dve, "k_ctx0")
            pair_evacuated(dve, "k_ctx1")
            for h in range(H):
                if h >= 2:
                    dve.wait_ge(S("state_done"), h - 1)
                kd = tmp[:, h % 2, :].rearrange("p (t d n) -> p t d n", t=NT, d=2)
                for tt in range(NT):
                    for d in range(2):
                        ins = dve.tensor_scalar(kd[:, tt, d, :], k_ctx[:, tt, DK * h:DK * (h + 1)], wdec[:, d, tt, h:h + 1], None, ALU.mult)
                        if tt == 1 and d == 1:
                            ins.then_inc(S("k_decayed"), 1)
                        else:
                            link(ins)

            def decay_exponents(h):
                E = tmp[:, 2 + h % 2, :]
                link(dve.scalar_tensor_tensor(E, dist_f.rearrange("p a b -> p (a b)"), lg[:, h:h + 1], log_c.rearrange("p a b -> p (a b)"), ALU.mult, ALU.add))
                settle()
                dve.scalar_tensor_tensor(E, dist_b.rearrange("p a b -> p (a b)"), lg[:, H + h:H + h + 1], E, ALU.mult, ALU.add).then_inc(S("ret_exps"), 1)

            def mask_scores(i):
                dve.wait_ge(S("ret_scored"), i + 1)
                for h in (2 * i, 2 * i + 1):
                    dve.wait_ge(S("ret_exped"), h + 1)
                    if h >= 2:
                        dve.wait_ge(S("ret_summed"), h - 1)
                    Q = tmp[:, 4 + h % 2, :].rearrange("p (d n) -> p d n", d=2)
                    link(dve.tensor_tensor(Q, Q, qT[:, h:h + 1, :].broadcast_to([P, 2, T]), ALU.mult))
                    settle()
                    dve.tensor_tensor(tmp[:, h % 2, :], buf(("sc", i))[:, h % 2, :], tmp[:, 2 + h % 2, :], ALU.mult).then_inc(S("ret_masked"), 1)
                dve.wait_ge(S("ret_masked"), 2 * i + 2)
                free_pair(("sc", i))

            def head_norm(i):
                o = buf(("av", i))
                for h in (2 * i, 2 * i + 1):
                    dve.wait_ge(S("ret_summed"), h + 1)
                    for tt in range(NT):
                        link(dve.bn_stats(stats[:, tt, 0, :], o[:, h % 2, DV * tt:DV * (tt + 1)]))
                    settle()
                    for tt in range(NT):
                        ins = dve.bn_aggr(mv[:, tt, :], stats[:, tt, 0:1, :])
                        if tt == 0:
                            link(ins)
                        else:
                            norms[0] += 1
                            ins.then_inc(S("stats_ready"), 1)
                    dve.wait_ge(S("rstd_ready"), norms[0])
                    settle()
                    dst = (o_lo, o_hi)[h // 4]
                    for tt in range(NT):
                        link(dve.tensor_scalar(dst[:, tt, DV * (h % 4):DV * (h % 4 + 1)], o[:, h % 2, DV * tt:DV * (tt + 1)],
                                               mv[:, tt, 0:1], rstd[:, tt:tt + 1], ALU.subtract, ALU.mult))
                settle()
                free_pair(("av", i))

            dve.wait_ge(S("state_done"), H)
            for name in ("load_c_dist_f", "load_c_dist_b", "load_c_log"):
                dve.wait_ge(S(name), 16)
            pair_evacuated(dve, ("qT", 0))
            pair_evacuated(dve, ("qT", 1))
            decay_exponents(0)
            decay_exponents(1)
            for i in range(4):
                mask_scores(i)
                if i < 3:
                    decay_exponents(2 * i + 2)
                    decay_exponents(2 * i + 3)
                ins = biased(("g", i), sg[:, :, W * i:W * (i + 1)], "unit_done", end_of("g", i))
                freed(ins, ("g", i))
                row_done(("g", i))
                head_norm(i)

            dve.wait_ge(S("silu_g"), 4)
            for half, src in ((0, o_lo), (1, o_hi)):
                v = sg[:, :, D * half:D * (half + 1)]
                dve.tensor_tensor(v, v, src, ALU.mult).then_inc(S("ret_ready"), 1)
            dve.tensor_copy(kT[:, 0:4, :].rearrange("p a b -> p (a b)").rearrange("p (k n) -> p k n", k=KC),
                            sT[:, 0:KC].unsqueeze(2).broadcast_to([P, KC, P])).then_inc(S("s_ready"), 1)
            pair_evacuated(dve, ("cz", 0))
            pair_evacuated(dve, ("cz", 1))
            row_stats(lambda tt: cz[:, tt, :], D)
            apply_norm(lambda tt: cz[:, tt, :], lambda tt: cz[:, tt, :])
            for c in range(2):
                gain_bias(cz, "conv_g", "conv_b", c)
            dve.sem_inc(S("cz_normed"), 1)
            for t in range(4):
                ins = biased(("gate", t), gates[:, :, W * t:W * (t + 1)], "unit_done", end_of("gate", t))
                freed(ins, ("gate", t))
                row_done(("gate", t))
            for t in range(8):
                row = row_ready(dve, ("ada_tail", t))
                dve.wait_ge(S("unit_done"), end_of("ada_tail", t))
                src = buf(("ada_tail", t))[:, 0, :]
                dst = mod_tail[:, W * t:W * (t + 1)]
                if t in (4, 5):
                    freed(dve.scalar_tensor_tensor(dst, src, 1.0, row, ALU.add, ALU.add), ("ada_tail", t))
                else:
                    freed(dve.tensor_tensor(dst, src, row, ALU.add), ("ada_tail", t))
                row_done(("ada_tail", t))
            dve.wait_ge(S("sig_gates"), 4)
            for t in range(2):
                dve.wait_ge(S("unit_done"), end_of("ret", t, 4))
                v = gates[:, :, W * t:W * (t + 1)]
                freed(dve.tensor_tensor(v, v, buf(("ret", t)), ALU.mult), ("ret", t))
            for t in range(2):
                dve.wait_ge(S("cvT_turned"), 2)
                v = cz[:, :, W * t:W * (t + 1)]
                freed(biased(("conv", t), v, "unit_done", end_of("conv", t)), ("conv", t))
                pair_evacuated(dve, ("conv", t))
                row_done(("conv", t))
                link(dve.tensor_tensor(v, v, gates[:, :, D + W * t:D + W * (t + 1)], ALU.mult))
                settle()
                pair_evacuated(dve, ("ret", t))
                ins = dve.tensor_tensor(v, v, gates[:, :, W * t:W * (t + 1)], ALU.add)
                if t == 1:
                    ins.then_inc(S("merged"), 1)
                else:
                    link(ins)
            pair_evacuated(dve, ("ada_tail", 7))
            gt = mod_tail

            def residual_ln(t, gate_row):
                v = h_tok[:, :, W * t:W * (t + 1)]
                link(dve.tensor_tensor(v, v, bc2(gate_row), ALU.mult))
                settle()
                xv = x[:, :, W * t:W * (t + 1)]
                link(dve.scalar_tensor_tensor(xv, xv, ALPHA, v, ALU.mult, ALU.add))
                settle()

            for t in range(2):
                v = h_tok[:, :, W * t:W * (t + 1)]
                freed(biased(("mix", t), v, "unit_done", end_of("mix", t)), ("mix", t))
                pair_evacuated(dve, ("mix", t))
                row_done(("mix", t))
                residual_ln(t, gt[:, W * t:W * (t + 1)])
            row_stats(lambda tt: x[:, tt, :], D)
            apply_norm(lambda tt: x[:, tt, :], lambda tt: x[:, tt, :])
            for c in range(2):
                gain_bias(x, "ln1_g", "ln1_b", c)
            link(dve.tensor_tensor(h_tok, x, gt[:, 2 * D:3 * D].unsqueeze(1).broadcast_to([P, NT, D]), ALU.mult))
            settle()
            dve.tensor_tensor(h_tok, h_tok, gt[:, D:2 * D].unsqueeze(1).broadcast_to([P, NT, D]), ALU.add).then_inc(S("h_ready"), 1)

            dve.wait_ge(S("load_brg"), 16)
            dve.wait_ge(S("load_bre"), 16)
            dve.wait_ge(S("load_c_rows"), 16)
            dve.wait_ge(S("routed"), 1)
            freed(dve.tensor_tensor(lgt, buf("router")[:, :, 0:36], br.unsqueeze(1).broadcast_to([P, NT, 36]), ALU.add), "router")
            pair_evacuated(dve, "router")
            oo = [o_rt]

            def rb(*shape):
                v, _ = carve(*shape, on=oo[0])
                oo[0] += int(np.prod(shape))
                return v
            g_max, g_e, g_sum, g_hit, g_first = rb(NT), rb(NT, NG), rb(NT), rb(NT, NG), rb(NT)
            pick, l8, m1, hit1, hit2, m2, e2, wsum, w1, w2 = rb(NT, NG, NEG), rb(NT, NEG), rb(NT), rb(NT, NEG), rb(NT, NEG), rb(NT), rb(NT), rb(NT), rb(NT), rb(NT)
            l8b, c8, m8 = rb(NT, NEG), rb(NT, NEG), rb(NT, NEG)
            rank = rb(NEG)

            def one(ins):
                link(ins)
                settle()

            def wide(v, n):
                return v.unsqueeze(2).broadcast_to([P, NT, n])

            one(dve.tensor_scalar(rank, row_fb[:, 1, 0:NEG], -(T - NEG - 1.0), None, ALU.add))

            def first_max(hit, src, mx, n):
                one(dve.tensor_reduce(mx, src, AX_X, ALU.max))
                one(dve.tensor_tensor(hit, src, wide(mx, n), ALU.is_equal))
                one(dve.tensor_tensor(hit, hit, rank[:, 0:n].unsqueeze(1).broadcast_to([P, NT, n]), ALU.mult))
                one(dve.tensor_reduce(g_first, hit, AX_X, ALU.max))
                one(dve.tensor_tensor(hit, hit, wide(g_first, n), ALU.is_equal))

            gl = lgt[:, :, 0:NG]
            first_max(g_hit, gl, g_max, NG)
            dve.tensor_tensor(g_e, gl, wide(g_max, NG), ALU.subtract).then_inc(S("router_exp"), 1)
            el = lgt[:, :, NG:36].rearrange("p t (g e) -> p t g e", g=NG)
            for tt in range(NT):
                link(dve.tensor_tensor(pick[:, tt], el[:, tt], g_hit[:, tt].unsqueeze(2).broadcast_to([P, NG, NEG]), ALU.mult))
            settle()
            for tt in range(NT):
                link(dve.tensor_reduce(l8[:, tt], pick[:, tt].rearrange("p g e -> p e g"), AX_X, ALU.add))
            settle()
            first_max(hit1, l8, m1, NEG)
            one(dve.tensor_scalar(l8b, hit1, -3.0e38, None, ALU.mult))
            one(dve.tensor_tensor(l8b, l8b, l8, ALU.add))
            first_max(hit2, l8b, m2, NEG)
            dve.tensor_tensor(e2, m2, m1, ALU.subtract).then_inc(S("router_exp"), 1)
            dve.wait_ge(S("router_exped"), 2)
            one(dve.tensor_reduce(g_sum, g_e, AX_X, ALU.add))
            one(dve.tensor_tensor(m8, hit1, hit2, ALU.add))
            for tt in range(NT):
                one(dve.tensor_tensor(hits[:, tt].rearrange("p (g e) -> p g e", g=NG), g_hit[:, tt].unsqueeze(2).broadcast_to([P, NG, NEG]),
                                      m8[:, tt].unsqueeze(1).broadcast_to([P, NG, NEG]), ALU.mult))
            dve.memset(ones, 1.0).then_inc(S("hits_ready"), 1)
            one(dve.tensor_scalar(wsum, e2, 1.0, None, ALU.add))
            one(dve.tensor_tensor(wsum, wsum, g_sum, ALU.mult))
            one(dve.reciprocal(w1, wsum))
            one(dve.tensor_tensor(w2, w1, e2, ALU.mult))
            one(dve.tensor_tensor(hit1, hit1, wide(w1, NEG), ALU.mult))
            one(dve.tensor_tensor(hit2, hit2, wide(w2, NEG), ALU.mult))
            one(dve.tensor_tensor(c8, hit1, hit2, ALU.add))
            for tt in range(NT):
                one(dve.tensor_tensor(comb[:, tt].rearrange("p (g e) -> p g e", g=NG), g_hit[:, tt].unsqueeze(2).broadcast_to([P, NG, NEG]),
                                      c8[:, tt].unsqueeze(1).broadcast_to([P, NG, NEG]), ALU.mult))

            dve.wait_ge(S("ranked"), 1)
            settle()
            link(dve.scalar_tensor_tensor(slot_of, buf(("rank", 0))[:, :, 0:NE], 1.0, hits, ALU.add, ALU.mult))
            settle()
            free_pair(("rank", 0))
            one(dve.tensor_scalar(slot_of, slot_of, -1.0, None, ALU.add))
            dve.tensor_reduce(most[:, 0:1], slot_of.rearrange("p t e -> p (t e)"), AX_X, ALU.max).then_inc(S("most_ready"), 1)
            dve.wait_ge(S("most_turned"), 1)
            dve.tensor_reduce(flag_f, ps[0:1, 2 * plan["most"][0], 0:P], AX_X, ALU.max).then_inc(S("pair_free%d" % plan["most"][0]), 1)
            pair_evacuated(dve, "most")
            dve.tensor_scalar(flag[0:1, 0:1], flag_f, float(SLOTS), None, ALU.is_ge).then_inc(S("flag_set"), 1)

            def select(e, rd, r, wait):
                if wait:
                    dve.wait_ge(S("gathered1"), (e + OFF[r]))
                slots_ = iota[:, SLOTS * rd:SLOTS * (rd + 1)]
                for tt in range(NT):
                    ins = dve.tensor_scalar(sel[:, tt, :], slots_, slot_of[:, tt, bass.ds(e, 1)], None, ALU.is_equal)
                    if tt == NT - 1:
                        ins.then_inc(S("sel_ready"), 1)
                if wait:
                    dve.wait_ge(S("sel_turned"), (e + OFF[r]))
                for tt in range(NT):
                    ins = dve.tensor_scalar(selw[:, tt, :], slots_, slot_of[:, tt, bass.ds(e, 1)], comb[:, tt, bass.ds(e, 1)],
                                            ALU.is_equal, ALU.mult)
                    if tt == NT - 1:
                        ins.then_inc(S("selw_ready"), 1)

            def remainder(n, e, base, r):
                dve.wait_ge(S("hi_ready"), (e + OFF[r]) * 6 + (n + 1))
                dve.tensor_tensor(w_lo[:, (base + n) % RING], ring[:, (base + n) % RING], w_hi[:, n % HI].bitcast(F32), ALU.subtract).then_inc(S("dve_lo"), 1)

            def gathered0(e, r):
                dve.wait_ge(S("xe_hi0"), (e + OFF[r]) + 1)
                dve.tensor_tensor(xe_lo[:, 0:4, :], four_chunks(2), xe_hi[:, 0:4, :].bitcast(F32), ALU.subtract).then_inc(S("xe0"), 1)

            def gathered1(e, r):
                dve.wait_ge(S("gathered1"), (e + OFF[r]) + 1)
                dve.tensor_copy(xe_hi[:, 4:8, :], four_chunks(0)).then_inc(S("xe_hi1"), 1)
                dve.wait_ge(S("xe_hi1"), (e + OFF[r]) + 1)
                dve.tensor_tensor(xe_lo[:, 4:8, :], four_chunks(0), xe_hi[:, 4:8, :].bitcast(F32), ALU.subtract).then_inc(S("xe1"), 1)

            def four_chunks(bank):
                return ps[:, bank, :].rearrange("p (k s) -> p k s", k=4)

            def output_left(e, j, base, r):
                dve.wait_ge(S("ye_hi"), (e + OFF[r]) * 2 + (j + 1))
                half = slice(W * j, W * (j + 1))
                dve.scalar_tensor_tensor(ye_lo[:, half], ps[:, 1 + j, :], slot_weight[:, 0:1], ye_hi[:, half].bitcast(F32),
                                         ALU.mult, ALU.subtract).then_inc(S("ye_lo"), 1)

            def expert(e, base, r, rd, tail):
                if not tail:
                    select(e + 1, rd, r, True)
                remainder(3, e, base, r)
                dve.wait_ge(S("slot_weight"), (e + OFF[r]) + 1)
                dve.wait_ge(S("unit_done" + r), e * 6 + (base + 3))
                dve.tensor_scalar(selT[:, :], ps[:, 3, 0:T], 0.0, None, ALU.is_gt).then_inc(S("selT"), 1)
                dve.wait_ge(S("silu"), (e + OFF[r]) + 1)
                dve.wait_ge(S("unit_done" + r), e * 6 + (base + 4))
                dve.tensor_tensor(he, ps[:, 1, :], sge, ALU.mult).then_inc(S("act_ready"), 1)
                if not tail:
                    gathered0(e + 1, r)
                dve.wait_ge(S("hT"), (e + OFF[r]) + 1)
                dve.tensor_tensor(heT_lo[:, :, :], four_chunks(3), heT_hi[:, :, :].bitcast(F32), ALU.subtract).then_inc(S("hT_lo"), 1)
                remainder(5, e, base, r)
                if not tail:
                    gathered1(e + 1, r)
                    remainder(0, e + 1, base, r)
                output_left(e, 0, base, r)
                if not tail:
                    remainder(1, e + 1, base, r)
                output_left(e, 1, base, r)

            def experts(base, r, rd):
                select(0, rd, r, False)
                gathered0(0, r)
                gathered1(0, r)
                remainder(0, 0, base, r)
                remainder(1, 0, base, r)
                with dve.Fori(0, NE - 1) as e:
                    expert(e, base, r, rd, False)
                expert(NE - 1, base, r, rd, True)
                dve.wait_ge(S("scattered"), (NE + OFF[r]))

            dve.wait_ge(S("load_iota"), 16)
            dve.wait_ge(S("flag_set"), 1)
            settle()
            experts(n_before, "", 0)
            more = dve.value_load(flag[0:1, 0:1], min_val=0, max_val=1)
            with dve.If(more > 0):
                experts(0, "_b", 1)

            for tt in range(NT):
                g2 = gt[:, 3 * D:4 * D].rearrange("p (a b) -> p a b", a=2)
                hv = h_tok[:, tt, :].rearrange("p (a b) -> p a b", a=2)
                freed(dve.tensor_tensor(hv, buf("moe_y%d" % tt), g2, ALU.mult), "moe_y%d" % tt)
            pair_evacuated(dve, "moe_y0")
            pair_evacuated(dve, "moe_y1")
            link(dve.scalar_tensor_tensor(x, x, ALPHA, h_tok, ALU.mult, ALU.add))
            settle()
            row_stats(lambda tt: x[:, tt, :], D)
            apply_norm(lambda tt: x[:, tt, :], lambda tt: x[:, tt, :])
            for c in range(2):
                gain_bias(x, "ln2_g", "ln2_b", c)

            rms(x, h_tok, None, "pre0")
            dve.sem_inc(S("a_in_ready"), 1)

            def rest_part(name, c, hi, lo):
                dve.wait_ge(S(name + "_hi"), c + 1)

                def part(v):
                    return v[:, 4 * c:4 * c + 4, :].rearrange("p k (t n) -> p t k n", t=NT)
                src = buf((name, c)).rearrange("p t (k n) -> p t k n", k=4)
                freed(dve.tensor_tensor(part(lo), src, part(hi).bitcast(F32), ALU.subtract), (name, c))

            for c in range(2):
                rest_part("aT", c, xt2_hi, xt2_lo)
            for t in range(4):
                pair_evacuated(dve, ("a", t))
            row_stats(lambda tt: a_v[:, tt, :], 2048)
            apply_norm(lambda tt: a_v[:, tt, :], lambda tt: a_v[:, tt, :])
            for c in range(4):
                gain_bias(a_v, "a_ln_g", "a_ln_b", c)
            dve.sem_inc(S("v_normed"), 1)
            dve.wait_ge(S("load_tri"), 16)
            for c in range(2):
                dve.wait_ge(S("wsT_turned"), c + 1)
                o = buf(("wsT", c))
                ins = dve.tensor_tensor(a_wsT[:, 4 * c:4 * c + 4, :], o[:, 0, :].rearrange("p (g t) -> p g t", g=4),
                                        a_tri.unsqueeze(1).broadcast_to([P, 4, P]), ALU.mult)
                ins.then_inc(S("wsT_ready"), 1)
                if c == 1:
                    link(dve.tensor_copy(a_bs, o[:, 1, 0:KC]))
                dve.wait_ge(S("wsT_ready"), c + 1)
                settle()
                free_pair(("wsT", c))
            for i in range(4):
                pair_evacuated(dve, ("a", 4 + i))
                dve.wait_ge(S("sv_done"), i + 1)
                o = buf(("sv", i))
                for g in (2 * i, 2 * i + 1):
                    uv = a_u[:, :, 256 * g:256 * (g + 1)]
                    link(dve.scalar_tensor_tensor(uv, o[:, :, 256 * (g % 2):256 * (g % 2 + 1)], a_bs[:, g:g + 1], uv, ALU.add, ALU.mult))
                settle()
                free_pair(("sv", i))
            for t in range(4):
                pair_evacuated(dve, ("a", 8 + t))
                v = a_z[:, :, W * t:W * (t + 1)]
                dve.tensor_tensor(v, v, a_u[:, :, W * t:W * (t + 1)], ALU.mult).then_inc(S("y_gated"), 1)
            for c in range(4):
                rest_part("yT", c, yt_hi, yt_lo)
            for t in range(2):
                pair_evacuated(dve, ("a_out", t))
            rms(y2, y2, None, "post0")
            link(dve.tensor_tensor(x, x, y2, ALU.add))
            settle()
            rms(x, y2, None, "pre1")
            dve.sem_inc(S("b_in_ready"), 1)
            for c in range(2):
                rest_part("bT", c, xt2_hi, xt2_lo)

            dve.wait_ge(S("load_c_rope2"), 16)
            dve.wait_ge(S("load_c_mask"), 16)
            n_rope = 0
            for t in range(20):
                if BKIND[t] in "qk":
                    tab = 0 if BKIND[t] == "q" else 1
                    dve.wait_ge(S("unit_done"), end_of("b", t))
                    raw = buf(("b", t))
                    if n_rope >= 1:
                        dve.wait_ge(S("b_roped"), n_rope)
                    if n_rope >= 2:
                        dve.wait_ge(S("b_turned"), n_rope - 1)
                    dst = b_rope[:, n_rope % 2]
                    for tt in range(NT):
                        s = raw[:, tt, :].rearrange("p (h s d) -> p h s d", h=8, s=2)
                        q = b_t2[:, tt, :].rearrange("p (h s d) -> p h s d", h=8, s=2)
                        cos = rope2[:, tab, 0, tt, :].unsqueeze(1).broadcast_to([P, 8, HD])
                        link(dve.tensor_tensor(dst[:, tt, :].rearrange("p (h d) -> p h d", h=8),
                                               raw[:, tt, :].rearrange("p (h d) -> p h d", h=8), cos, ALU.mult))
                        for s_ in range(2):
                            sin = rope2[:, tab, 1, tt, 32 * s_:32 * (s_ + 1)].unsqueeze(1).broadcast_to([P, 8, 32])
                            link(dve.tensor_tensor(q[:, :, s_, :], s[:, :, 1 - s_, :], sin, ALU.mult))
                    settle()
                    free_pair(("b", t))
                    dve.tensor_tensor(dst, dst, b_t2, ALU.add).then_inc(S("b_roped"), 1)
                    n_rope += 1
                for act, g, c in slots[t]:
                    if act == "scores":
                        for i in range(2):
                            dve.wait_ge(S("b_scored"), 2 * (4 * g + c) + i + 1)
                            o = buf((act, g, c, i))
                            for hh in range(2):
                                h = 4 * c + 2 * i + hh
                                if i == 0 and hh == 0 and (g or c):
                                    dve.wait_ge(S("b_p_turned"), 2 * (4 * g + c))
                                for tt in range(NT):
                                    r = slice(P * tt, P * tt + P * (tt + 1))
                                    link(dve.tensor_tensor(b_p[:, 2 * i + hh, r], o[:, hh, r], amask[:, g, P * (1 - tt):2 * P], ALU.add))
                            settle()
                            free_pair((act, g, c, i))
                            for hh in range(2):
                                h = 4 * c + 2 * i + hh
                                for tt in range(NT):
                                    r = slice(P * tt, P * tt + P * (tt + 1))
                                    ins = dve.tensor_reduce(b_nm[:, g, tt, h:h + 1], b_p[:, 2 * i + hh, r], AX_X, ALU.max, negate=True)
                                    if tt == 1:
                                        ins.then_inc(S("b_maxed"), 1)
                                    else:
                                        link(ins)
                    elif act == "values":
                        dve.wait_ge(S("b_valued"), 4 * g + c + 1)
                        o = buf((act, g, c))
                        freed(dve.tensor_copy(b_acc[:, g, :, 4 * c:4 * c + 4, :],
                                              o[:, :, 0:256].rearrange("p t (h d) -> p t h d", h=4)), (act, g, c))
            dve.wait_ge(S("b_maxed"), 48)
            settle()
            dve.wait_ge(S("b_probs"), 48)
            one(dve.tensor_tensor(b_q, b_nm[:, 0], b_nm[:, 1], ALU.min))
            one(dve.tensor_tensor(b_q, b_q, b_nm[:, 2], ALU.min))
            for g in range(DIL):
                ins = dve.tensor_tensor(b_e[:, g], b_q, b_nm[:, g], ALU.subtract)
                if g == 2:
                    ins.then_inc(S("b_ediff"), 1)
                else:
                    link(ins)
            dve.wait_ge(S("b_eexp"), 1)
            one(dve.tensor_tensor(b_s, b_s, b_e, ALU.mult))
            one(dve.tensor_tensor(b_q, b_s[:, 0], b_s[:, 1], ALU.add))
            one(dve.tensor_tensor(b_q, b_q, b_s[:, 2], ALU.add))
            one(dve.reciprocal(b_q, b_q))
            for g in range(DIL):
                link(dve.tensor_tensor(b_e[:, g], b_e[:, g], b_q, ALU.mult))
            settle()
            for c in range(4):
                pair_evacuated(dve, ("values", 2, c))
            for g in range(DIL):
                for tt in range(NT):
                    v = b_acc[:, g, tt]
                    link(dve.tensor_tensor(v, v, b_e[:, g, tt, :].unsqueeze(2).broadcast_to([P, HEADS, HD]), ALU.mult))
            settle()
            acc = [b_acc[:, g].rearrange("p t h d -> p t (h d)") for g in range(DIL)]
            one(dve.tensor_tensor(acc[0], acc[0], acc[1], ALU.add))
            one(dve.tensor_tensor(acc[0], acc[0], acc[2], ALU.add))
            for t in (16, 17):
                pair_evacuated(dve, ("b", t))
            dve.tensor_tensor(b_z, b_z, acc[0], ALU.mult).then_inc(S("b_o_ready"), 1)
            for c in range(2):
                rest_part("oT", c, ot_hi, ot_lo)
            for t in range(2):
                pair_evacuated(dve, ("b_out", t))
            rms(y2, y2, None, "post1")
            dve.tensor_tensor(x, x, y2, ALU.add).then_inc(S("out_ready"), 1)

        @block.gpsimd
        def _(pool):
            pool.memset(minus_half, -0.5).then_inc(S("half_set"), 1)
            pool.wait_ge(S("half_set"), 1)

            def norm_powers(first_norm, last_norm):
                for n in range(first_norm, last_norm):
                    pool.wait_ge(S("stats_ready"), n + 1)
                    pool.tensor_scalar(ms, mv[:, :, 1], norm_eps[n], None, ALU.add).then_inc(S("eps_added"), 1)
                    pool.wait_ge(S("eps_added"), n + 1)
                    pool.tensor_tensor(rstd, ms, minus_half, ALU.pow).then_inc(S("rstd_ready"), 1)

            def remainders(base, r):
                with pool.Fori(0, NE) as e:
                    for j, n in enumerate(POOL_UNITS):
                        pool.wait_ge(S("hi_ready"), (e + OFF[r]) * 6 + (n + 1))
                        pool.tensor_tensor(w_lo[:, (base + n) % RING], ring[:, (base + n) % RING], w_hi[:, n % HI].bitcast(F32), ALU.subtract).then_inc(S("pool_lo"), 1)

            norm_powers(0, MOE_NORM)
            remainders(n_before, "")
            pool.wait_ge(S("flag_set"), 1)
            more = pool.value_load(flag[0:1, 0:1], min_val=0, max_val=1)
            with pool.If(more > 0):
                remainders(0, "_b")
            def remainders_to(end):
                for n in range(first["a"] + left[0], end):
                    m = n - first["a"]
                    pool.wait_ge(S("w_hi_full"), m + 1)
                    pool.tensor_tensor(w_lo2[:, m % RING2], ring[:, m % RING2], w_hi2[m % HI][:, :, :].bitcast(F32), ALU.subtract).then_inc(S("w_lo_full"), 1)
                left[0] = end - first["a"]

            left = [0]
            for n, end in ((0, first["a"] + 1), (1, first["a"] + 11), (2, first["b"] + 1),
                           (3, first["b"] + 2), (4, len(units)), (5, len(units))):
                norm_powers(MOE_NORM + n, MOE_NORM + n + 1)
                remainders_to(end)

        @block.scalar
        def _(act):
            def evacuate(key, dst, view=None, func=ACT.Copy):
                src = buf(key) if view is None else view(buf(key))
                freed(act.activation(dst, src, func), key)

            def chunks(dstT, c, o=0):
                return dstT[:, o + 4 * c:o + 4 * c + 4, :].rearrange("p k (t n) -> p t k n", t=NT)

            def four(p_):
                return p_.rearrange("p t (k n) -> p t k n", k=4)

            act.wait_ge(S("rows_turned"), 1)
            act.activation(sT, buf("turn_rows")[:, 0, 0:16], ACT.Silu).then_inc(S("silu_c"), 1)
            act.activation(cwT, buf("turn_rows")[:, 1, 0:256].rearrange("p (k n) -> p k n", k=KC), ACT.Copy).then_inc(S("pair_free2"), 1)
            act.wait_ge(S("neg_abs"), 1)
            act.activation(la[:, 0, :], la[:, 0, :], ACT.Exp).then_inc(S("exp_abs"), 1)
            act.wait_ge(S("wdec_exps"), 1)
            act.activation(wdec, wdec, ACT.Exp).then_inc(S("wdec_exp"), 1)
            for s in range(2):
                for c in range(2):
                    act.wait_ge(S("uT_turned"), 2 * s + c + 1)
                    evacuate(("uT", s, c), chunks(XT, c, 8 * s), four)

            def sigmoid_z(i):
                pair_evacuated(act, ("glu", 2 * i + 1))
                v = tmp[:, 2 * i:2 * i + 2, :]
                act.activation(v, v, ACT.Sigmoid).then_inc(S("sig_z"), 1)

            def turned_z(i):
                act.wait_ge(S("zT_turned"), i + 1)
                evacuate(("zT", i), z_pad[:, 4 * i:4 * i + 4, PAD:PAD + T].rearrange("p k (t n) -> p t k n", t=NT), four)
            sigmoid_z(0)
            turned_z(0)
            sigmoid_z(1)
            turned_z(1)
            for n, (dst, t) in enumerate(((kT, 0), (kT, 1), (qT, 0), (qT, 1))):
                act.wait_ge(S("heads_turned"), n + 1)
                evacuate((("kT", t), ("qT", t))[n // 2], chunks(dst, t), four)
            for i in range(4):
                act.wait_ge(S("state_done"), 2 * i + 2)
                freed(act.activation(state[:, 2 * i:2 * i + 2].rearrange("p h d v -> p h (d v)"), buf(("S", i)), ACT.Copy), ("S", i))
            for c in range(2):
                act.wait_ge(S("cz_turned"), c + 1)
                evacuate(("cz", c), cz[:, :, W * c:W * (c + 1)])

            def decays(h):
                if h >= 2:
                    act.wait_ge(S("ret_summed"), h - 1)
                Q = tmp[:, 4 + h % 2, :].rearrange("p (d n) -> p d n", d=2)
                act.activation(Q[:, 0, :], row_fb[:, 0, :], ACT.Exp, scale=lg[:, h:h + 1])
                act.activation(Q[:, 1, :], row_fb[:, 1, :], ACT.Exp, scale=lg[:, H + h:H + h + 1])
                act.wait_ge(S("ret_exps"), h + 1)
                E = tmp[:, 2 + h % 2, :]
                act.activation(E, E, ACT.Exp).then_inc(S("ret_exped"), 1)
            act.wait_ge(S("load_c_rows"), 16)
            decays(0)
            decays(1)
            for i in range(4):
                pair_evacuated(act, ("g", i))
                v = sg[:, :, W * i:W * (i + 1)]
                act.activation(v, v, ACT.Silu).then_inc(S("silu_g"), 1)
                if i < 3:
                    decays(2 * i + 2)
                    decays(2 * i + 3)
            act.wait_ge(S("cz_normed"), 1)
            act.activation(cz, cz, ACT.Silu).then_inc(S("cz_ready"), 1)
            for t in range(4):
                pair_evacuated(act, ("gate", t))
                v = gates[:, :, W * t:W * (t + 1)]
                act.activation(v, v, ACT.Sigmoid).then_inc(S("sig_gates"), 1)
            act.wait_ge(S("unit_done"), end_of("gate", 3))
            for c in range(4):
                act.wait_ge(S("retT_turned"), c + 1)
                evacuate(("retT", c), chunks(XT, c), four)
            for c in range(2):
                act.wait_ge(S("cvT_turned"), c + 1)
                evacuate(("cvT", c), chunks(XT2, c), four)
            for c in range(2):
                act.wait_ge(S("mT_turned"), c + 1)
                evacuate(("mT", c), chunks(XT, c), four)
            for c in range(2):
                act.wait_ge(S("eT_turned"), c + 1)
                evacuate(("eT", c), chunks(XT2, c), four)
            act.wait_ge(S("router_exp"), 1)
            g_e, _ = carve(NT, NG, on=o_rt + NT)
            e2, _ = carve(NT, on=o_rt + NT + NT * NG + NT + NT * NG + NT + NT * NG * NEG + NT * NEG + NT + 2 * NT * NEG + NT)
            act.activation(g_e, g_e, ACT.Exp).then_inc(S("router_exped"), 1)
            act.wait_ge(S("router_exp"), 2)
            act.activation(e2, e2, ACT.Exp).then_inc(S("router_exped"), 1)

            def leading(n, e, base, r, start=False):
                m = base + n
                if not start:
                    act.wait_ge(S("unit_done" + r), e * 6 + (m - HI + 1))
                act.wait_ge(S("w_full%d%s" % (m % RING, r)), e * 16 + 16 * (m // RING + 1))
                act.activation(w_hi[:, n % HI], ring[:, m % RING], ACT.Copy).then_inc(S("hi_ready"), 1)

            def gathered(e, r):
                act.wait_ge(S("gathered0"), (e + OFF[r]) + 1)
                act.activation(xe_hi[:, 0:4, :], ps[:, 2, :].rearrange("p (k s) -> p k s", k=4), ACT.Copy).then_inc(S("xe_hi0"), 1)

            def output(e, j, base, r):
                act.wait_ge(S("unit_done" + r), e * 6 + (base + 5 + j))
                act.activation(ye_hi[:, W * j:W * (j + 1)], ps[:, 1 + j, :], ACT.Copy, scale=slot_weight[:, 0:1]).then_inc(S("ye_hi"), 1)

            def expert(e, base, r, head, tail):
                leading(3, e, base, r)
                act.wait_ge(S("unit_done" + r), e * 6 + (base + 2))
                act.activation(sge, ps[:, 0, :], ACT.Silu).then_inc(S("silu"), 1)
                act.wait_ge(S("sel_turned"), (e + OFF[r]) + 1)
                if not head:
                    act.wait_ge(S("ye_lo"), (e + OFF[r]) * 2)
                act.activation(weighted, ps[:, 3, 0:T], ACT.Copy, accum_out=slot_weight[:, 0:1]).then_inc(S("slot_weight"), 1)
                leading(4, e, base, r)
                leading(5, e, base, r)
                if not tail:
                    gathered(e + 1, r)
                act.wait_ge(S("h_turned"), (e + OFF[r]) + 1)
                act.activation(heT_hi[:, :, :], ps[:, 3, :].rearrange("p (k s) -> p k s", k=4), ACT.Copy).then_inc(S("hT"), 1)
                if not tail:
                    leading(0, e + 1, base, r)
                output(e, 0, base, r)
                if not tail:
                    leading(1, e + 1, base, r)
                output(e, 1, base, r)
                if not tail:
                    leading(2, e + 1, base, r)

            def experts(base, r):
                for n in range(HI):
                    leading(n, 0, base, r, True)
                gathered(0, r)
                expert(0, base, r, True, False)
                with act.Fori(1, NE - 1) as e:
                    expert(e, base, r, False, False)
                expert(NE - 1, base, r, False, True)

            experts(n_before, "")
            act.wait_ge(S("flag_set"), 1)
            more = act.value_load(flag[0:1, 0:1], min_val=0, max_val=1)
            with act.If(more > 0):
                experts(0, "_b")

            led = [first["a"]]

            def leading_to(done):
                while led[0] < min(done + HI, len(units)):
                    n = led[0]
                    m = n - first["a"]
                    if m >= HI:
                        act.wait_ge(S("unit_done"), n - HI + 1)
                    elif m == HI - 1:
                        act.wait_ge(S("stats_ready"), MOE_NORM + 1)
                    act.wait_ge(S("w_full%d" % slots_of[n]), 16 * fills[n])
                    act.activation(w_hi2[m % HI][:, :, :], ring[:, slots_of[n]], ACT.Copy).then_inc(S("w_hi_full"), 1)
                    led[0] += 1

            def lead_part(name, c, dst):
                act.wait_ge(S(name + "_turned"), c + 1)
                act.activation(chunks(dst, c), four(buf((name, c))), ACT.Copy).then_inc(S(name + "_hi"), 1)

            leading_to(first["a"])
            for c in range(2):
                lead_part("aT", c, xt2_hi)
            for t in range(12):
                leading_to(end_of("a", t) - 1)
                act.wait_ge(S("unit_done"), end_of("a", t))
                dst = (a_v, a_u, a_z)[t // 4][:, :, W * (t % 4):W * (t % 4 + 1)]
                freed(act.activation(dst, buf(("a", t)), ACT.Gelu if t < 8 else ACT.Silu), ("a", t))
            for c in range(4):
                lead_part("yT", c, yt_hi)

            def evac_y(key, ready):
                freed(act.activation(y2[:, :, W * key[1]:W * (key[1] + 1)], buf(key), ACT.Copy), key)
            for t in range(2):
                leading_to(end_of("a_out", t, 4) - 1)
                act.wait_ge(S("unit_done"), end_of("a_out", t, 4))
                evac_y(("a_out", t), None)
            leading_to(first["b"])
            for c in range(2):
                lead_part("bT", c, xt2_hi)
            n_rope = 0
            for t in range(20):
                g = BGROUP[t]
                leading_to(end_of("b", t) - 1)
                if BKIND[t] in "vz":
                    act.wait_ge(S("unit_done"), end_of("b", t))
                    if BKIND[t] == "v":
                        if g:
                            act.wait_ge(S("b_valued"), 4 * (g - 1) + 2 * BIDX[t] + 2)
                        dst = b_v[:, :, W * BIDX[t]:W * (BIDX[t] + 1)]
                        freed(act.activation(dst, buf(("b", t)), ACT.Copy), ("b", t))
                    else:
                        freed(act.activation(b_z[:, :, W * BIDX[t]:W * (BIDX[t] + 1)], buf(("b", t)), ACT.Silu), ("b", t))
                if t and BKIND[t - 1] in "qk":
                    n_rope += 1
                    act.wait_ge(S("b_turned"), n_rope)
                    dst = (b_qT, b_kT)[BKIND[t - 1] == "k"][:, BGROUP[t - 1] % 2]
                    evacuate(("bqk", t - 1), chunks(dst, BIDX[t - 1]), four)
                for what, g, c in slots[t]:
                    if what == "turn":
                        n = 4 * g + c
                        for i in range(2):
                            act.wait_ge(S("b_p_turned"), 2 * n + i + 1)
                            if n >= 2:
                                act.wait_ge(S("b_valued"), n - 1)
                            freed(act.activation(b_pT[:, c % 2, 2 * i:2 * i + 2, :], buf(("turn", g, c, i))[:, :, 0:384], ACT.Copy), ("turn", g, c, i))
                    elif what == "scores":
                        for hh in range(4):
                            h = 4 * c + hh
                            act.wait_ge(S("b_maxed"), 4 * (4 * g + c) + hh + 1)
                            for tt in range(NT):
                                r = slice(P * tt, P * tt + P * (tt + 1))
                                ins = act.activation(b_p[:, hh, r], b_p[:, hh, r], ACT.Exp, bias=b_nm[:, g, tt, h:h + 1],
                                                     accum_out=b_s[:, g, tt, h:h + 1])
                                if tt == 1:
                                    ins.then_inc(S("b_probs"), 1)
            leading_to(first["b_out"])
            act.wait_ge(S("b_ediff"), 1)
            act.activation(b_e, b_e, ACT.Exp).then_inc(S("b_eexp"), 1)
            for c in range(2):
                lead_part("oT", c, ot_hi)
            for t in range(2):
                leading_to(end_of("b_out", t) - 1)
                act.wait_ge(S("unit_done"), end_of("b_out", t))
                evac_y(("b_out", t), None)


def tables():
    f = np.float32
    tok = np.arange(T)
    m = (np.arange(P)[:, None] + P * np.arange(NT)[None, :])[:, :, None]
    n = tok[None, None, :]
    out = {
        "c_dist_f": np.maximum(n - m, 0).astype(f),
        "c_dist_b": np.maximum(m - n, 0).astype(f),
        "c_log": (np.log(DK ** -0.5) + np.log(2.0) * (n == m)).astype(f),
        "c_rows": np.broadcast_to(np.stack([tok + 1, T - tok]), (P, 2, T)).astype(f).copy(),
        "c_pos": np.stack([T - 1 - m[:, :, 0], m[:, :, 0]], axis=1).astype(f),
        "c_ident": np.eye(P, dtype=f),
        "c_tri": np.triu(np.ones((P, P), f)),
        "c_before": np.triu(np.ones((P, P), f), 1),
        "c_iota": np.broadcast_to(tok, (P, T)).astype(f).copy(),
    }

    def halves(ang, scale=1.0):
        cos, sin = np.cos(ang.astype(f)), np.sin(ang.astype(f))
        t = np.stack([np.concatenate([cos, cos], -1), np.concatenate([-sin, sin], -1)])
        return (t * scale).astype(f).reshape(2, NT, P, -1).transpose(2, 0, 1, 3)

    inv = (f(10000.0) ** (-np.arange(DK // 4, dtype=f) / f(DK // 4))).astype(f)
    r, col = (tok // 64).astype(f), (tok % 64).astype(f)
    out["c_rope1"] = halves(np.concatenate([r[:, None] * inv, col[:, None] * inv], -1)).copy()
    inv2 = (f(1.0) / (f(10000.0) ** (np.arange(0, HD, 2, dtype=f) / f(HD)))).astype(f)
    ang = tok.astype(f)[:, None] * inv2[None, :]
    out["c_rope2"] = np.stack([halves(ang, HD ** -0.5), halves(ang)], axis=1).copy()
    rel = np.concatenate([P + np.arange(P)[:, None] - np.arange(P), np.arange(P)[:, None] - np.arange(P)], -1)
    masks = []
    for window, step in ((128, 1), (512, 4), (2048, 16)):
        masks.append(np.where((rel >= 0) & (rel <= window) & (rel % step == 0), 0.0, -1.0e30))
    out["c_mask"] = np.stack(masks, axis=1).astype(f)
    return out


_INS = ["x", "c", "ctx", "c_ctx", "w_ada", "b_ada", "w_in", "b_in", "ret_decay_fwd", "ret_decay_bwd", "w_ret_out",
        "conv_dw", "conv_dw_b", "conv_ln_g", "conv_ln_b", "w_conv_out", "b_conv_out", "w_mix_out", "b_mix_out",
        "ln1_g", "ln1_b", "w_router_grp", "b_router_grp", "w_router_exp", "b_router_exp", "w_exp_gate", "w_exp_up",
        "w_exp_down", "ln2_g", "ln2_b", "norm_pre_2", "norm_post_2", "a_w_in_2", "a_ln_g_2", "a_ln_b_2", "a_w_s_2",
        "a_b_s_2", "a_w_out_2", "b_w_in_2", "b_w_out_2"]


def kernel(**inputs):
    import concourse.bacc as bacc
    from concourse.bass_utils import run_bass_kernel_spmd

    nc = bacc.Bacc("TRN2", target_bir_lowering=False, num_devices=1)
    given = {name: np.ascontiguousarray(inputs[name]) for name in _INS}
    given.update({name: np.ascontiguousarray(t) for name, t in tables().items()})
    arrays, aps = {}, {}
    for name, v in given.items():
        arrays["in_" + name] = v
        aps[name] = nc.dram_tensor("in_" + name, v.shape, mybir.dt.from_np(v.dtype), kind="ExternalInput").ap()
    out = nc.dram_tensor("out_0", (1, T, D), F32, kind="ExternalOutput").ap()
    build(nc, aps, out)
    r = run_bass_kernel_spmd(nc, [arrays], core_ids=[0])
    return r.results[0]["out_0"]
```

```python
from contextlib import ExitStack

import numpy as np

import concourse.bass as bass
from concourse import mybir

F32 = mybir.dt.float32
F32R = mybir.dt.float32r
BF16 = mybir.dt.bfloat16
ALU = mybir.AluOpType
ACT = mybir.ActivationFunctionType
AX_X = mybir.AxisListType.X

P = 128
T = 256
NT = T // P
D = 1024
KC = D // P
W = 512
HALF_K = 512
UC = HALF_K // P
H = 8
DK = 128
DV = 256
TAPS = 31
PAD = TAPS // 2
NG, NEG = 4, 8
NE = NG * NEG
FF = 512
SLOTS = 128
ROUNDS = T // SLOTS
HEADS = 16
HD = 64
DIL = 3
LN_EPS = 1e-5
RMS_EPS = 1e-6
ALPHA = 2.0 ** 0.25
RING = 6
ARENA = 53200 - RING * UC * W
FLAG_AT = 16512
RING_AT = FLAG_AT + 32
ARENA_AT = RING_AT + 4 * RING * UC * W
HI = 3
POOL_UNITS = (2, 4)
DVE_UNITS = (0, 1, 3, 5)
RING2 = 4
HI1 = RING - RING2
AUXN = 4

GLU = [12, 14, 13, 15]
KCOLS = [2, 3]
VCOLS = [4, 5, 6, 7]
QCOLS = [0, 1]
GCOLS = [8, 9, 10, 11]
GATECOLS = [16, 17, 18, 19]
BCOLS = list(range(12)) + [12, 13, 14, 15, 18, 19, 16, 17]
BKIND = (["q", "q", "k", "k", "v", "v"] * 2) + ["q", "q", "k", "k", "z", "z", "v", "v"]
BGROUP = [0] * 6 + [1] * 6 + [2] * 8
BIDX = [0, 1] * 10


def attention_slots():
    after = {t: [] for t in range(20)}
    for g, first in ((0, 5), (1, 11), (2, 16)):
        for c in range(4):
            for stage, name in enumerate(("scores", "turn", "values")):
                if first + c + stage < 19:
                    after[first + c + stage].append(((2 - stage, c), name, g, c))
    steps = {t: [s[1:] for s in sorted(a)] for t, a in after.items()}
    steps[18] = [s for s in steps[18] if s[0] != "values"]
    steps[19] = [("values", 2, 0), ("turn", 2, 2), ("scores", 2, 3), ("values", 2, 1), ("turn", 2, 3), ("values", 2, 2), ("values", 2, 3)]
    return steps


def build(nc, a, out):
    with ExitStack() as ctx:
        sems = {}

        def S(name):
            if name not in sems:
                sems[name] = ctx.enter_context(nc.semaphore(name))
            return sems[name]

        arena = nc.alloc_sbuf_tensor_at("arena", [P, ARENA], F32, offset=ARENA_AT)
        at = [0]

        def carve(*shape, on=None):
            n = int(np.prod(shape))
            o = at[0] if on is None else on
            if on is None:
                at[0] += n
                assert at[0] <= ARENA, at[0]
            v = arena[:, o:o + n]
            if len(shape) == 2:
                v = v.rearrange("p (a b) -> p a b", a=shape[0])
            if len(shape) == 3:
                v = v.rearrange("p (a b c) -> p a b c", a=shape[0], b=shape[1])
            if len(shape) == 4:
                v = v.rearrange("p (a b c d) -> p a b c d", a=shape[0], b=shape[1], c=shape[2])
            return v, o

        def single_pass(name, *shape, on=None):
            return nc.alloc_sbuf_tensor_at(name, [P] + list(shape), F32R, offset=RING_AT if on is None else ARENA_AT + 4 * on)

        ring = nc.alloc_sbuf_tensor_at("ring", [P, RING, UC, W], F32, offset=RING_AT)
        aux, _ = carve(AUXN, W)
        x, o_x = carve(NT, D)
        XT, o_XT = carve(16, T)
        XT2, o_XT2 = carve(8, T)
        mod_lat, o_ml = carve(2048)
        z_pad, o_zp = carve(KC, T + 2 * PAD)
        tmp, o_tmp = carve(6, W)
        qT, o_qT = carve(H, T)
        kT, o_kT = carve(H, T)
        v_lat, o_v = carve(NT, H * DV)
        k_ctx, o_kc = carve(NT, D)
        v_ctx, o_vc = carve(NT, H * DV)
        state, o_S = carve(H, 2, DV)
        consts, o_cn = carve(3 * NT * T + 2 * T + 2 * NT * P + 4 * NT * HD + DIL * 2 * P + P)
        small, o_sm = carve(836)

        conv, _ = carve(KC, T, on=o_ml)
        cz, _ = carve(NT, D, on=o_zp)
        mod_ctx, _ = carve(2048, on=o_S)
        z_tok, _ = carve(2, NT, W, on=o_S + 2048)
        roped, _ = carve(2, NT, W, on=o_XT2)
        o_lo, _ = carve(NT, 4 * DV, on=o_kc)
        o_hi, _ = carve(NT, 4 * DV, on=o_XT2)
        sg, _ = carve(NT, H * DV, on=o_vc)
        gates, _ = carve(NT, 2048, on=o_v)
        mod_tail, _ = carve(4096, on=o_S)
        u_lat, _ = carve(NT, D, on=o_v)
        u_ctx, _ = carve(NT, D, on=o_v + 2048)
        x_ctx, _ = carve(NT, D, on=o_vc)
        rows16 = arena[0:16, o_tmp:o_tmp + P]
        rows32 = arena[0:32, o_tmp + 1024:o_tmp + 2048]

        o = o_cn

        def const(*shape):
            nonlocal o
            v, _ = carve(*shape, on=o)
            o += int(np.prod(shape))
            return v
        dist_f = const(NT, T)
        dist_b = const(NT, T)
        log_c = const(NT, T)
        amask = const(DIL, 2 * P)
        row_fb = const(2, T)
        rope1 = const(2, NT, P)
        rope2 = const(2, 2, NT, HD)
        ident = const(P)
        o = o_sm
        lg = const(2 * H)
        la = const(3, 2 * H)
        pos = const(2, NT)
        wdec = const(2, NT, H)
        sT = const(2 * KC)
        cwT = const(KC, 32)
        stats = const(NT, 4, 6)
        mv = const(NT, 2)
        ms = const(NT)
        rstd = const(NT)
        minus_half = const(NT)
        sq = const(NT)
        wr = const(KC, 36)
        br = const(36)
        lgt = const(NT, 36)
        assert o <= o_sm + 836

        flag = nc.alloc_sbuf_tensor_at("flag", [1, 1], mybir.dt.int32, offset=FLAG_AT)
        ps = ctx.enter_context(nc.psum_tensor("ps", [P, 8, W], F32))

        def pair(p):
            return ps[:, 2 * p:2 * p + 2, :]

        units = []
        first = {}

        def stream(name, w, cols, nk):
            first[name] = len(units)
            for c in cols:
                for j in range(nk):
                    units.append(w[HALF_K * j:HALF_K * (j + 1), W * c:W * (c + 1)])

        w_in = a["w_in"][0]
        stream("ada", a["w_ada"][0], range(4), 2)
        for name, cols in (("glu", GLU), ("k", KCOLS), ("v", VCOLS), ("q", QCOLS), ("g", GCOLS), ("gate", GATECOLS)):
            stream(name, w_in, cols, 2)
        stream("ada_tail", a["w_ada"][0], range(4, 12), 2)
        stream("ret", a["w_ret_out"][0], range(2), 4)
        stream("conv", a["w_conv_out"][0], range(2), 2)
        stream("mix", a["w_mix_out"][0], range(2), 2)
        n_before = len(units)
        first["moe"] = n_before
        n_moe = 6 * NE
        units += [None] * n_moe
        stream("a", a["a_w_in_2"][0], [4, 5, 6, 7, 0, 1, 2, 3, 8, 9, 10, 11], 2)
        stream("a_out", a["a_w_out_2"][0], range(2), 4)
        stream("b", a["b_w_in_2"][0], BCOLS, 2)
        stream("b_out", a["b_w_out_2"][0], range(2), 2)

        slots_of, fills = [], []
        for n in range(len(units)):
            slots_of.append(n % RING2 if n < n_before else (n - n_before) % RING if n < first["a"] else (n - first["a"]) % RING2)
            fills.append(slots_of.count(slots_of[n]))

        fills_before = [slots_of[:n_before].count(k) for k in range(RING)]

        def part_of(n):
            return (n, w_hi2[n % HI1]) if n < n_before else (n - n_moe, w_hi2[(n - first["a"]) % HI])

        by_vector = [n for name, tiles in (("ada", 4), ("ada_tail", 8)) for n in range(first[name] + 1, first[name] + 2 * tiles, 2)]
        by_pool = [n for n in range(len(units)) if n not in by_vector and not n_before <= n < first["a"]]

        def remainder_ready(eng, n):
            if n in by_vector:
                eng.wait_ge(S("w_lo_vector"), by_vector.index(n) + 1)
            else:
                eng.wait_ge(S("w_lo_full"), by_pool.index(n) + 1)

        def moe_src(kind, e, j):
            if kind == "down":
                return a["w_exp_down"][0, bass.ds(e, 1), :, W * j:W * (j + 1)].rearrange("e (k p) c -> p (e k) c", p=P)
            w = a["w_exp_gate"] if kind == "gate" else a["w_exp_up"]
            return w[0, bass.ds(e, 1), HALF_K * j:HALF_K * (j + 1), :].rearrange("e (k p) c -> p (e k) c", p=P)

        def end_of(name, t, nk=2):
            return first[name] + (t + 1) * nk

        rows = []
        row_after = {}
        row_of = {}

        def bring(key, vec, unit):
            row_of[key] = len(rows)
            rows.append(vec)
            row_after.setdefault(unit, []).append(len(rows) - 1)

        def vec(name, c, i=0):
            return a[name][i:i + 1, W * c:W * (c + 1)]

        used = [0] * 4
        plan = {}

        def take(key, p):
            used[p] += 1
            plan[key] = (p, used[p])

        main = [0]

        def take_main(key):
            take(key, main[0] % 2)
            main[0] += 1

        side = [0]

        def take_side(key):
            take(key, 2 + side[0] % 2)
            side[0] += 1

        take("turn_rows", 2)
        for t in range(4):
            take_main(("ada", t))
            bring(("ada", t), vec("b_ada", t), t)
        for s in range(2):
            for c in range(2):
                take_side(("uT", s, c))
        for t in range(4):
            take_main(("glu", t))
            bring(("glu", t), vec("b_in", GLU[t]), first["glu"] + 2 * t + 1)
        take_side(("zT", 0))
        take_side(("zT", 1))
        if main[0] % 2:
            main[0] += 1
        for t in range(2):
            take("k_lat%d" % t, 0)
            take("k_ctx%d" % t, 1)
            bring(("k", t), vec("b_in", KCOLS[t]), first["k"] + 2 * t + 1)
        take_side(("kT", 0))
        for t in range(4):
            take("v_lat%d" % t, 0)
            take("v_ctx%d" % t, 1)
            bring(("v", t), vec("b_in", VCOLS[t]), first["v"] + 2 * t + 1)
        take_side(("kT", 1))
        for t in range(2):
            take_main(("q", t))
            bring(("q", t), vec("b_in", QCOLS[t]), first["q"] + 2 * t + 1)
        take_side(("qT", 0))
        take_side(("qT", 1))
        for i in range(4):
            take_side(("S", i))
        for c in range(2):
            take_side(("cz", c))
        side[0] += side[0] % 2
        for i in range(4):
            take(("sc", i), 2)
            take(("av", i), 3)
            take_main(("g", i))
            bring(("g", i), vec("b_in", GCOLS[i]), first["g"] + 2 * i + 1)
        for c in range(2):
            bring(("conv_g", c), vec("conv_ln_g", c), first["gate"] + 1)
            bring(("conv_b", c), vec("conv_ln_b", c), first["gate"] + 1)
        for t in range(4):
            take_main(("gate", t))
            bring(("gate", t), vec("b_in", GATECOLS[t]), first["gate"] + 2 * t + 4)
        for t in range(8):
            take_main(("ada_tail", t))
            bring(("ada_tail", t), vec("b_ada", 4 + t), first["ada_tail"] + 2 * t + 4)
        for c in range(4):
            take_side(("retT", c))
        for c in range(2):
            take_side(("cvT", c))
        for t in range(2):
            take_main(("ret", t))
        for t in range(2):
            take_main(("conv", t))
            bring(("conv", t), vec("b_conv_out", t), first["conv"] + 2 * t + 1)
        for c in range(2):
            take_side(("mT", c))
        for t in range(2):
            take_main(("mix", t))
            bring(("mix", t), vec("b_mix_out", t), first["mix"] + 2 * t + 1)
        for c in range(2):
            bring(("ln1_g", c), vec("ln1_g", c), first["mix"] + 3)
            bring(("ln1_b", c), vec("ln1_b", c), first["mix"] + 3)
        for c in range(2):
            take_side(("eT", c))
        main[0] += main[0] % 2
        take("router", 0)
        take_side(("rank", 0))
        take_side("most")
        entry0, entry1 = used[0], used[1]
        take("moe_y0", 2)
        take("moe_y1", 3)
        for c in range(2):
            bring(("ln2_g", c), vec("ln2_g", c), first["a"])
            bring(("ln2_b", c), vec("ln2_b", c), first["a"])
        for c in range(2):
            bring(("pre0", c), vec("norm_pre_2", c, 0), first["a"] + RING2 - 1)
        for c in range(2):
            take_side(("aT", c))
        for t in range(8):
            take_main(("a", t))
        for c in range(4):
            bring(("a_ln_g", c), vec("a_ln_g_2", c), first["a"] + (8 if c < 2 else 14))
            bring(("a_ln_b", c), vec("a_ln_b_2", c), first["a"] + (8 if c < 2 else 14))
        for c in range(2):
            take_side(("wsT", c))
        for i in range(4):
            take_side(("sv", i))
        for t in range(8, 12):
            take_main(("a", t))
        for c in range(4):
            take_side(("yT", c))
        for t in range(2):
            take_main(("a_out", t))
        for c in range(2):
            bring(("post0", c), vec("norm_post_2", c, 0), first["a_out"] + 7)
        for c in range(2):
            bring(("pre1", c), vec("norm_pre_2", c, 1), first["a_out"] + 7)
        for c in range(2):
            take_side(("bT", c))
        slots = attention_slots()
        for t in range(20):
            take_main(("b", t))
            if t and BKIND[t - 1] in "qk":
                take_side(("bqk", t - 1))
            for act, g, c in slots[t]:
                if act in ("scores", "turn"):
                    for i in range(2):
                        take((act, g, c, i), 2 + i)
                else:
                    take_main((act, g, c))
        for c in range(2):
            take_side(("oT", c))
        for t in range(2):
            take_main(("b_out", t))
        for c in range(2):
            bring(("post1", c), vec("norm_post_2", c, 1), first["b_out"] + 3)

        def row_ready(eng, key):
            n = row_of[key]
            eng.wait_ge(S("row_full%d" % (n % AUXN)), 16 * (n // AUXN + 1))
            return aux[:, n % AUXN, :]

        def bc2(v, n=W):
            return v.unsqueeze(1).broadcast_to([P, NT, n])

        def pair_evacuated(eng, key):
            p, k = plan[key]
            eng.wait_ge(S("pair_free%d" % p), k)

        def freed(ins, key):
            ins.then_inc(S("pair_free%d" % plan[key][0]), 1)

        def buf(key):
            return pair(plan[key][0])

        def heads_T(t, tt):
            return slice(4 * t, 4 * t + 4), slice(P * tt, P * (tt + 1))

        free0 = o_XT2 + 2048
        b_qT, _ = carve(2, KC, T, on=o_XT)
        b_kT, _ = carve(2, KC, T, on=free0)
        b_v, _ = carve(NT, D, on=free0 + 4096)
        b_acc, _ = carve(DIL, NT, HEADS, HD, on=free0 + 6144)
        b_z, _ = carve(NT, D, on=free0 + 12288)
        b_p, _ = carve(4, 384, on=free0 + 14336)
        b_pT, _ = carve(2, 4, 384, on=free0 + 15872)
        b_t2, _ = carve(NT, W, on=free0 + 18944)
        b_rope, _ = carve(2, NT, W, on=free0 + 19968)
        b_nm, _ = carve(DIL, NT, HEADS, on=o_sm)
        b_s, _ = carve(DIL, NT, HEADS, on=o_sm + 96)
        b_e, _ = carve(DIL, NT, HEADS, on=o_sm + 192)
        b_q, _ = carve(NT, HEADS, on=o_sm + 288)
        a_v, _ = carve(NT, 2048, on=free0)
        a_u, _ = carve(NT, 2048, on=free0 + 4096)
        a_z, _ = carve(NT, 2048, on=free0 + 8192)
        a_ws, _ = carve(KC, P, on=free0 + 12288)
        a_wsT, _ = carve(KC, P, on=free0 + 13312)
        a_tri, _ = carve(P, on=free0 + 14336)
        a_bs, _ = carve(KC, on=free0 + 14336 + P)
        a_bsr = arena[0:KC, free0 + 14600:free0 + 14600 + P]
        y2, _ = carve(NT, D, on=free0 + 6144)
        xt2_hi = single_pass("xt2_hi", KC, T, on=o_XT2)
        xt2_lo = single_pass("xt2_lo", KC, T, on=free0 + 22016)
        yt_hi = single_pass("yt_hi", 16, T, on=o_XT)
        yt_lo = single_pass("yt_lo", 16, T, on=free0)
        ot_hi = single_pass("ot_hi", KC, T, on=o_XT)
        ot_lo = single_pass("ot_lo", KC, T, on=o_XT + KC * T)
        w_hi2 = [single_pass("w_hi2_%d" % i, UC, W, on=(RING2 + i - RING) * UC * W) for i in range(2)]
        w_hi2.append(single_pass("w_hi2_2", UC, W, on=free0 + 24064))
        w_lo2 = single_pass("w_lo2", RING2, UC, W)
        ut_lo = [single_pass("ut_lo_lat", KC, T, on=o_x), single_pass("ut_lo_ctx", KC, T, on=o_cn)]
        rt_lo = single_pass("rt_lo", 16, T, on=o_qT)
        cv_lo = single_pass("cv_lo", KC, T, on=o_tmp)
        s_parts = single_pass("s_parts", KC, 4, 32, on=o_kT)
        pick, _ = carve(2, P, on=o_kT + 1024)
        mod_rows, _ = carve(2, W, on=o_qT)
        xe_hi = single_pass("xe_hi", KC, SLOTS, on=free0)
        xe_lo = single_pass("xe_lo", KC, SLOTS, on=free0 + 10240)
        sge, _ = carve(FF, on=free0 + 1024)
        he, _ = carve(FF, on=free0 + 1536)
        heT_hi = single_pass("heT_hi", FF // P, SLOTS, on=free0 + 2048)
        heT_lo = single_pass("heT_lo", FF // P, SLOTS, on=free0 + 11264)
        ye_hi = single_pass("ye_hi", D, on=free0 + 2560)
        ye_lo = single_pass("ye_lo", D, on=free0 + 5008)
        slot_weight, _ = carve(2, on=free0 + 21150)
        weighted, _ = carve(T, on=free0 + 21154)
        w_hi = single_pass("w_hi", HI, UC, W, on=free0 + 15000)
        w_lo = single_pass("w_lo", RING, UC, W)
        assert free0 + 15000 + HI * UC * W <= o_S
        sel = nc.alloc_sbuf_tensor_at("sel", [P, NT, SLOTS], BF16, offset=ARENA_AT + 4 * (free0 + 3584))
        h_parts = [nc.alloc_sbuf_tensor_at("h_part%d" % i, [P, NT, D], BF16, offset=ARENA_AT + 4 * (free0 + 11776 + 1024 * i)) for i in range(3)]
        h_rest, _ = carve(NT, D, on=free0 + 15000)
        selw, _ = carve(NT, SLOTS, on=free0 + 3840)
        selT = single_pass("selT", T, on=free0 + 4096)
        iota, _ = carve(T, on=free0 + 4352)
        before, _ = carve(P, on=free0 + 4608)
        ones, _ = carve(P, on=free0 + 4736)
        hits, _ = carve(NT, NE, on=free0 + 4864)
        slot_of, _ = carve(NT, NE, on=free0 + 4928)
        most, _ = carve(2, on=free0 + 4992)
        flag_f = arena[0:1, free0 + 5000:free0 + 5001]
        comb, _ = carve(NT, NE, on=free0 + 6144)
        rt, o_rt = carve(1024, on=free0 + 6300)
        h_tok, _ = carve(NT, D, on=free0 + 8192)
        assert free0 + 8192 + 2048 <= o_v + 4096

        norm_eps = [LN_EPS] * H + [LN_EPS, LN_EPS, LN_EPS, RMS_EPS, LN_EPS, RMS_EPS, RMS_EPS, RMS_EPS]

        OFF = {"": 0, "_b": NE}
        MOE_NORM = H + 2

        block = ctx.enter_context(nc.Block())

        @block.sync
        def _(sp):
            names = ["c_rows", "c_rope1", "c_rope2", "c_dist_f", "c_dist_b", "c_log", "c_mask"]
            views = [row_fb, rope1, rope2, dist_f, dist_b, log_c, amask]
            sp.dma_start(ident, a["c_ident"]).then_inc(S("load_ident"), 16)
            sp.dma_start(rows16[0:8], a["c"].rearrange("o (k p) -> (o k) p", p=P)).then_inc(S("load_rows"), 16)
            sp.dma_start(rows16[8:16], a["c_ctx"].rearrange("(k p) -> k p", p=P)).then_inc(S("load_rows"), 16)
            sp.dma_start(rows32[0:TAPS], a["conv_dw"][0]).then_inc(S("load_rows"), 16)
            sp.dma_start(rows32[TAPS:32], a["conv_dw_b"]).then_inc(S("load_rows"), 16)
            sp.dma_start(lg[:, 0:H], a["ret_decay_fwd"].broadcast_to([P, H])).then_inc(S("load_decays"), 16)
            sp.dma_start(lg[:, H:2 * H], a["ret_decay_bwd"].broadcast_to([P, H])).then_inc(S("load_decays"), 16)
            sp.dma_start(pick, a["c_pick"]).then_inc(S("load_pick"), 16)
            sp.dma_start(pos, a["c_pos"]).then_inc(S("load_pos"), 16)

            def unit(n, src):
                if n >= RING2:
                    sp.wait_ge(S("unit_done"), n - RING2 + 1 if n < first["a"] else max(first["a"], n - RING2 + 1))
                k = slots_of[n]
                sp.dma_start(ring[:, k], src.rearrange("(k p) c -> p k c", p=P)).then_inc(S("w_full%d" % k), 16)

            def rows_for(n):
                for r in row_after.get(n, []):
                    if r >= AUXN:
                        sp.wait_ge(S("row_used"), r - AUXN + 1)
                    sp.dma_start(aux[:, r % AUXN, :], rows[r].broadcast_to([P, W])).then_inc(S("row_full%d" % (r % AUXN)), 16)

            for n in range(n_before):
                unit(n, units[n])
                rows_for(n)
                if n == end_of("v", 3) + RING2:
                    sp.wait_ge(S("unit_done"), end_of("v", 3))
                    for name, v in list(zip(names, views))[3:]:
                        sp.dma_start(v, a[name]).then_inc(S("load_" + name), 16)
                if n == end_of("g", 3) + RING2:
                    sp.wait_ge(S("ret_scored"), 4)
                    sp.dma_start(pick, a["c_pick"]).then_inc(S("load_pick"), 16)
                if n == end_of("gate", 3) + RING2:
                    sp.wait_ge(S("unit_done"), end_of("gate", 3))
                    sp.dma_start(x, a["x"][0].rearrange("(t p) c -> p t c", p=P)).then_inc(S("load_x"), 16)
                if n == n_before - 1:
                    sp.wait_ge(S("unit_done"), end_of("conv", 1))
                    sp.wait_ge(S("mT_turned"), 2)
                    sp.dma_start(iota, a["c_iota"]).then_inc(S("load_iota"), 16)
                    sp.dma_start(before, a["c_before"]).then_inc(S("load_before"), 16)
                if n == 3:
                    sp.dma_start(x, a["x"][0].rearrange("(t p) c -> p t c", p=P)).then_inc(S("load_x"), 16)
                    sp.dma_start(x_ctx, a["ctx"][0].rearrange("(t p) c -> p t c", p=P)).then_inc(S("load_ctx"), 16)
                    for name, v in list(zip(names, views))[:3]:
                        sp.dma_start(v, a[name]).then_inc(S("load_" + name), 16)
                    sp.dma_start(wr[:, :, 0:NG], a["w_router_grp"][0].rearrange("(k p) g -> p k g", p=P)).then_inc(S("load_router_w"), 16)
                    sp.dma_start(wr[:, :, NG:36], a["w_router_exp"][0].rearrange("(k p) g -> p k g", p=P)).then_inc(S("load_router_w"), 16)
                    sp.dma_start(br[:, 0:NG], a["b_router_grp"].broadcast_to([P, NG])).then_inc(S("load_router_b"), 16)
                    sp.dma_start(br[:, NG:36], a["b_router_exp"].broadcast_to([P, NE])).then_inc(S("load_router_b"), 16)

            def expert_units(r, e, waits):
                for n, kind in enumerate(("gate", "gate", "up", "up", "down", "down")):
                    sp.wait_ge(S("unit_done" + r), waits(n))
                    sp.dma_start(ring[:, n], moe_src(kind, e, n % 2)).then_inc(S("w_full%d%s" % (n, r)), 16)
            expert_units("", 0, lambda n: n_before - RING2 + n + 1 if n < RING2 else n_before)
            with sp.Fori(1, NE) as e:
                expert_units("", e, lambda n: e * 6 + (n_before - RING + n + 1))
            sp.wait_ge(S("flag_set"), 1)
            more = sp.value_load(flag[0:1, 0:1], min_val=0, max_val=1)
            with sp.If(more > 0):
                sp.wait_ge(S("unit_done"), n_before + n_moe)
                for j, kind in enumerate(("gate", "gate", "up", "up", "down", "down")):
                    sp.dma_start(ring[:, j], moe_src(kind, 0, j % 2)).then_inc(S("w_full%d_b" % j), 16)
                with sp.Fori(1, NE) as e:
                    expert_units("_b", e, lambda n: e * 6 + (n - RING + 1))
                sp.wait_ge(S("unit_done_b"), n_moe)

            for n in range(n_before + n_moe, len(units)):
                if n == first["a"]:
                    sp.wait_ge(S("unit_done"), n)
                    sp.dma_start(a_ws, a["a_w_s_2"][0].rearrange("g t s -> t g s")).then_inc(S("load_ws"), 16)
                    sp.dma_start(a_tri, a["c_tri"]).then_inc(S("load_tri"), 16)
                    sp.dma_start(a_bsr, a["a_b_s_2"][0]).then_inc(S("load_bs"), 16)
                unit(n, units[n])
                rows_for(n)
            sp.wait_ge(S("out_ready"), 1)
            sp.dma_start(out[0].rearrange("(t p) c -> p t c", p=P), x).then_inc(S("stored"), 16)
            sp.wait_ge(S("stored"), 16)

        @block.tensor
        def _(pe):
            def claim(key):
                p, k = plan[key]
                if k > 1:
                    pe.wait_ge(S("pair_free%d" % p), k - 1)
                return pair(p)

            def gemm_parts(name, t, key, hi, lo, nk=2):
                o = claim(key)
                for j in range(nk):
                    n = first[name] + nk * t + j
                    m, w = part_of(n)
                    pe.wait_ge(S("w_hi_full"), m + 1)
                    for tt in range(NT):
                        for c in range(UC):
                            x_ = slice(P * tt, P * (tt + 1))
                            pe.matmul(o[:, tt, :], hi[:, UC * j + c, x_], w[:, c, :], start=(j == 0 and c == 0), stop=False)
                            pe.matmul(o[:, tt, :], lo[:, UC * j + c, x_], w[:, c, :], start=False, stop=False)
                    remainder_ready(pe, n)
                    for tt in range(NT):
                        for c in range(UC):
                            x_ = slice(P * tt, P * (tt + 1))
                            mm = pe.matmul(o[:, tt, :], hi[:, UC * j + c, x_], w_lo2[:, slots_of[n], c, :],
                                           start=False, stop=(j == nk - 1 and c == UC - 1))
                    mm.then_inc(S("unit_done"), 1)

            def xt2(k, tt):
                return XT2[:, k, P * tt:P * (tt + 1)]

            def turn(key, src, sem, value=1):
                o = claim(key)
                for tt in range(NT):
                    for j in range(4):
                        mm = pe.transpose(o[:, tt, P * j:P * (j + 1)], src(tt, j), ident)
                mm.then_inc(S(sem), 1)

            pe.wait_ge(S("load_ident"), 16)
            pe.wait_ge(S("load_rows"), 64)
            o = claim("turn_rows")
            pe.transpose(o[:, 0, 0:16], rows16, ident[0:16, 0:16])
            for k in range(KC):
                mm = pe.transpose(o[:, 1, 32 * k:32 * (k + 1)], rows32[:, P * k:P * (k + 1)], ident[0:32, 0:32])
            mm.then_inc(S("rows_turned"), 1)
            def row_products(name, t, i):
                o = claim((name, t))
                for j in range(2):
                    n = first[name] + 2 * t + j
                    m, w = part_of(n)
                    pe.wait_ge(S("w_hi_full"), m + 1)
                    for c in range(UC):
                        pe.matmul(o[:, 0, :], s_parts[:, UC * j + c].rearrange("p a b -> p (a b)"), w[:, c, :], start=(j == 0 and c == 0), stop=False)
                    remainder_ready(pe, n)
                    for c in range(UC):
                        mm = pe.matmul(o[:, 0, :], s_parts[:, UC * j + c].rearrange("p a b -> p (a b)"), w_lo2[:, slots_of[n], c, :],
                                       start=False, stop=(j == 1 and c == UC - 1))
                    mm.then_inc(S("unit_done"), 1)

            def spread_rows(name, t, i):
                pe.wait_ge(S("mod_rows"), i + 1)
                o = buf((name, t))
                if name == "ada":
                    pe.matmul(o[:, 0, :], pick[:, 1, :], mod_rows[:, i % 2, :], start=True, stop=True)
                pe.matmul(o[:, 1, :], pick[:, 0, :], mod_rows[:, i % 2, :], start=True, stop=True).then_inc(S("mod_spread"), 1)

            pe.wait_ge(S("s_ready"), 1)
            pe.wait_ge(S("load_pick"), 16)
            for t in range(4):
                row_products("ada", t, t)
                if t:
                    spread_rows("ada", t - 1, t - 1)
            spread_rows("ada", 3, 3)
            for s in range(2):
                pe.wait_ge(S("u_ready"), s + 1)
                src = (u_lat, u_ctx)[s]
                for c in range(2):
                    turn(("uT", s, c), lambda tt, j: src[:, tt, W * c + P * j:W * c + P * (j + 1)], "uT_turned")
            pair_evacuated(pe, ("uT", 0, 0))
            pair_evacuated(pe, ("uT", 0, 1))
            for t in range(3):
                gemm_parts("glu", t, ("glu", t), yt_hi, ut_lo[0])

            def turn_z(i):
                pe.wait_ge(S("z_ready"), i + 1)
                turn(("zT", i), lambda tt, j: z_tok[:, i, tt, P * j:P * (j + 1)], "zT_turned")
            turn_z(0)
            gemm_parts("glu", 3, ("glu", 3), yt_hi, ut_lo[0])
            pair_evacuated(pe, ("uT", 1, 0))
            pair_evacuated(pe, ("uT", 1, 1))

            def gemm_both(name, t):
                o = [None, None]
                for j in range(2):
                    n = first[name] + 2 * t + j
                    m, w = part_of(n)
                    pe.wait_ge(S("w_hi_full"), m + 1)
                    for s in range(2):
                        if j == 0:
                            o[s] = claim("%s_%s%d" % (name, ("lat", "ctx")[s], t))
                        for tt in range(NT):
                            x_ = slice(P * tt, P * (tt + 1))
                            for c in range(UC):
                                k = UC * j + c
                                pe.matmul(o[s][:, tt, :], yt_hi[:, 8 * s + k, x_], w[:, c, :], start=(j == 0 and c == 0), stop=False)
                                pe.matmul(o[s][:, tt, :], ut_lo[s][:, k, x_], w[:, c, :], start=False, stop=False)
                        if s == 0:
                            remainder_ready(pe, n)
                        for tt in range(NT):
                            x_ = slice(P * tt, P * (tt + 1))
                            for c in range(UC):
                                mm = pe.matmul(o[s][:, tt, :], yt_hi[:, 8 * s + UC * j + c, x_], w_lo2[:, slots_of[n], c, :],
                                               start=False, stop=(j == 1 and c == UC - 1))
                        if s == 1:
                            mm.then_inc(S("unit_done"), 1)
                        elif j == 1:
                            mm.then_inc(S("lat_done"), 1)

            def turn_roped(sem, t, key):
                pe.wait_ge(S(sem), t + 1)
                turn(key, lambda tt, j: roped[:, t, tt, P * j:P * (j + 1)], "heads_turned")

            gemm_both("k", 0)
            turn_z(1)
            gemm_both("k", 1)
            turn_roped("k_roped", 0, ("kT", 0))
            gemm_both("v", 0)
            turn_roped("k_roped", 1, ("kT", 1))
            for t in range(1, 4):
                gemm_both("v", t)
            for t in range(2):
                gemm_parts("q", t, ("q", t), yt_hi, ut_lo[0])
            for t in range(2):
                turn_roped("q_roped", t, ("qT", t))
            for i in range(4):
                o = claim(("S", i))
                for h in (2 * i, 2 * i + 1):
                    pe.wait_ge(S("k_decayed"), h + 1)
                    kd = tmp[:, h % 2, :].rearrange("p (t d n) -> p t d n", t=NT, d=2)
                    for d in range(2):
                        for tt in range(NT):
                            mm = pe.matmul(o[:, h % 2, DV * d:DV * (d + 1)], kd[:, tt, d, :],
                                           v_ctx[:, tt, DV * h:DV * (h + 1)], start=(tt == 0), stop=(tt == NT - 1))
                    mm.then_inc(S("state_done"), 1)
            pe.wait_ge(S("conv_done"), 1)
            for c in range(2):
                turn(("cz", c), lambda tt, j: conv[:, 4 * c + j, P * tt:P * (tt + 1)], "cz_turned")

            def ret_scores(i):
                o = claim(("sc", i))
                for h in (2 * i, 2 * i + 1):
                    for mt in range(NT):
                        mm = pe.matmul(o[:, h % 2, T * mt:T * (mt + 1)], kT[:, h, P * mt:P * (mt + 1)], qT[:, h, :],
                                       start=True, stop=True)
                mm.then_inc(S("ret_scored"), 1)

            def ret_values(i):
                o = claim(("av", i))
                for h in (2 * i, 2 * i + 1):
                    pe.wait_ge(S("ret_masked"), h + 1)
                    A = tmp[:, h % 2, :].rearrange("p (m n) -> p m n", m=NT)
                    Q = tmp[:, 4 + h % 2, :].rearrange("p (d n) -> p d n", d=2)
                    for nt in range(NT):
                        for mt in range(NT):
                            pe.matmul(o[:, h % 2, DV * nt:DV * (nt + 1)], A[:, mt, P * nt:P * (nt + 1)],
                                      v_lat[:, mt, DV * h:DV * (h + 1)], start=(mt == 0), stop=False)
                        for d in range(2):
                            mm = pe.matmul(o[:, h % 2, DV * nt:DV * (nt + 1)], Q[:, d, P * nt:P * (nt + 1)],
                                           state[:, h, d, :], start=False, stop=(d == 1))
                    mm.then_inc(S("ret_summed"), 1)

            for i in range(4):
                pair_evacuated(pe, ("S", i))
            pair_evacuated(pe, ("kT", 0))
            pair_evacuated(pe, ("kT", 1))
            pair_evacuated(pe, ("qT", 0))
            pair_evacuated(pe, ("qT", 1))
            ret_scores(0)
            for i in range(4):
                gemm_parts("g", i, ("g", i), yt_hi, ut_lo[0])
                ret_values(i)
                if i < 3:
                    ret_scores(i + 1)
            for t in range(4):
                gemm_parts("gate", t, ("gate", t), yt_hi, ut_lo[0])
            pe.wait_ge(S("s_ready"), 2)
            pe.wait_ge(S("load_pick"), 32)
            for t in range(8):
                row_products("ada_tail", t, 4 + t)
                if t:
                    spread_rows("ada_tail", t - 1, 3 + t)
            spread_rows("ada_tail", 7, 11)
            pe.wait_ge(S("ret_ready"), 2)
            for c in range(4):
                turn(("retT", c), lambda tt, j: sg[:, tt, W * c + P * j:W * c + P * (j + 1)], "retT_turned")
            pe.wait_ge(S("cz_ready"), 1)
            for c in range(2):
                turn(("cvT", c), lambda tt, j: cz[:, tt, W * c + P * j:W * c + P * (j + 1)], "cvT_turned")
            for c in range(4):
                pair_evacuated(pe, ("retT", c))
            for t in range(2):
                gemm_parts("ret", t, ("ret", t), yt_hi, rt_lo, nk=4)
            for c in range(2):
                pair_evacuated(pe, ("cvT", c))
            for t in range(2):
                gemm_parts("conv", t, ("conv", t), xt2_hi, cv_lo)
            pe.wait_ge(S("merged"), 1)
            for c in range(2):
                turn(("mT", c), lambda tt, j: cz[:, tt, W * c + P * j:W * c + P * (j + 1)], "mT_turned")
            for c in range(2):
                pair_evacuated(pe, ("mT", c))
            for t in range(2):
                gemm_parts("mix", t, ("mix", t), ot_hi, ot_lo)
            pe.wait_ge(S("h_ready"), 1)
            for c in range(2):
                turn(("eT", c), lambda tt, j: h_tok[:, tt, W * c + P * j:W * c + P * (j + 1)], "eT_turned")
            for c in range(2):
                pair_evacuated(pe, ("eT", c))
            pe.wait_ge(S("load_router_w"), 32)
            o = claim("router")
            for tt in range(NT):
                for k in range(KC):
                    mm = pe.matmul(o[:, tt, 0:36], xt2(k, tt), wr[:, k, :], start=(k == 0), stop=(k == KC - 1))
            mm.then_inc(S("routed"), 1)

            pe.wait_ge(S("load_before"), 16)
            pe.wait_ge(S("hits_ready"), 1)
            o = claim(("rank", 0))
            pe.matmul(o[:, 0, 0:NE], before, hits[:, 0, :], start=True, stop=True)
            pe.matmul(o[:, 1, 0:NE], ones, hits[:, 0, :], start=True, stop=False)
            pe.matmul(o[:, 1, 0:NE], before, hits[:, 1, :], start=False, stop=True).then_inc(S("ranked"), 1)
            pe.wait_ge(S("most_ready"), 1)
            pe.transpose(ps[0:1, 2 * plan["most"][0], 0:P], most[:, 0:1], ident).then_inc(S("most_turned"), 1)

            y = [claim("moe_y0"), claim("moe_y1")]

            def wide_product(bank, lhs_hi, lhs_lo, n, base, e, r, begin, end, rest=None):
                pe.wait_ge(S("hi_ready"), (e + OFF[r]) * 6 + (n + 1))
                for c in range(UC):
                    pe.matmul(ps[:, bank, :], lhs_hi(c), w_hi[:, n % HI, c, :], start=(begin and c == 0), stop=False)
                if rest:
                    pe.wait_ge(S(rest), (e + OFF[r]) + 1)
                for c in range(UC):
                    pe.matmul(ps[:, bank, :], lhs_lo(c), w_hi[:, n % HI, c, :], start=False, stop=False)
                if n in POOL_UNITS:
                    pe.wait_ge(S("pool_lo"), (e + OFF[r]) * len(POOL_UNITS) + (POOL_UNITS.index(n) + 1))
                else:
                    pe.wait_ge(S("dve_lo"), (e + OFF[r]) * len(DVE_UNITS) + (DVE_UNITS.index(n) + 1))
                for c in range(UC):
                    mm = pe.matmul(ps[:, bank, :], lhs_hi(c), w_lo[:, n, c, :], start=False, stop=(end and c == UC - 1))
                mm.then_inc(S("unit_done" + r), 1)

            def xe_part(part, j):
                return lambda c: part[:, UC * j + c, :]

            def gather(half, e, r):
                for k in range(4):
                    for i, part in enumerate(h_parts):
                        for tt in range(NT):
                            mm = pe.matmul(ps[:, (2, 0)[half], P * k:P * (k + 1)],
                                           part[:, tt, P * (4 * half + k):P * (4 * half + k + 1)], sel[:, tt, :],
                                           start=(i == 0 and tt == 0), stop=(i == 2 and tt == NT - 1))
                mm.then_inc(S("gathered%d" % half), 1)

            def turn_selection(r):
                for tt in range(NT):
                    mm = pe.transpose(ps[:, 3, P * tt:P * (tt + 1)], selw[:, tt, :], ident)
                mm.then_inc(S("sel_turned"), 1)

            def scatter(begin, r):
                for tt in range(NT):
                    for j in range(2):
                        pe.matmul(y[tt][:, j, :], selT[:, P * tt:P * (tt + 1)], ye_hi[:, W * j:W * (j + 1)],
                                  start=begin, stop=False, skip_group_check=True)
                        mm = pe.matmul(y[tt][:, j, :], selT[:, P * tt:P * (tt + 1)], ye_lo[:, W * j:W * (j + 1)],
                                       start=False, stop=False, skip_group_check=True)
                mm.then_inc(S("scattered"), 1)

            def expert(e, base, r, head, tail, begin):
                pe.wait_ge(S("xe0"), (e + OFF[r]) + 1)
                pe.wait_ge(S("xe1"), (e + OFF[r]) + 1)
                for j in range(2):
                    wide_product(0, xe_part(xe_hi, j), xe_part(xe_lo, j), j, base, e, r, j == 0, j == 1)
                if not head:
                    pe.wait_ge(S("ye_hi"), (e + OFF[r]) * 2)
                    pe.wait_ge(S("ye_lo"), (e + OFF[r]) * 2)
                    pe.wait_ge(S("selT"), (e + OFF[r]))
                    scatter(begin, r)
                for j in range(2):
                    wide_product(1, xe_part(xe_hi, j), xe_part(xe_lo, j), 2 + j, base, e, r, j == 0, j == 1)
                if not tail:
                    pe.wait_ge(S("sel_ready"), (e + OFF[r]) + 2)
                    gather(0, e, r)
                pe.wait_ge(S("selT"), (e + OFF[r]) + 1)
                pe.wait_ge(S("slot_weight"), (e + OFF[r]) + 1)
                pe.wait_ge(S("act_ready"), (e + OFF[r]) + 1)
                for j in range(FF // P):
                    mm = pe.transpose(ps[:, 3, P * j:P * (j + 1)], he[:, P * j:P * (j + 1)], ident)
                mm.then_inc(S("h_turned"), 1)
                if not tail:
                    pe.wait_ge(S("silu"), (e + OFF[r]) + 1)
                    gather(1, e, r)
                pe.wait_ge(S("hT"), (e + OFF[r]) + 1)
                wide_product(1, lambda c: heT_hi[:, c, :], lambda c: heT_lo[:, c, :], 4, base, e, r, True, True, "hT_lo")
                if not tail:
                    pe.wait_ge(S("xe0"), (e + OFF[r]) + 2)
                wide_product(2, lambda c: heT_hi[:, c, :], lambda c: heT_lo[:, c, :], 5, base, e, r, True, True)
                if not tail:
                    pe.wait_ge(S("selw_ready"), (e + OFF[r]) + 2)
                    turn_selection(r)

            def experts(base, r, first_round):
                pe.wait_ge(S("sel_ready"), 1 + OFF[r])
                gather(0, 0, r)
                gather(1, 0, r)
                pe.wait_ge(S("selw_ready"), 1 + OFF[r])
                turn_selection(r)
                expert(0, base, r, True, False, False)
                expert(1, base, r, False, False, first_round)
                with pe.Fori(2, NE - 1) as e:
                    expert(e, base, r, False, False, False)
                expert(NE - 1, base, r, False, True, False)
                pe.wait_ge(S("ye_hi"), 2 * (NE + OFF[r]))
                pe.wait_ge(S("ye_lo"), 2 * (NE + OFF[r]))
                pe.wait_ge(S("selT"), (NE + OFF[r]))
                scatter(False, r)

            pe.wait_ge(S("h_left"), 2)
            pe.wait_ge(S("flag_set"), 1)
            pe.wait_ge(S("pair_free0"), entry0)
            pe.wait_ge(S("pair_free1"), entry1)
            experts(n_before, "", True)
            more = pe.value_load(flag[0:1, 0:1], min_val=0, max_val=1)
            with pe.If(more > 0):
                experts(0, "_b", False)

            pe.wait_ge(S("a_in_ready"), 1)
            for c in range(2):
                turn(("aT", c), lambda tt, j: h_tok[:, tt, W * c + P * j:W * c + P * (j + 1)], "aT_turned")
            for c in range(2):
                pair_evacuated(pe, ("aT", c))
            for t in range(8):
                gemm_parts("a", t, ("a", t), xt2_hi, xt2_lo)
            pe.wait_ge(S("load_ws"), 16)
            pe.wait_ge(S("load_bs"), 16)
            for c in range(2):
                o = claim(("wsT", c))
                for j in range(4):
                    mm = pe.transpose(o[:, 0, P * j:P * (j + 1)], a_ws[:, 4 * c + j, :], ident)
                if c == 1:
                    mm = pe.transpose(o[:, 1, 0:KC], a_bsr, ident[0:KC, 0:KC])
                mm.then_inc(S("wsT_turned"), 1)
            pe.wait_ge(S("wsT_ready"), 2)
            pe.wait_ge(S("v_normed"), 1)
            for i in range(4):
                o = claim(("sv", i))
                for tt in range(NT):
                    for g in (2 * i, 2 * i + 1):
                        mm = pe.matmul(o[:, tt, 256 * (g % 2):256 * (g % 2 + 1)], a_wsT[:, g, :],
                                       a_v[:, tt, 256 * g:256 * (g + 1)], start=True, stop=True)
                mm.then_inc(S("sv_done"), 1)
            for t in range(8, 12):
                gemm_parts("a", t, ("a", t), xt2_hi, xt2_lo)
            for c in range(4):
                pe.wait_ge(S("y_gated"), c + 1)
                turn(("yT", c), lambda tt, j: a_z[:, tt, W * c + P * j:W * c + P * (j + 1)], "yT_turned")
            for c in range(4):
                pair_evacuated(pe, ("yT", c))
            for t in range(2):
                gemm_parts("a_out", t, ("a_out", t), yt_hi, yt_lo, nk=4)

            pe.wait_ge(S("b_in_ready"), 1)
            for c in range(2):
                turn(("bT", c), lambda tt, j: y2[:, tt, W * c + P * j:W * c + P * (j + 1)], "bT_turned")
            for c in range(2):
                pair_evacuated(pe, ("bT", c))
            n_rope = 0
            for t in range(20):
                gemm_parts("b", t, ("b", t), xt2_hi, xt2_lo)
                if t and BKIND[t - 1] in "qk":
                    n_rope += 1
                    pe.wait_ge(S("b_roped"), n_rope)
                    turn(("bqk", t - 1), lambda tt, j: b_rope[:, (n_rope - 1) % 2, tt, P * j:P * (j + 1)], "b_turned")
                for act, g, c in slots[t]:
                    if act == "scores":
                        if c == 0:
                            for key in [("bqk", tq) for tq in range(20) if BKIND[tq] in "qk" and BGROUP[tq] == g]:
                                pair_evacuated(pe, key)
                        for i in range(2):
                            o = claim((act, g, c, i))
                            for hh in range(2):
                                h = 4 * c + 2 * i + hh
                                r = slice(HD * (h % 2), HD * (h % 2) + HD)
                                for tt in range(NT):
                                    n = P * (tt + 1)
                                    mm = pe.matmul(o[:, hh, P * tt:P * tt + n], b_qT[r, g % 2, h // 2, P * tt:P * (tt + 1)],
                                                   b_kT[r, g % 2, h // 2, 0:n], start=True, stop=True)
                            mm.then_inc(S("b_scored"), 1)
                    elif act == "turn":
                        pe.wait_ge(S("b_probs"), 4 * (4 * g + c) + 4)
                        for i in range(2):
                            o = claim((act, g, c, i))
                            for hh in range(2):
                                for s in range(3):
                                    mm = pe.transpose(o[:, hh, P * s:P * (s + 1)], b_p[:, 2 * i + hh, P * s:P * (s + 1)], ident)
                            mm.then_inc(S("b_p_turned"), 1)
                    else:
                        for i in range(2):
                            pair_evacuated(pe, ("turn", g, c, i))
                        if c == 0:
                            for tv in range(20):
                                if BKIND[tv] == "v" and BGROUP[tv] == g:
                                    pair_evacuated(pe, ("b", tv))
                        o = claim((act, g, c))
                        for hh in range(4):
                            h = 4 * c + hh
                            pT = b_pT[:, c % 2, hh, :]
                            cols = slice(HD * h, HD * (h + 1))
                            pe.matmul(o[:, 0, HD * hh:HD * (hh + 1)], pT[:, 0:P], b_v[:, 0, cols], start=True, stop=True)
                            pe.matmul(o[:, 1, HD * hh:HD * (hh + 1)], pT[:, P:2 * P], b_v[:, 0, cols], start=True, stop=False)
                            mm = pe.matmul(o[:, 1, HD * hh:HD * (hh + 1)], pT[:, 2 * P:3 * P], b_v[:, 1, cols], start=False, stop=True)
                        mm.then_inc(S("b_valued"), 1)
            pe.wait_ge(S("b_o_ready"), 1)
            for c in range(2):
                turn(("oT", c), lambda tt, j: b_z[:, tt, W * c + P * j:W * c + P * (j + 1)], "oT_turned")
            for c in range(2):
                pair_evacuated(pe, ("oT", c))
            for t in range(2):
                gemm_parts("b_out", t, ("b_out", t), ot_hi, ot_lo)

        @block.vector
        def _(dve):
            chain = [0]

            def link(ins):
                chain[0] += 1
                ins.then_inc(S("dve_step"), 1)

            def settle():
                dve.wait_ge(S("dve_step"), chain[0])

            def row_done(key=None):
                if key is None:
                    settle()
                else:
                    pair_evacuated(dve, key)
                dve.sem_inc(S("row_used"), 1)

            def free_pair(key):
                dve.sem_inc(S("pair_free%d" % plan[key][0]), 1)

            norms = [0]

            def power(eps):
                norms[0] += 1
                return norms[0]

            def row_stats(src, width):
                n = width // W
                for tt in range(NT):
                    for c in range(n):
                        link(dve.bn_stats(stats[:, tt, c, :], src(tt)[:, W * c:W * (c + 1)]))
                settle()
                for tt in range(NT):
                    ins = dve.bn_aggr(mv[:, tt, :], stats[:, tt, 0:n, :])
                    if tt == 1:
                        norms[0] += 1
                        ins.then_inc(S("stats_ready"), 1)
                    else:
                        link(ins)
                dve.wait_ge(S("rstd_ready"), norms[0])
                settle()

            def norm_gain_bias(v, g, b, chunks):
                for c in range(chunks):
                    cols = slice(W * c, W * (c + 1))
                    row = row_ready(dve, (g, c))
                    for tt in range(NT):
                        link(dve.scalar_tensor_tensor(v[:, tt, cols], v[:, tt, cols], mv[:, tt, 0:1], row, ALU.subtract, ALU.mult))
                    settle()
                    row_done()
                    row = row_ready(dve, (b, c))
                    for tt in range(NT):
                        link(dve.scalar_tensor_tensor(v[:, tt, cols], v[:, tt, cols], rstd[:, tt:tt + 1], row, ALU.mult, ALU.add))
                    settle()
                    row_done()

            def rms(src, dst, g, rows_key):
                for tt in range(NT):
                    for c in range(2):
                        link(dve.bn_stats(stats[:, tt, c, :], src[:, tt, W * c:W * (c + 1)]))
                settle()
                for tt in range(NT):
                    link(dve.bn_aggr(mv[:, tt, :], stats[:, tt, 0:2, :]))
                settle()
                link(dve.tensor_tensor(sq, mv[:, :, 0], mv[:, :, 0], ALU.mult))
                settle()
                norms[0] += 1
                dve.tensor_tensor(mv[:, :, 1], sq, mv[:, :, 1], ALU.add).then_inc(S("stats_ready"), 1)
                dve.wait_ge(S("rstd_ready"), norms[0])
                for c in range(2):
                    row = row_ready(dve, (rows_key, c))
                    cols = slice(W * c, W * (c + 1))
                    for tt in range(NT):
                        link(dve.scalar_tensor_tensor(dst[:, tt, cols], src[:, tt, cols], rstd[:, tt:tt + 1], row, ALU.mult, ALU.mult))
                    settle()
                    row_done()

            def biased(key, dst, wait_name, wait_value, free=True):
                dve.wait_ge(S(wait_name), wait_value)
                return dve.tensor_tensor(dst, buf(key), bc2(row_ready(dve, key)), ALU.add)

            dve.wait_ge(S("silu_c"), 1)
            def conditioning_parts():
                wide_s = [sT[:, KC * i:KC * (i + 1)].unsqueeze(2).broadcast_to([P, KC, 32]) for i in range(2)]
                for i in range(2):
                    link(dve.tensor_copy(s_parts[:, :, 2 * i, :], wide_s[i]))
                settle()
                link(dve.tensor_tensor(s_parts[:, :, 1, :], wide_s[0], s_parts[:, :, 0, :].bitcast(F32), ALU.subtract))
                dve.tensor_tensor(s_parts[:, :, 3, :], wide_s[1], s_parts[:, :, 2, :].bitcast(F32), ALU.subtract).then_inc(S("s_ready"), 1)
                dve.wait_ge(S("s_ready"), 1)
                settle()

            conditioning_parts()
            dve.wait_ge(S("load_decays"), 32)
            link(dve.tensor_scalar(la[:, 0, :], lg, -1.0, None, ALU.mult))
            settle()
            dve.tensor_tensor(la[:, 0, :], la[:, 0, :], lg, ALU.min).then_inc(S("neg_abs"), 1)
            dve.wait_ge(S("exp_abs"), 1)
            link(dve.tensor_scalar(la[:, 1, :], la[:, 0, :], 2.0, None, ALU.add))
            settle()
            link(dve.reciprocal(la[:, 1, :], la[:, 1, :]))
            settle()
            link(dve.tensor_tensor(la[:, 0, :], la[:, 0, :], la[:, 1, :], ALU.mult))
            settle()
            link(dve.tensor_tensor(la[:, 1, :], la[:, 0, :], la[:, 0, :], ALU.mult))
            settle()
            link(dve.tensor_scalar(la[:, 2, :], la[:, 1, :], 2.0 / 17, 2.0 / 15, ALU.mult, ALU.add))
            settle()
            for n in (13, 11, 9, 7, 5, 3, 1):
                link(dve.tensor_tensor(la[:, 2, :], la[:, 2, :], la[:, 1, :], ALU.mult))
                settle()
                link(dve.tensor_scalar(la[:, 2, :], la[:, 2, :], 2.0 / n, None, ALU.add))
                settle()
            link(dve.tensor_tensor(la[:, 2, :], la[:, 2, :], la[:, 0, :], ALU.mult))
            link(dve.tensor_scalar(lg, lg, 0.0, None, ALU.min))
            settle()
            link(dve.tensor_tensor(lg, lg, la[:, 2, :], ALU.subtract))
            settle()
            dve.wait_ge(S("load_pos"), 16)
            for d in range(2):
                for tt in range(NT):
                    ins = dve.tensor_scalar(wdec[:, d, tt, :], lg[:, H * d:H * (d + 1)], pos[:, d, tt:tt + 1], None, ALU.mult)
                    if d == 1 and tt == 1:
                        ins.then_inc(S("wdec_exps"), 1)
                    else:
                        link(ins)

            def rest_part(name, c, hi, lo, key=None, f=None):
                dve.wait_ge(S(name + "_hi"), c + 1)

                def part(v, f):
                    return v[:, f:f + 4, :].rearrange("p k (t n) -> p t k n", t=NT)
                key = key or (name, c)
                src = buf(key).rearrange("p t (k n) -> p t k n", k=4)
                freed(dve.tensor_tensor(part(lo, 4 * c if f is None else f), src, part(hi, 4 * c).bitcast(F32), ALU.subtract), key)

            def own_remainder(n):
                m, w = part_of(n)
                dve.wait_ge(S("w_hi_full"), m + 1)
                dve.tensor_tensor(w_lo2[:, slots_of[n]], ring[:, slots_of[n]], w[:, :, :].bitcast(F32), ALU.subtract).then_inc(S("w_lo_vector"), 1)

            own_remainder(end_of("ada", 0) - 1)
            for t in range(4):
                if t < 3:
                    own_remainder(end_of("ada", t + 1) - 1)
                row = row_ready(dve, ("ada", t))
                dve.wait_ge(S("mod_spread"), t + 1)
                p_ = buf(("ada", t))
                for m, dst in enumerate((mod_lat, mod_ctx)):
                    if t < 2:
                        ins = dve.tensor_tensor(dst[:, W * t:W * (t + 1)], p_[:, 1 - m, :], row, ALU.add)
                    else:
                        ins = dve.scalar_tensor_tensor(dst[:, W * t:W * (t + 1)], p_[:, 1 - m, :], 1.0, row, ALU.add, ALU.add)
                    if m == 0:
                        link(ins)
                    else:
                        freed(ins, ("ada", t))
                row_done(("ada", t))
            pair_evacuated(dve, ("ada", 2))
            pair_evacuated(dve, ("ada", 3))
            settle()
            for s, (src, dst, m) in enumerate(((x, u_lat, mod_lat), (x_ctx, u_ctx, mod_ctx))):
                dve.wait_ge(S(("load_x", "load_ctx")[s]), 16)
                link(dve.tensor_tensor(dst, src, m[:, D:2 * D].unsqueeze(1).broadcast_to([P, NT, D]), ALU.mult))
                settle()
                dve.tensor_tensor(dst, dst, m[:, 0:D].unsqueeze(1).broadcast_to([P, NT, D]), ALU.add).then_inc(S("u_ready"), 1)

            for n in range(4):
                rest_part("uT", n, yt_hi, ut_lo[n // 2], ("uT", n // 2, n % 2), 4 * (n % 2))

            link(dve.memset(z_pad[:, :, 0:PAD], 0.0))
            link(dve.memset(z_pad[:, :, PAD + T:T + 2 * PAD], 0.0))
            dve.wait_ge(S("wdec_exp"), 1)
            link(dve.tensor_scalar(wdec, wdec, DK ** -0.5, None, ALU.mult))

            for i in range(2):
                ins = biased(("glu", 2 * i), z_tok[:, i], "unit_done", end_of("glu", 2 * i))
                freed(ins, ("glu", 2 * i))
                row_done(("glu", 2 * i))
                ins = biased(("glu", 2 * i + 1), tmp[:, 2 * i:2 * i + 2, :], "unit_done", end_of("glu", 2 * i + 1))
                freed(ins, ("glu", 2 * i + 1))
                row_done(("glu", 2 * i + 1))
                dve.wait_ge(S("sig_z"), i + 1)
                pair_evacuated(dve, ("glu", 2 * i))
                dve.tensor_tensor(z_tok[:, i], z_tok[:, i], tmp[:, 2 * i:2 * i + 2, :], ALU.mult).then_inc(S("z_ready"), 1)

            taps_done = [0]

            def conv_taps(n):
                for _ in range(n):
                    j = taps_done[0]
                    if j == 0:
                        dve.wait_ge(S("pair_free%d" % plan[("zT", 0)][0]), plan[("zT", 0)][1])
                        dve.wait_ge(S("pair_free%d" % plan[("zT", 1)][0]), plan[("zT", 1)][1])
                        pair_evacuated(dve, "turn_rows")
                    settle()
                    for k in range(KC):
                        z = z_pad[:, k, j:j + T]
                        if j == 0:
                            link(dve.tensor_scalar(conv[:, k, :], z, cwT[:, k, 0:1], cwT[:, k, TAPS:TAPS + 1], ALU.mult, ALU.add))
                        elif j < TAPS - 1 or k < KC - 1:
                            link(dve.scalar_tensor_tensor(conv[:, k, :], z, cwT[:, k, j:j + 1], conv[:, k, :], ALU.mult, ALU.add))
                        else:
                            dve.scalar_tensor_tensor(conv[:, k, :], z, cwT[:, k, j:j + 1], conv[:, k, :], ALU.mult, ALU.add).then_inc(S("conv_done"), 1)
                    taps_done[0] += 1

            def rope_four(t, ready):
                for tt in range(NT):
                    s = tmp[:, tt, :].rearrange("p (h s d) -> p h s d", h=4, s=2)
                    r = roped[:, t, tt, :].rearrange("p (h s d) -> p h s d", h=4, s=2)
                    q = tmp[:, 2 + tt, :].rearrange("p (h s d) -> p h s d", h=4, s=2)
                    cos = rope1[:, 0, tt, :].unsqueeze(1).broadcast_to([P, 4, P])
                    link(dve.tensor_tensor(roped[:, t, tt, :].rearrange("p (h d) -> p h d", h=4),
                                           tmp[:, tt, :].rearrange("p (h d) -> p h d", h=4), cos, ALU.mult))
                    for s_ in range(2):
                        sin = rope1[:, 1, tt, 64 * s_:64 * (s_ + 1)].unsqueeze(1).broadcast_to([P, 4, 64])
                        link(dve.tensor_tensor(q[:, :, s_, :], s[:, :, 1 - s_, :], sin, ALU.mult))
                settle()
                for tt in range(NT):
                    ins = dve.tensor_tensor(roped[:, t, tt, :], roped[:, t, tt, :], tmp[:, 2 + tt, :], ALU.add)
                    if tt == 1:
                        ins.then_inc(S(ready), 1)
                    else:
                        link(ins)

            dve.wait_ge(S("load_c_rope1"), 16)
            for t in range(2):
                row = row_ready(dve, ("k", t))
                dve.wait_ge(S("lat_done"), t + 1)
                freed(dve.tensor_tensor(tmp[:, 0:2, :], buf("k_lat%d" % t), bc2(row), ALU.add), "k_lat%d" % t)
                pair_evacuated(dve, "k_lat%d" % t)
                rope_four(t, "k_roped")
                if t == 1:
                    conv_taps(4)
                dve.wait_ge(S("unit_done"), end_of("k", t))
                freed(dve.tensor_tensor(k_ctx[:, :, W * t:W * (t + 1)], buf("k_ctx%d" % t), bc2(row), ALU.add), "k_ctx%d" % t)
                row_done("k_ctx%d" % t)
            for t in range(4):
                row = row_ready(dve, ("v", t))
                dve.wait_ge(S("lat_done"), t + 3)
                freed(dve.tensor_tensor(v_lat[:, :, W * t:W * (t + 1)], buf("v_lat%d" % t), bc2(row), ALU.add), "v_lat%d" % t)
                dve.wait_ge(S("unit_done"), end_of("v", t))
                freed(dve.tensor_tensor(v_ctx[:, :, W * t:W * (t + 1)], buf("v_ctx%d" % t), bc2(row), ALU.add), "v_ctx%d" % t)
                row_done("v_ctx%d" % t)
                conv_taps(7 if t < 3 else 6)
            assert taps_done[0] == TAPS, taps_done
            for t in range(2):
                if t == 0:
                    dve.wait_ge(S("heads_turned"), 2)
                ins = biased(("q", t), tmp[:, 0:2, :], "unit_done", end_of("q", t))
                freed(ins, ("q", t))
                pair_evacuated(dve, ("q", t))
                row_done(("q", t))
                rope_four(t, "q_roped")
            pair_evacuated(dve, "k_ctx0")
            pair_evacuated(dve, "k_ctx1")
            for h in range(H):
                if h >= 2:
                    dve.wait_ge(S("state_done"), h - 1)
                kd = tmp[:, h % 2, :].rearrange("p (t d n) -> p t d n", t=NT, d=2)
                for tt in range(NT):
                    for d in range(2):
                        ins = dve.tensor_scalar(kd[:, tt, d, :], k_ctx[:, tt, DK * h:DK * (h + 1)], wdec[:, d, tt, h:h + 1], None, ALU.mult)
                        if tt == 1 and d == 1:
                            ins.then_inc(S("k_decayed"), 1)
                        else:
                            link(ins)

            def decay_exponents(h):
                E = tmp[:, 2 + h % 2, :]
                link(dve.scalar_tensor_tensor(E, dist_f.rearrange("p a b -> p (a b)"), lg[:, h:h + 1], log_c.rearrange("p a b -> p (a b)"), ALU.mult, ALU.add))
                settle()
                dve.scalar_tensor_tensor(E, dist_b.rearrange("p a b -> p (a b)"), lg[:, H + h:H + h + 1], E, ALU.mult, ALU.add).then_inc(S("ret_exps"), 1)

            def mask_scores(i):
                dve.wait_ge(S("ret_scored"), i + 1)
                for h in (2 * i, 2 * i + 1):
                    dve.wait_ge(S("ret_exped"), h + 1)
                    if h >= 2:
                        dve.wait_ge(S("ret_summed"), h - 1)
                    Q = tmp[:, 4 + h % 2, :].rearrange("p (d n) -> p d n", d=2)
                    link(dve.tensor_tensor(Q, Q, qT[:, h:h + 1, :].broadcast_to([P, 2, T]), ALU.mult))
                    settle()
                    dve.tensor_tensor(tmp[:, h % 2, :], buf(("sc", i))[:, h % 2, :], tmp[:, 2 + h % 2, :], ALU.mult).then_inc(S("ret_masked"), 1)
                dve.wait_ge(S("ret_masked"), 2 * i + 2)
                free_pair(("sc", i))

            def head_norm(i):
                o = buf(("av", i))
                for h in (2 * i, 2 * i + 1):
                    dve.wait_ge(S("ret_summed"), h + 1)
                    for tt in range(NT):
                        link(dve.bn_stats(stats[:, tt, 0, :], o[:, h % 2, DV * tt:DV * (tt + 1)]))
                    settle()
                    for tt in range(NT):
                        ins = dve.bn_aggr(mv[:, tt, :], stats[:, tt, 0:1, :])
                        if tt == 0:
                            link(ins)
                        else:
                            norms[0] += 1
                            ins.then_inc(S("stats_ready"), 1)
                    dve.wait_ge(S("rstd_ready"), norms[0])
                    settle()
                    dst = (o_lo, o_hi)[h // 4]
                    for tt in range(NT):
                        link(dve.tensor_scalar(dst[:, tt, DV * (h % 4):DV * (h % 4 + 1)], o[:, h % 2, DV * tt:DV * (tt + 1)],
                                               mv[:, tt, 0:1], rstd[:, tt:tt + 1], ALU.subtract, ALU.mult))
                settle()
                free_pair(("av", i))

            dve.wait_ge(S("state_done"), H)
            for name in ("load_c_dist_f", "load_c_dist_b", "load_c_log"):
                dve.wait_ge(S(name), 16)
            pair_evacuated(dve, ("qT", 0))
            pair_evacuated(dve, ("qT", 1))
            decay_exponents(0)
            decay_exponents(1)
            for i in range(4):
                mask_scores(i)
                if i < 3:
                    decay_exponents(2 * i + 2)
                    decay_exponents(2 * i + 3)
                ins = biased(("g", i), sg[:, :, W * i:W * (i + 1)], "unit_done", end_of("g", i))
                freed(ins, ("g", i))
                row_done(("g", i))
                head_norm(i)

            dve.wait_ge(S("silu_g"), 4)
            for half, src in ((0, o_lo), (1, o_hi)):
                v = sg[:, :, D * half:D * (half + 1)]
                dve.tensor_tensor(v, v, src, ALU.mult).then_inc(S("ret_ready"), 1)
            conditioning_parts()
            pair_evacuated(dve, ("cz", 0))
            pair_evacuated(dve, ("cz", 1))
            row_stats(lambda tt: cz[:, tt, :], D)
            norm_gain_bias(cz, "conv_g", "conv_b", 2)
            dve.sem_inc(S("cz_normed"), 1)
            for t in range(4):
                ins = biased(("gate", t), gates[:, :, W * t:W * (t + 1)], "unit_done", end_of("gate", t))
                freed(ins, ("gate", t))
                row_done(("gate", t))
            own_remainder(end_of("ada_tail", 0) - 1)
            for t in range(8):
                if t < 7:
                    own_remainder(end_of("ada_tail", t + 1) - 1)
                row = row_ready(dve, ("ada_tail", t))
                dve.wait_ge(S("mod_spread"), 5 + t)
                src = buf(("ada_tail", t))[:, 1, :]
                dst = mod_tail[:, W * t:W * (t + 1)]
                if t in (4, 5):
                    freed(dve.scalar_tensor_tensor(dst, src, 1.0, row, ALU.add, ALU.add), ("ada_tail", t))
                else:
                    freed(dve.tensor_tensor(dst, src, row, ALU.add), ("ada_tail", t))
                row_done(("ada_tail", t))
            for c in range(4):
                rest_part("retT", c, yt_hi, rt_lo)
            for c in range(2):
                rest_part("cvT", c, xt2_hi, cv_lo)
            dve.wait_ge(S("sig_gates"), 4)
            for t in range(2):
                dve.wait_ge(S("unit_done"), end_of("ret", t, 4))
                v = gates[:, :, W * t:W * (t + 1)]
                freed(dve.tensor_tensor(v, v, buf(("ret", t)), ALU.mult), ("ret", t))
            for t in range(2):
                dve.wait_ge(S("cvT_turned"), 2)
                v = cz[:, :, W * t:W * (t + 1)]
                freed(biased(("conv", t), v, "unit_done", end_of("conv", t)), ("conv", t))
                pair_evacuated(dve, ("conv", t))
                row_done(("conv", t))
                link(dve.tensor_tensor(v, v, gates[:, :, D + W * t:D + W * (t + 1)], ALU.mult))
                settle()
                pair_evacuated(dve, ("ret", t))
                ins = dve.tensor_tensor(v, v, gates[:, :, W * t:W * (t + 1)], ALU.add)
                if t == 1:
                    ins.then_inc(S("merged"), 1)
                else:
                    link(ins)
            for c in range(2):
                rest_part("mT", c, ot_hi, ot_lo)
            pair_evacuated(dve, ("ada_tail", 7))
            dve.wait_ge(S("load_x"), 32)
            gt = mod_tail

            def residual_ln(t, gate_row):
                v = h_tok[:, :, W * t:W * (t + 1)]
                link(dve.tensor_tensor(v, v, bc2(gate_row), ALU.mult))
                settle()
                xv = x[:, :, W * t:W * (t + 1)]
                link(dve.scalar_tensor_tensor(xv, xv, ALPHA, v, ALU.mult, ALU.add))
                settle()

            for t in range(2):
                v = h_tok[:, :, W * t:W * (t + 1)]
                freed(biased(("mix", t), v, "unit_done", end_of("mix", t)), ("mix", t))
                pair_evacuated(dve, ("mix", t))
                row_done(("mix", t))
                residual_ln(t, gt[:, W * t:W * (t + 1)])
            row_stats(lambda tt: x[:, tt, :], D)
            norm_gain_bias(x, "ln1_g", "ln1_b", 2)
            link(dve.tensor_tensor(h_tok, x, gt[:, 2 * D:3 * D].unsqueeze(1).broadcast_to([P, NT, D]), ALU.mult))
            settle()
            dve.tensor_tensor(h_tok, h_tok, gt[:, D:2 * D].unsqueeze(1).broadcast_to([P, NT, D]), ALU.add).then_inc(S("h_ready"), 1)

            dve.wait_ge(S("load_router_b"), 32)
            dve.wait_ge(S("load_c_rows"), 16)
            dve.wait_ge(S("routed"), 1)
            freed(dve.tensor_tensor(lgt, buf("router")[:, :, 0:36], br.unsqueeze(1).broadcast_to([P, NT, 36]), ALU.add), "router")
            pair_evacuated(dve, "router")
            oo = [o_rt]

            def rb(*shape):
                v, _ = carve(*shape, on=oo[0])
                oo[0] += int(np.prod(shape))
                return v
            g_max, g_e, g_sum, g_hit, g_first = rb(NT), rb(NT, NG), rb(NT), rb(NT, NG), rb(NT)
            pick, l8, m1, hit1, hit2, m2, e2, wsum, w1, w2 = rb(NT, NG, NEG), rb(NT, NEG), rb(NT), rb(NT, NEG), rb(NT, NEG), rb(NT), rb(NT), rb(NT), rb(NT), rb(NT)
            l8b, c8, m8 = rb(NT, NEG), rb(NT, NEG), rb(NT, NEG)
            rank = rb(NEG)

            def one(ins):
                link(ins)
                settle()

            def wide(v, n):
                return v.unsqueeze(2).broadcast_to([P, NT, n])

            one(dve.tensor_scalar(rank, row_fb[:, 1, 0:NEG], -(T - NEG - 1.0), None, ALU.add))

            def first_max(hit, src, mx, n):
                one(dve.tensor_reduce(mx, src, AX_X, ALU.max))
                one(dve.tensor_tensor(hit, src, wide(mx, n), ALU.is_equal))
                one(dve.tensor_tensor(hit, hit, rank[:, 0:n].unsqueeze(1).broadcast_to([P, NT, n]), ALU.mult))
                one(dve.tensor_reduce(g_first, hit, AX_X, ALU.max))
                one(dve.tensor_tensor(hit, hit, wide(g_first, n), ALU.is_equal))

            gl = lgt[:, :, 0:NG]
            first_max(g_hit, gl, g_max, NG)
            dve.tensor_tensor(g_e, gl, wide(g_max, NG), ALU.subtract).then_inc(S("router_exp"), 1)
            el = lgt[:, :, NG:36].rearrange("p t (g e) -> p t g e", g=NG)
            for tt in range(NT):
                link(dve.tensor_tensor(pick[:, tt], el[:, tt], g_hit[:, tt].unsqueeze(2).broadcast_to([P, NG, NEG]), ALU.mult))
            settle()
            for tt in range(NT):
                link(dve.tensor_reduce(l8[:, tt], pick[:, tt].rearrange("p g e -> p e g"), AX_X, ALU.add))
            settle()
            first_max(hit1, l8, m1, NEG)
            one(dve.tensor_scalar(l8b, hit1, -3.0e38, None, ALU.mult))
            one(dve.tensor_tensor(l8b, l8b, l8, ALU.add))
            first_max(hit2, l8b, m2, NEG)
            dve.tensor_tensor(e2, m2, m1, ALU.subtract).then_inc(S("router_exp"), 1)
            dve.wait_ge(S("router_exped"), 2)
            one(dve.tensor_reduce(g_sum, g_e, AX_X, ALU.add))
            one(dve.tensor_tensor(m8, hit1, hit2, ALU.add))
            for tt in range(NT):
                one(dve.tensor_tensor(hits[:, tt].rearrange("p (g e) -> p g e", g=NG), g_hit[:, tt].unsqueeze(2).broadcast_to([P, NG, NEG]),
                                      m8[:, tt].unsqueeze(1).broadcast_to([P, NG, NEG]), ALU.mult))
            dve.memset(ones, 1.0).then_inc(S("hits_ready"), 1)
            one(dve.tensor_scalar(wsum, e2, 1.0, None, ALU.add))
            one(dve.tensor_tensor(wsum, wsum, g_sum, ALU.mult))
            one(dve.reciprocal(w1, wsum))
            one(dve.tensor_tensor(w2, w1, e2, ALU.mult))
            one(dve.tensor_tensor(hit1, hit1, wide(w1, NEG), ALU.mult))
            one(dve.tensor_tensor(hit2, hit2, wide(w2, NEG), ALU.mult))
            one(dve.tensor_tensor(c8, hit1, hit2, ALU.add))
            for tt in range(NT):
                one(dve.tensor_tensor(comb[:, tt].rearrange("p (g e) -> p g e", g=NG), g_hit[:, tt].unsqueeze(2).broadcast_to([P, NG, NEG]),
                                      c8[:, tt].unsqueeze(1).broadcast_to([P, NG, NEG]), ALU.mult))

            dve.wait_ge(S("ranked"), 1)
            settle()
            link(dve.scalar_tensor_tensor(slot_of, buf(("rank", 0))[:, :, 0:NE], 1.0, hits, ALU.add, ALU.mult))
            settle()
            free_pair(("rank", 0))
            one(dve.tensor_scalar(slot_of, slot_of, -1.0, None, ALU.add))
            dve.tensor_reduce(most[:, 0:1], slot_of.rearrange("p t e -> p (t e)"), AX_X, ALU.max).then_inc(S("most_ready"), 1)
            dve.wait_ge(S("most_turned"), 1)
            dve.tensor_reduce(flag_f, ps[0:1, 2 * plan["most"][0], 0:P], AX_X, ALU.max).then_inc(S("pair_free%d" % plan["most"][0]), 1)
            pair_evacuated(dve, "most")
            dve.tensor_scalar(flag[0:1, 0:1], flag_f, float(SLOTS), None, ALU.is_ge).then_inc(S("flag_set"), 1)

            def select(e, rd, r, wait):
                if wait:
                    dve.wait_ge(S("gathered1"), (e + OFF[r]))
                slots_ = iota[:, SLOTS * rd:SLOTS * (rd + 1)]
                for tt in range(NT):
                    ins = dve.tensor_scalar(sel[:, tt, :], slots_, slot_of[:, tt, bass.ds(e, 1)], None, ALU.is_equal)
                    if tt == NT - 1:
                        ins.then_inc(S("sel_ready"), 1)
                if wait:
                    dve.wait_ge(S("sel_turned"), (e + OFF[r]))
                for tt in range(NT):
                    ins = dve.tensor_scalar(selw[:, tt, :], slots_, slot_of[:, tt, bass.ds(e, 1)], comb[:, tt, bass.ds(e, 1)],
                                            ALU.is_equal, ALU.mult)
                    if tt == NT - 1:
                        ins.then_inc(S("selw_ready"), 1)

            def remainder(n, e, base, r):
                dve.wait_ge(S("hi_ready"), (e + OFF[r]) * 6 + (n + 1))
                dve.tensor_tensor(w_lo[:, n], ring[:, n], w_hi[:, n % HI].bitcast(F32), ALU.subtract).then_inc(S("dve_lo"), 1)

            def gathered0(e, r):
                dve.wait_ge(S("xe_hi0"), (e + OFF[r]) + 1)
                dve.tensor_tensor(xe_lo[:, 0:4, :], four_chunks(2), xe_hi[:, 0:4, :].bitcast(F32), ALU.subtract).then_inc(S("xe0"), 1)

            def gathered1(e, r):
                dve.wait_ge(S("gathered1"), (e + OFF[r]) + 1)
                dve.tensor_copy(xe_hi[:, 4:8, :], four_chunks(0)).then_inc(S("xe_hi1"), 1)
                dve.wait_ge(S("xe_hi1"), (e + OFF[r]) + 1)
                dve.tensor_tensor(xe_lo[:, 4:8, :], four_chunks(0), xe_hi[:, 4:8, :].bitcast(F32), ALU.subtract).then_inc(S("xe1"), 1)

            def four_chunks(bank):
                return ps[:, bank, :].rearrange("p (k s) -> p k s", k=4)

            def output_left(e, j, base, r):
                dve.wait_ge(S("ye_hi"), (e + OFF[r]) * 2 + (j + 1))
                half = slice(W * j, W * (j + 1))
                dve.scalar_tensor_tensor(ye_lo[:, half], ps[:, 1 + j, :], slot_weight[:, 0:1], ye_hi[:, half].bitcast(F32),
                                         ALU.mult, ALU.subtract).then_inc(S("ye_lo"), 1)

            def expert(e, base, r, rd, tail):
                if not tail:
                    select(e + 1, rd, r, True)
                remainder(3, e, base, r)
                dve.wait_ge(S("slot_weight"), (e + OFF[r]) + 1)
                dve.wait_ge(S("unit_done" + r), e * 6 + (base + 3))
                dve.tensor_scalar(selT[:, :], ps[:, 3, 0:T], 0.0, None, ALU.is_gt).then_inc(S("selT"), 1)
                dve.wait_ge(S("silu"), (e + OFF[r]) + 1)
                dve.wait_ge(S("unit_done" + r), e * 6 + (base + 4))
                dve.tensor_tensor(he, ps[:, 1, :], sge, ALU.mult).then_inc(S("act_ready"), 1)
                if not tail:
                    gathered0(e + 1, r)
                dve.wait_ge(S("hT"), (e + OFF[r]) + 1)
                dve.tensor_tensor(heT_lo[:, :, :], four_chunks(3), heT_hi[:, :, :].bitcast(F32), ALU.subtract).then_inc(S("hT_lo"), 1)
                remainder(5, e, base, r)
                if not tail:
                    gathered1(e + 1, r)
                    remainder(0, e + 1, base, r)
                output_left(e, 0, base, r)
                if not tail:
                    remainder(1, e + 1, base, r)
                output_left(e, 1, base, r)

            def experts(base, r, rd):
                select(0, rd, r, False)
                gathered0(0, r)
                gathered1(0, r)
                remainder(0, 0, base, r)
                remainder(1, 0, base, r)
                with dve.Fori(0, NE - 1) as e:
                    expert(e, base, r, rd, False)
                expert(NE - 1, base, r, rd, True)
                dve.wait_ge(S("scattered"), (NE + OFF[r]))

            dve.wait_ge(S("load_iota"), 16)
            dve.wait_ge(S("flag_set"), 1)
            settle()
            experts(n_before, "", 0)
            more = dve.value_load(flag[0:1, 0:1], min_val=0, max_val=1)
            with dve.If(more > 0):
                experts(0, "_b", 1)

            for tt in range(NT):
                g2 = gt[:, 3 * D:4 * D].rearrange("p (a b) -> p a b", a=2)
                hv = h_tok[:, tt, :].rearrange("p (a b) -> p a b", a=2)
                freed(dve.tensor_tensor(hv, buf("moe_y%d" % tt), g2, ALU.mult), "moe_y%d" % tt)
            pair_evacuated(dve, "moe_y0")
            pair_evacuated(dve, "moe_y1")
            link(dve.scalar_tensor_tensor(x, x, ALPHA, h_tok, ALU.mult, ALU.add))
            settle()
            row_stats(lambda tt: x[:, tt, :], D)
            norm_gain_bias(x, "ln2_g", "ln2_b", 2)

            rms(x, h_tok, None, "pre0")
            dve.sem_inc(S("a_in_ready"), 1)

            for c in range(2):
                rest_part("aT", c, xt2_hi, xt2_lo)
            for t in range(4):
                pair_evacuated(dve, ("a", t))
            row_stats(lambda tt: a_v[:, tt, :], 2048)
            norm_gain_bias(a_v, "a_ln_g", "a_ln_b", 4)
            dve.sem_inc(S("v_normed"), 1)
            dve.wait_ge(S("load_tri"), 16)
            for c in range(2):
                dve.wait_ge(S("wsT_turned"), c + 1)
                o = buf(("wsT", c))
                ins = dve.tensor_tensor(a_wsT[:, 4 * c:4 * c + 4, :], o[:, 0, :].rearrange("p (g t) -> p g t", g=4),
                                        a_tri.unsqueeze(1).broadcast_to([P, 4, P]), ALU.mult)
                ins.then_inc(S("wsT_ready"), 1)
                if c == 1:
                    link(dve.tensor_copy(a_bs, o[:, 1, 0:KC]))
                dve.wait_ge(S("wsT_ready"), c + 1)
                settle()
                free_pair(("wsT", c))
            for i in range(4):
                pair_evacuated(dve, ("a", 4 + i))
                dve.wait_ge(S("sv_done"), i + 1)
                o = buf(("sv", i))
                for g in (2 * i, 2 * i + 1):
                    uv = a_u[:, :, 256 * g:256 * (g + 1)]
                    link(dve.scalar_tensor_tensor(uv, o[:, :, 256 * (g % 2):256 * (g % 2 + 1)], a_bs[:, g:g + 1], uv, ALU.add, ALU.mult))
                settle()
                free_pair(("sv", i))
            for t in range(4):
                pair_evacuated(dve, ("a", 8 + t))
                v = a_z[:, :, W * t:W * (t + 1)]
                dve.tensor_tensor(v, v, a_u[:, :, W * t:W * (t + 1)], ALU.mult).then_inc(S("y_gated"), 1)
            for c in range(4):
                rest_part("yT", c, yt_hi, yt_lo)
            for t in range(2):
                pair_evacuated(dve, ("a_out", t))
            rms(y2, y2, None, "post0")
            link(dve.tensor_tensor(x, x, y2, ALU.add))
            settle()
            rms(x, y2, None, "pre1")
            dve.sem_inc(S("b_in_ready"), 1)
            for c in range(2):
                rest_part("bT", c, xt2_hi, xt2_lo)

            dve.wait_ge(S("load_c_rope2"), 16)
            dve.wait_ge(S("load_c_mask"), 16)
            n_rope = 0
            for t in range(20):
                if BKIND[t] in "qk":
                    tab = 0 if BKIND[t] == "q" else 1
                    dve.wait_ge(S("unit_done"), end_of("b", t))
                    raw = buf(("b", t))
                    if n_rope >= 1:
                        dve.wait_ge(S("b_roped"), n_rope)
                    if n_rope >= 2:
                        dve.wait_ge(S("b_turned"), n_rope - 1)
                    dst = b_rope[:, n_rope % 2]
                    for tt in range(NT):
                        s = raw[:, tt, :].rearrange("p (h s d) -> p h s d", h=8, s=2)
                        q = b_t2[:, tt, :].rearrange("p (h s d) -> p h s d", h=8, s=2)
                        cos = rope2[:, tab, 0, tt, :].unsqueeze(1).broadcast_to([P, 8, HD])
                        link(dve.tensor_tensor(dst[:, tt, :].rearrange("p (h d) -> p h d", h=8),
                                               raw[:, tt, :].rearrange("p (h d) -> p h d", h=8), cos, ALU.mult))
                        for s_ in range(2):
                            sin = rope2[:, tab, 1, tt, 32 * s_:32 * (s_ + 1)].unsqueeze(1).broadcast_to([P, 8, 32])
                            link(dve.tensor_tensor(q[:, :, s_, :], s[:, :, 1 - s_, :], sin, ALU.mult))
                    settle()
                    free_pair(("b", t))
                    dve.tensor_tensor(dst, dst, b_t2, ALU.add).then_inc(S("b_roped"), 1)
                    n_rope += 1
                for act, g, c in slots[t]:
                    if act == "scores":
                        for i in range(2):
                            dve.wait_ge(S("b_scored"), 2 * (4 * g + c) + i + 1)
                            o = buf((act, g, c, i))
                            for hh in range(2):
                                h = 4 * c + 2 * i + hh
                                if i == 0 and hh == 0 and (g or c):
                                    dve.wait_ge(S("b_p_turned"), 2 * (4 * g + c))
                                for tt in range(NT):
                                    r = slice(P * tt, P * tt + P * (tt + 1))
                                    link(dve.tensor_tensor(b_p[:, 2 * i + hh, r], o[:, hh, r], amask[:, g, P * (1 - tt):2 * P], ALU.add))
                            settle()
                            free_pair((act, g, c, i))
                            for hh in range(2):
                                h = 4 * c + 2 * i + hh
                                for tt in range(NT):
                                    r = slice(P * tt, P * tt + P * (tt + 1))
                                    ins = dve.tensor_reduce(b_nm[:, g, tt, h:h + 1], b_p[:, 2 * i + hh, r], AX_X, ALU.max, negate=True)
                                    if tt == 1:
                                        ins.then_inc(S("b_maxed"), 1)
                                    else:
                                        link(ins)
                    elif act == "values":
                        dve.wait_ge(S("b_valued"), 4 * g + c + 1)
                        o = buf((act, g, c))
                        freed(dve.tensor_copy(b_acc[:, g, :, 4 * c:4 * c + 4, :],
                                              o[:, :, 0:256].rearrange("p t (h d) -> p t h d", h=4)), (act, g, c))
            dve.wait_ge(S("b_maxed"), 48)
            settle()
            dve.wait_ge(S("b_probs"), 48)
            one(dve.tensor_tensor(b_q, b_nm[:, 0], b_nm[:, 1], ALU.min))
            one(dve.tensor_tensor(b_q, b_q, b_nm[:, 2], ALU.min))
            for g in range(DIL):
                ins = dve.tensor_tensor(b_e[:, g], b_q, b_nm[:, g], ALU.subtract)
                if g == 2:
                    ins.then_inc(S("b_ediff"), 1)
                else:
                    link(ins)
            dve.wait_ge(S("b_eexp"), 1)
            one(dve.tensor_tensor(b_s, b_s, b_e, ALU.mult))
            one(dve.tensor_tensor(b_q, b_s[:, 0], b_s[:, 1], ALU.add))
            one(dve.tensor_tensor(b_q, b_q, b_s[:, 2], ALU.add))
            one(dve.reciprocal(b_q, b_q))
            for g in range(DIL):
                link(dve.tensor_tensor(b_e[:, g], b_e[:, g], b_q, ALU.mult))
            settle()
            for c in range(4):
                pair_evacuated(dve, ("values", 2, c))
            for g in range(DIL):
                for tt in range(NT):
                    v = b_acc[:, g, tt]
                    link(dve.tensor_tensor(v, v, b_e[:, g, tt, :].unsqueeze(2).broadcast_to([P, HEADS, HD]), ALU.mult))
            settle()
            acc = [b_acc[:, g].rearrange("p t h d -> p t (h d)") for g in range(DIL)]
            one(dve.tensor_tensor(acc[0], acc[0], acc[1], ALU.add))
            one(dve.tensor_tensor(acc[0], acc[0], acc[2], ALU.add))
            for t in (16, 17):
                pair_evacuated(dve, ("b", t))
            dve.tensor_tensor(b_z, b_z, acc[0], ALU.mult).then_inc(S("b_o_ready"), 1)
            for c in range(2):
                rest_part("oT", c, ot_hi, ot_lo)
            for t in range(2):
                pair_evacuated(dve, ("b_out", t))
            rms(y2, y2, None, "post1")
            dve.tensor_tensor(x, x, y2, ALU.add).then_inc(S("out_ready"), 1)

        @block.gpsimd
        def _(pool):
            pool.memset(minus_half, -0.5).then_inc(S("half_set"), 1)
            pool.wait_ge(S("half_set"), 1)

            def norm_powers(first_norm, last_norm):
                for n in range(first_norm, last_norm):
                    pool.wait_ge(S("stats_ready"), n + 1)
                    pool.tensor_scalar(ms, mv[:, :, 1], norm_eps[n], None, ALU.add).then_inc(S("eps_added"), 1)
                    pool.wait_ge(S("eps_added"), n + 1)
                    pool.tensor_tensor(rstd, ms, minus_half, ALU.pow).then_inc(S("rstd_ready"), 1)

            def remainders(base, r):
                with pool.Fori(0, NE) as e:
                    for j, n in enumerate(POOL_UNITS):
                        pool.wait_ge(S("hi_ready"), (e + OFF[r]) * 6 + (n + 1))
                        pool.tensor_tensor(w_lo[:, n], ring[:, n], w_hi[:, n % HI].bitcast(F32), ALU.subtract).then_inc(S("pool_lo"), 1)

            left = [0]

            def remainders_to(end):
                for n in by_pool:
                    if not left[0] <= n < end:
                        continue
                    m, w = part_of(n)
                    pool.wait_ge(S("w_hi_full"), m + 1)
                    pool.tensor_tensor(w_lo2[:, slots_of[n]], ring[:, slots_of[n]], w[:, :, :].bitcast(F32), ALU.subtract).then_inc(S("w_lo_full"), 1)
                left[0] = end

            for i in range(4):
                remainders_to(end_of("g", i) + 1)
                norm_powers(2 * i, 2 * i + 2)
            remainders_to(end_of("g", 3) + 2)
            norm_powers(H, H + 1)
            remainders_to(n_before)
            norm_powers(H + 1, MOE_NORM)
            pool.wait_ge(S("h_ready"), 1)
            pool.wait_ge(S("h_part"), 1)
            pool.tensor_tensor(h_rest, h_tok, h_parts[0][:, :, :], ALU.subtract).then_inc(S("h_left"), 1)
            pool.wait_ge(S("h_part"), 2)
            pool.wait_ge(S("h_left"), 1)
            pool.tensor_tensor(h_parts[2][:, :, :], h_rest, h_parts[1][:, :, :], ALU.subtract).then_inc(S("h_left"), 1)
            remainders(n_before, "")
            pool.wait_ge(S("flag_set"), 1)
            more = pool.value_load(flag[0:1, 0:1], min_val=0, max_val=1)
            with pool.If(more > 0):
                remainders(0, "_b")
            left[0] = first["a"]
            for n, end in ((0, first["a"] + 1), (1, first["a"] + 11), (2, first["b"] + 1),
                           (3, first["b"] + 2), (4, len(units)), (5, len(units))):
                norm_powers(MOE_NORM + n, MOE_NORM + n + 1)
                remainders_to(end)

        @block.scalar
        def _(act):
            def evacuate(key, dst, view=None, func=ACT.Copy):
                src = buf(key) if view is None else view(buf(key))
                freed(act.activation(dst, src, func), key)

            def chunks(dstT, c, o=0):
                return dstT[:, o + 4 * c:o + 4 * c + 4, :].rearrange("p k (t n) -> p t k n", t=NT)

            def four(p_):
                return p_.rearrange("p t (k n) -> p t k n", k=4)

            led = [0]

            def leading_to(done):
                held, end = (HI1, n_before) if led[0] < n_before else (HI, len(units))
                while led[0] < min(done + held, end):
                    n = led[0]
                    if n >= (HI1 if n < n_before else first["a"] + HI):
                        act.wait_ge(S("unit_done"), n - held + 1)
                    elif n == first["a"] + HI - 1:
                        act.wait_ge(S("stats_ready"), MOE_NORM + 1)
                    act.wait_ge(S("w_full%d" % slots_of[n]), 16 * fills[n])
                    act.activation(part_of(n)[1][:, :, :], ring[:, slots_of[n]], ACT.Copy).then_inc(S("w_hi_full"), 1)
                    led[0] += 1

            def lead_part(name, c, dst, key=None):
                act.wait_ge(S(name + "_turned"), c + 1)
                act.activation(chunks(dst, c), four(buf(key or (name, c))), ACT.Copy).then_inc(S(name + "_hi"), 1)

            def product_rows(name, t, i):
                leading_to(end_of(name, t) - 1)
                act.wait_ge(S("unit_done"), end_of(name, t))
                if i >= 2:
                    act.wait_ge(S("mod_spread"), i - 1)
                act.activation(mod_rows[:, i % 2, :], buf((name, t))[:, 0, :], ACT.Copy).then_inc(S("mod_rows"), 1)

            act.wait_ge(S("rows_turned"), 1)
            act.activation(sT, buf("turn_rows")[:, 0, 0:16], ACT.Silu).then_inc(S("silu_c"), 1)
            act.activation(cwT, buf("turn_rows")[:, 1, 0:256].rearrange("p (k n) -> p k n", k=KC), ACT.Copy).then_inc(S("pair_free2"), 1)
            act.wait_ge(S("neg_abs"), 1)
            act.activation(la[:, 0, :], la[:, 0, :], ACT.Exp).then_inc(S("exp_abs"), 1)
            act.wait_ge(S("wdec_exps"), 1)
            act.activation(wdec, wdec, ACT.Exp).then_inc(S("wdec_exp"), 1)
            for t in range(4):
                product_rows("ada", t, t)
            leading_to(end_of("ada", 3))
            for n in range(4):
                lead_part("uT", n, yt_hi, ("uT", n // 2, n % 2))

            def sigmoid_z(i):
                pair_evacuated(act, ("glu", 2 * i + 1))
                v = tmp[:, 2 * i:2 * i + 2, :]
                act.activation(v, v, ACT.Sigmoid).then_inc(S("sig_z"), 1)

            def turned_z(i):
                act.wait_ge(S("zT_turned"), i + 1)
                evacuate(("zT", i), z_pad[:, 4 * i:4 * i + 4, PAD:PAD + T].rearrange("p k (t n) -> p t k n", t=NT), four)
            leading_to(end_of("glu", 1) - 1)
            sigmoid_z(0)
            leading_to(end_of("glu", 2) - 1)
            turned_z(0)
            leading_to(end_of("glu", 3) - 1)
            sigmoid_z(1)
            leading_to(end_of("k", 0) - 1)
            turned_z(1)
            for n, (dst, t) in enumerate(((kT, 0), (kT, 1), (qT, 0), (qT, 1))):
                leading_to((end_of("k", 1), end_of("v", 0), end_of("q", 1), end_of("q", 1))[n] - 1)
                act.wait_ge(S("heads_turned"), n + 1)
                evacuate((("kT", t), ("qT", t))[n // 2], chunks(dst, t), four)
            for i in range(4):
                act.wait_ge(S("state_done"), 2 * i + 2)
                freed(act.activation(state[:, 2 * i:2 * i + 2].rearrange("p h d v -> p h (d v)"), buf(("S", i)), ACT.Copy), ("S", i))
            for c in range(2):
                act.wait_ge(S("cz_turned"), c + 1)
                evacuate(("cz", c), cz[:, :, W * c:W * (c + 1)])

            def decays(h):
                if h >= 2:
                    act.wait_ge(S("ret_summed"), h - 1)
                Q = tmp[:, 4 + h % 2, :].rearrange("p (d n) -> p d n", d=2)
                act.activation(Q[:, 0, :], row_fb[:, 0, :], ACT.Exp, scale=lg[:, h:h + 1])
                act.activation(Q[:, 1, :], row_fb[:, 1, :], ACT.Exp, scale=lg[:, H + h:H + h + 1])
                act.wait_ge(S("ret_exps"), h + 1)
                E = tmp[:, 2 + h % 2, :]
                act.activation(E, E, ACT.Exp).then_inc(S("ret_exped"), 1)
            leading_to(end_of("q", 1))
            act.wait_ge(S("load_c_rows"), 16)
            decays(0)
            decays(1)
            for i in range(4):
                leading_to(end_of("g", i) - 1)
                pair_evacuated(act, ("g", i))
                v = sg[:, :, W * i:W * (i + 1)]
                act.activation(v, v, ACT.Silu).then_inc(S("silu_g"), 1)
                leading_to(end_of("g", i))
                if i < 3:
                    decays(2 * i + 2)
                    decays(2 * i + 3)
            leading_to(end_of("gate", 1) - 1)
            act.wait_ge(S("cz_normed"), 1)
            act.activation(cz, cz, ACT.Silu).then_inc(S("cz_ready"), 1)
            for t in range(4):
                leading_to(end_of("gate", t) - 1)
                pair_evacuated(act, ("gate", t))
                v = gates[:, :, W * t:W * (t + 1)]
                act.activation(v, v, ACT.Sigmoid).then_inc(S("sig_gates"), 1)
            act.wait_ge(S("unit_done"), end_of("gate", 3))
            for t in range(8):
                product_rows("ada_tail", t, 4 + t)
            leading_to(end_of("ada_tail", 7))
            for c in range(4):
                lead_part("retT", c, yt_hi)
            for c in range(2):
                lead_part("cvT", c, xt2_hi)
            leading_to(end_of("conv", 1))
            for c in range(2):
                lead_part("mT", c, ot_hi)
            leading_to(n_before)
            for c in range(2):
                act.wait_ge(S("eT_turned"), c + 1)
                evacuate(("eT", c), chunks(XT2, c), four)
            act.wait_ge(S("h_ready"), 1)
            act.activation(h_parts[0][:, :, :], h_tok, ACT.Copy).then_inc(S("h_part"), 1)
            act.wait_ge(S("h_left"), 1)
            act.activation(h_parts[1][:, :, :], h_rest, ACT.Copy).then_inc(S("h_part"), 1)
            act.wait_ge(S("router_exp"), 1)
            g_e, _ = carve(NT, NG, on=o_rt + NT)
            e2, _ = carve(NT, on=o_rt + NT + NT * NG + NT + NT * NG + NT + NT * NG * NEG + NT * NEG + NT + 2 * NT * NEG + NT)
            act.activation(g_e, g_e, ACT.Exp).then_inc(S("router_exped"), 1)
            act.wait_ge(S("router_exp"), 2)
            act.activation(e2, e2, ACT.Exp).then_inc(S("router_exped"), 1)

            def leading(n, e, base, r, start=False):
                if not start:
                    act.wait_ge(S("unit_done" + r), e * 6 + (base + n - HI + 1))
                act.wait_ge(S("w_full%d%s" % (n, r)), e * 16 + 16 * ((0 if r else fills_before[n]) + 1))
                act.activation(w_hi[:, n % HI], ring[:, n], ACT.Copy).then_inc(S("hi_ready"), 1)

            def gathered(e, r):
                act.wait_ge(S("gathered0"), (e + OFF[r]) + 1)
                act.activation(xe_hi[:, 0:4, :], ps[:, 2, :].rearrange("p (k s) -> p k s", k=4), ACT.Copy).then_inc(S("xe_hi0"), 1)

            def output(e, j, base, r):
                act.wait_ge(S("unit_done" + r), e * 6 + (base + 5 + j))
                act.activation(ye_hi[:, W * j:W * (j + 1)], ps[:, 1 + j, :], ACT.Copy, scale=slot_weight[:, 0:1]).then_inc(S("ye_hi"), 1)

            def expert(e, base, r, head, tail):
                leading(3, e, base, r)
                act.wait_ge(S("unit_done" + r), e * 6 + (base + 2))
                act.activation(sge, ps[:, 0, :], ACT.Silu).then_inc(S("silu"), 1)
                act.wait_ge(S("sel_turned"), (e + OFF[r]) + 1)
                if not head:
                    act.wait_ge(S("ye_lo"), (e + OFF[r]) * 2)
                act.activation(weighted, ps[:, 3, 0:T], ACT.Copy, accum_out=slot_weight[:, 0:1]).then_inc(S("slot_weight"), 1)
                leading(4, e, base, r)
                leading(5, e, base, r)
                if not tail:
                    gathered(e + 1, r)
                act.wait_ge(S("h_turned"), (e + OFF[r]) + 1)
                act.activation(heT_hi[:, :, :], ps[:, 3, :].rearrange("p (k s) -> p k s", k=4), ACT.Copy).then_inc(S("hT"), 1)
                if not tail:
                    leading(0, e + 1, base, r)
                output(e, 0, base, r)
                if not tail:
                    leading(1, e + 1, base, r)
                output(e, 1, base, r)
                if not tail:
                    leading(2, e + 1, base, r)

            def experts(base, r):
                act.wait_ge(S("h_left"), 2)
                for n in range(HI):
                    leading(n, 0, base, r, True)
                gathered(0, r)
                expert(0, base, r, True, False)
                with act.Fori(1, NE - 1) as e:
                    expert(e, base, r, False, False)
                expert(NE - 1, base, r, False, True)

            experts(n_before, "")
            act.wait_ge(S("flag_set"), 1)
            more = act.value_load(flag[0:1, 0:1], min_val=0, max_val=1)
            with act.If(more > 0):
                experts(0, "_b")

            led[0] = first["a"]
            leading_to(first["a"])
            for c in range(2):
                lead_part("aT", c, xt2_hi)
            for t in range(12):
                leading_to(end_of("a", t) - 1)
                act.wait_ge(S("unit_done"), end_of("a", t))
                dst = (a_v, a_u, a_z)[t // 4][:, :, W * (t % 4):W * (t % 4 + 1)]
                freed(act.activation(dst, buf(("a", t)), ACT.Gelu if t < 8 else ACT.Silu), ("a", t))
            for c in range(4):
                lead_part("yT", c, yt_hi)

            def evac_y(key, ready):
                freed(act.activation(y2[:, :, W * key[1]:W * (key[1] + 1)], buf(key), ACT.Copy), key)
            for t in range(2):
                leading_to(end_of("a_out", t, 4) - 1)
                act.wait_ge(S("unit_done"), end_of("a_out", t, 4))
                evac_y(("a_out", t), None)
            leading_to(first["b"])
            for c in range(2):
                lead_part("bT", c, xt2_hi)
            n_rope = 0
            for t in range(20):
                g = BGROUP[t]
                leading_to(end_of("b", t) - 1)
                if BKIND[t] in "vz":
                    act.wait_ge(S("unit_done"), end_of("b", t))
                    if BKIND[t] == "v":
                        if g:
                            act.wait_ge(S("b_valued"), 4 * (g - 1) + 2 * BIDX[t] + 2)
                        dst = b_v[:, :, W * BIDX[t]:W * (BIDX[t] + 1)]
                        freed(act.activation(dst, buf(("b", t)), ACT.Copy), ("b", t))
                    else:
                        freed(act.activation(b_z[:, :, W * BIDX[t]:W * (BIDX[t] + 1)], buf(("b", t)), ACT.Silu), ("b", t))
                if t and BKIND[t - 1] in "qk":
                    n_rope += 1
                    act.wait_ge(S("b_turned"), n_rope)
                    dst = (b_qT, b_kT)[BKIND[t - 1] == "k"][:, BGROUP[t - 1] % 2]
                    evacuate(("bqk", t - 1), chunks(dst, BIDX[t - 1]), four)
                for what, g, c in slots[t]:
                    if what == "turn":
                        n = 4 * g + c
                        for i in range(2):
                            act.wait_ge(S("b_p_turned"), 2 * n + i + 1)
                            if n >= 2:
                                act.wait_ge(S("b_valued"), n - 1)
                            freed(act.activation(b_pT[:, c % 2, 2 * i:2 * i + 2, :], buf(("turn", g, c, i))[:, :, 0:384], ACT.Copy), ("turn", g, c, i))
                    elif what == "scores":
                        for hh in range(4):
                            h = 4 * c + hh
                            act.wait_ge(S("b_maxed"), 4 * (4 * g + c) + hh + 1)
                            for tt in range(NT):
                                r = slice(P * tt, P * tt + P * (tt + 1))
                                ins = act.activation(b_p[:, hh, r], b_p[:, hh, r], ACT.Exp, bias=b_nm[:, g, tt, h:h + 1],
                                                     accum_out=b_s[:, g, tt, h:h + 1])
                                if tt == 1:
                                    ins.then_inc(S("b_probs"), 1)
            leading_to(first["b_out"])
            act.wait_ge(S("b_ediff"), 1)
            act.activation(b_e, b_e, ACT.Exp).then_inc(S("b_eexp"), 1)
            for c in range(2):
                lead_part("oT", c, ot_hi)
            for t in range(2):
                leading_to(end_of("b_out", t) - 1)
                act.wait_ge(S("unit_done"), end_of("b_out", t))
                evac_y(("b_out", t), None)


def tables():
    f = np.float32
    tok = np.arange(T)
    m = (np.arange(P)[:, None] + P * np.arange(NT)[None, :])[:, :, None]
    n = tok[None, None, :]
    out = {
        "c_dist_f": np.maximum(n - m, 0).astype(f),
        "c_dist_b": np.maximum(m - n, 0).astype(f),
        "c_log": (np.log(DK ** -0.5) + np.log(2.0) * (n == m)).astype(f),
        "c_rows": np.broadcast_to(np.stack([tok + 1, T - tok]), (P, 2, T)).astype(f).copy(),
        "c_pos": np.stack([T - 1 - m[:, :, 0], m[:, :, 0]], axis=1).astype(f),
        "c_ident": np.eye(P, dtype=f),
        "c_pick": np.broadcast_to(np.eye(2, dtype=f)[np.arange(P) // 64, :, None] * (np.arange(P)[:, None, None] % 32 == 0), (P, 2, P)).astype(f).copy(),
        "c_tri": np.triu(np.ones((P, P), f)),
        "c_before": np.triu(np.ones((P, P), f), 1),
        "c_iota": np.broadcast_to(tok, (P, T)).astype(f).copy(),
    }

    def halves(ang, scale=1.0):
        cos, sin = np.cos(ang.astype(f)), np.sin(ang.astype(f))
        t = np.stack([np.concatenate([cos, cos], -1), np.concatenate([-sin, sin], -1)])
        return (t * scale).astype(f).reshape(2, NT, P, -1).transpose(2, 0, 1, 3)

    inv = (f(10000.0) ** (-np.arange(DK // 4, dtype=f) / f(DK // 4))).astype(f)
    r, col = (tok // 64).astype(f), (tok % 64).astype(f)
    out["c_rope1"] = halves(np.concatenate([r[:, None] * inv, col[:, None] * inv], -1)).copy()
    inv2 = (f(1.0) / (f(10000.0) ** (np.arange(0, HD, 2, dtype=f) / f(HD)))).astype(f)
    ang = tok.astype(f)[:, None] * inv2[None, :]
    out["c_rope2"] = np.stack([halves(ang, HD ** -0.5), halves(ang)], axis=1).copy()
    rel = np.concatenate([P + np.arange(P)[:, None] - np.arange(P), np.arange(P)[:, None] - np.arange(P)], -1)
    masks = []
    for window, step in ((128, 1), (512, 4), (2048, 16)):
        masks.append(np.where((rel >= 0) & (rel <= window) & (rel % step == 0), 0.0, -1.0e30))
    out["c_mask"] = np.stack(masks, axis=1).astype(f)
    return out


_INS = ["x", "c", "ctx", "c_ctx", "w_ada", "b_ada", "w_in", "b_in", "ret_decay_fwd", "ret_decay_bwd", "w_ret_out",
        "conv_dw", "conv_dw_b", "conv_ln_g", "conv_ln_b", "w_conv_out", "b_conv_out", "w_mix_out", "b_mix_out",
        "ln1_g", "ln1_b", "w_router_grp", "b_router_grp", "w_router_exp", "b_router_exp", "w_exp_gate", "w_exp_up",
        "w_exp_down", "ln2_g", "ln2_b", "norm_pre_2", "norm_post_2", "a_w_in_2", "a_ln_g_2", "a_ln_b_2", "a_w_s_2",
        "a_b_s_2", "a_w_out_2", "b_w_in_2", "b_w_out_2"]


def kernel(**inputs):
    import concourse.bacc as bacc
    from concourse.bass_utils import run_bass_kernel_spmd

    nc = bacc.Bacc("TRN2", target_bir_lowering=False, num_devices=1)
    given = {name: np.ascontiguousarray(inputs[name]) for name in _INS}
    given.update({name: np.ascontiguousarray(t) for name, t in tables().items()})
    arrays, aps = {}, {}
    for name, v in given.items():
        arrays["in_" + name] = v
        aps[name] = nc.dram_tensor("in_" + name, v.shape, mybir.dt.from_np(v.dtype), kind="ExternalInput").ap()
    out = nc.dram_tensor("out_0", (1, T, D), F32, kind="ExternalOutput").ap()
    build(nc, aps, out)
    r = run_bass_kernel_spmd(nc, [arrays], core_ids=[0])
    return r.results[0]["out_0"]
```
